# Optimizing a Trainium2 kernel written in Bass

```python
import jax, jax.numpy as jnp
from jax import lax
import numpy as np
import math
import jax
import jax.numpy as jnp

D_MODEL = 1024
BATCH = 1
SEQ = 512
DEPTH = 1

CTX_LEN = 256
GRID_W = 64
A_CHUNK = 2 * GRID_W
A_WIDTH = D_MODEL
A_GROUPS = 8
A_GROUP_DIM = A_WIDTH // A_GROUPS
GLA_HEADS = 4
GLA_DK = D_MODEL // 2
GLA_DV = D_MODEL
GLA_HEAD_K = GLA_DK // GLA_HEADS
GLA_HEAD_V = GLA_DV // GLA_HEADS
GLA_GATE_RANK = 16
GLA_TAU = 16.0
GLA_CHUNK = 64
N_EXPERTS = 16
N_EXPERT_GROUPS = 4
EXPERTS_PER_GROUP = N_EXPERTS // N_EXPERT_GROUPS
TOP_K = 2
D_EXPERT = 3 * D_MODEL // 2
MOE_BLOCK = 128
EPS = 1e-6
IN_SIZES = (2 * A_WIDTH, GLA_DK, GLA_DK, GLA_DV, GLA_DV, GLA_GATE_RANK, GLA_GATE_RANK, 2 * D_MODEL)
IN_COLS = sum(IN_SIZES)


def rms_norm(x, g):
    xf = x.astype(jnp.float32)
    y = xf * lax.rsqrt(jnp.mean(xf * xf, axis=-1, keepdims=True) + EPS)
    return (y * g.astype(jnp.float32)).astype(x.dtype)

def layer_norm(x, g, b):
    xf = x.astype(jnp.float32)
    mu = jnp.mean(xf, axis=-1, keepdims=True)
    xc = xf - mu
    y = xc * lax.rsqrt(jnp.mean(xc * xc, axis=-1, keepdims=True) + EPS)
    return (y * g.astype(jnp.float32) + b.astype(jnp.float32)).astype(x.dtype)

def split_cols(p):
    idx, acc = [], 0
    for s in IN_SIZES[:-1]:
        acc += s
        idx.append(acc)
    return jnp.split(p, idx, axis=-1)

def spatial_gating(z, ln_g, ln_b, w_s, b_s):
    u, v = jnp.split(z, 2, axis=-1)
    v = layer_norm(v, ln_g, ln_b)
    bsz, length, width = v.shape
    vr = v.reshape(bsz, length // A_CHUNK, A_CHUNK, A_GROUPS, A_GROUP_DIM)
    mixed = jnp.einsum('gts,bnsgc->bntgc', w_s, vr) + b_s.T[:, :, None]
    return u * mixed.reshape(bsz, length, width)

def gla_chunk_scan(q, k, v, log_a, s0):
    bsz, nh, length, _ = q.shape
    dv = v.shape[-1]
    n = length // GLA_CHUNK
    cs = lambda t: t.astype(jnp.float32).reshape(bsz, nh, n, GLA_CHUNK, t.shape[-1])
    q, k, v, log_a = cs(q), cs(k), cs(v), cs(log_a)
    b = jnp.cumsum(log_a, axis=-2)
    b_last = b[..., -1:, :]
    q_in = q * jnp.exp(b)
    k_in = k * jnp.exp(-b)
    k_st = k * jnp.exp(b_last - b)
    mask = jnp.tril(jnp.ones((GLA_CHUNK, GLA_CHUNK), dtype=bool))
    att = jnp.where(mask, jnp.einsum('bhntk,bhnsk->bhnts', q_in, k_in), 0.0)
    o_intra = jnp.einsum('bhnts,bhnsv->bhntv', att, v)

    def step(state, xs):
        qc, kc, vc, dc = xs
        o = jnp.einsum('bhtk,bhkv->bhtv', qc, state)
        state = dc[..., 0, :, None] * state + jnp.einsum('bhsk,bhsv->bhkv', kc, vc)
        return state, o

    xs = tuple(jnp.moveaxis(t, 2, 0) for t in (q_in, k_st, v, jnp.exp(b_last)))
    s_fin, o_inter = lax.scan(step, s0, xs)
    o = o_intra + jnp.moveaxis(o_inter, 0, 2)
    return o.reshape(bsz, nh, length, dv), s_fin

def gla_bidirectional(q, k, v, la_f, la_b, s_f, s_b):
    o_f, s_f = gla_chunk_scan(q, k, v, la_f, s_f)
    flip = lambda t: jnp.flip(t, axis=2)
    o_b, s_b = gla_chunk_scan(flip(q), flip(k), flip(v), flip(la_b), s_b)
    return o_f + flip(o_b), s_f, s_b

def token_mixer(h_x, h_c, w_in, w_gate2, b_gate2, gla_g, sgu_ln_g, sgu_ln_b, sgu_w, sgu_b,
                w_a, w_b, b_branch, w_out, with_ctx):
    parts_x = split_cols(h_x @ w_in)
    parts_c = split_cols(h_c @ w_in)

    def heads(t):
        bsz, length, width = t.shape
        return t.reshape(bsz, length, GLA_HEADS, width // GLA_HEADS).transpose(0, 2, 1, 3)

    def gla_inputs(parts):
        _, q, k, v, _, lr_f, lr_b, _ = parts
        la = [heads(jax.nn.log_sigmoid((lr @ w_gate2[d] + b_gate2[d]).astype(jnp.float32)) / GLA_TAU)
              for d, lr in enumerate((lr_f, lr_b))]
        return heads(q) * GLA_HEAD_K ** -0.5, heads(k), heads(v), la[0], la[1]

    zero = jnp.zeros((h_c.shape[0], GLA_HEADS, GLA_HEAD_K, GLA_HEAD_V), jnp.float32)
    o_c, s_f, s_b = gla_bidirectional(*gla_inputs(parts_c), zero, zero)
    o_x, _, _ = gla_bidirectional(*gla_inputs(parts_x), s_f, s_b)

    def merge(parts, o):
        z_a, _, _, _, r, _, _, gates = parts
        y_a = spatial_gating(jax.nn.gelu(z_a), sgu_ln_g, sgu_ln_b, sgu_w, sgu_b) @ w_a
        o_n = o * lax.rsqrt(jnp.mean(o * o, axis=-1, keepdims=True) + EPS)
        bsz, _, length, _ = o.shape
        o_n = o_n.transpose(0, 2, 1, 3).reshape(bsz, length, GLA_DV) * gla_g
        y_b = (o_n.astype(r.dtype) * jax.nn.silu(r)) @ w_b
        g_a, g_b = jnp.split(jax.nn.sigmoid(gates + b_branch), 2, axis=-1)
        return (g_a * y_a + g_b * y_b) @ w_out

    y_x = merge(parts_x, o_x)
    y_c = merge(parts_c, o_c) if with_ctx else None
    return y_x, y_c

def moe_ffn(h, w_router, b_router, w_g, w_u, w_d):
    n_tok, d = h.shape
    logits = h.astype(jnp.float32) @ w_router.astype(jnp.float32) + b_router.astype(jnp.float32)
    probs = jax.nn.softmax(logits, axis=-1).reshape(n_tok, N_EXPERT_GROUPS, EXPERTS_PER_GROUP)
    group_score = lax.top_k(probs, TOP_K)[0].sum(-1)
    g_sel = jnp.argmax(group_score, axis=-1)
    in_group = jnp.take_along_axis(probs, g_sel[:, None, None], axis=1)[:, 0]
    top_w, top_i = lax.top_k(in_group, TOP_K)
    weight = top_w / jnp.sum(top_w, axis=-1, keepdims=True)
    expert = (g_sel[:, None] * EXPERTS_PER_GROUP + top_i).reshape(-1).astype(jnp.int32)

    n_slot = n_tok * TOP_K
    token = jnp.repeat(jnp.arange(n_tok, dtype=jnp.int32), TOP_K)
    order = jnp.argsort(expert)
    e_sorted = expert[order]
    counts = jnp.bincount(expert, length=N_EXPERTS).astype(jnp.int32)
    starts = jnp.cumsum(counts) - counts
    padded = (counts + MOE_BLOCK - 1) // MOE_BLOCK * MOE_BLOCK
    p_ends = jnp.cumsum(padded)
    p_starts = p_ends - padded
    dest_sorted = p_starts[e_sorted] + jnp.arange(n_slot, dtype=jnp.int32) - starts[e_sorted]
    n_blocks = -(-n_slot // MOE_BLOCK) + N_EXPERTS
    buf_tok = jnp.full((n_blocks * MOE_BLOCK,), n_tok, jnp.int32).at[dest_sorted].set(token[order])
    block_e = jnp.minimum(jnp.searchsorted(p_ends, jnp.arange(n_blocks, dtype=jnp.int32) * MOE_BLOCK,
                                           side='right'), N_EXPERTS - 1)
    h_pad = jnp.concatenate([h, jnp.zeros((1, d), h.dtype)], axis=0)
    x_blk = h_pad[buf_tok].reshape(n_blocks, MOE_BLOCK, d)

    def expert_block(args):
        xb, e = args
        return (jax.nn.silu(xb @ w_g[e]) * (xb @ w_u[e])) @ w_d[e]

    y_blk = lax.map(expert_block, (x_blk, block_e)).reshape(-1, d)
    dest = jnp.zeros((n_slot,), jnp.int32).at[order].set(dest_sorted)
    y = y_blk[dest].reshape(n_tok, TOP_K, d) * weight[..., None].astype(h.dtype)
    return jnp.sum(y, axis=1)

def first_inputs(seed: int = 0) -> dict:
    key = jax.random.key(seed)
    ks = iter(jax.random.split(key, 32))
    nrm = lambda shape, std: jax.random.normal(next(ks), shape, jnp.float32) * std
    L = DEPTH
    return {
        "x": nrm((BATCH, SEQ, D_MODEL), 1.0),
        "c": nrm((BATCH, D_MODEL), 1.0),
        "ctx": nrm((BATCH, CTX_LEN, D_MODEL), 1.0),
        "c_ctx": nrm((D_MODEL,), 1.0),
        "w_mod": nrm((L, D_MODEL, 6 * D_MODEL), 0.5 * D_MODEL ** -0.5),
        "b_mod": nrm((L, 6 * D_MODEL), 0.01),
        "g_norm1": 1.0 + nrm((L, D_MODEL), 0.01),
        "g_norm2": 1.0 + nrm((L, D_MODEL), 0.01),
        "w_in": nrm((L, D_MODEL, IN_COLS), D_MODEL ** -0.5),
        "w_gate2": nrm((L, 2, GLA_GATE_RANK, GLA_DK), GLA_GATE_RANK ** -0.5),
        "b_gate2": nrm((L, 2, GLA_DK), 0.1),
        "gla_norm_g": 1.0 + nrm((L, GLA_DV), 0.01),
        "sgu_ln_g": 1.0 + nrm((L, A_WIDTH), 0.01),
        "sgu_ln_b": nrm((L, A_WIDTH), 0.01),
        "sgu_w": nrm((L, A_GROUPS, A_CHUNK, A_CHUNK), A_CHUNK ** -0.5),
        "sgu_b": 1.0 + nrm((L, A_GROUPS, A_CHUNK), 0.01),
        "w_branch_a": nrm((L, A_WIDTH, D_MODEL), A_WIDTH ** -0.5),
        "w_branch_b": nrm((L, GLA_DV, D_MODEL), GLA_DV ** -0.5),
        "b_branch": nrm((L, 2 * D_MODEL), 0.01),
        "w_out": nrm((L, D_MODEL, D_MODEL), D_MODEL ** -0.5),
        "w_router": nrm((D_MODEL, N_EXPERTS), D_MODEL ** -0.5),
        "b_router": nrm((N_EXPERTS,), 0.01),
        "w_exp_gate": nrm((L, N_EXPERTS, D_MODEL, D_EXPERT), D_MODEL ** -0.5),
        "w_exp_up": nrm((L, N_EXPERTS, D_MODEL, D_EXPERT), D_MODEL ** -0.5),
        "w_exp_down": nrm((L, N_EXPERTS, D_EXPERT, D_MODEL), D_EXPERT ** -0.5),
        "g_final": 1.0 + nrm((D_MODEL,), 0.01),
    }

def first_block(x, c, ctx, c_ctx, w_mod, b_mod, g_norm1, g_norm2, w_in, w_gate2, b_gate2, gla_norm_g,
              sgu_ln_g, sgu_ln_b, sgu_w, sgu_b, w_branch_a, w_branch_b, b_branch, w_out,
              w_router, b_router, w_exp_gate, w_exp_up, w_exp_down, g_final):
    bsz, seq, d = x.shape
    n_lat = bsz * seq
    for layer in range(DEPTH):
        with_ctx = layer < DEPTH - 1
        mod_x = (jax.nn.silu(c) @ w_mod[layer] + b_mod[layer])[:, None, :]
        mod_c = jax.nn.silu(c_ctx) @ w_mod[layer] + b_mod[layer]
        sh1, sc1, gt1, sh2, sc2, gt2 = jnp.split(mod_x, 6, axis=-1)
        csh1, csc1, cgt1, csh2, csc2, cgt2 = jnp.split(mod_c, 6, axis=-1)

        h_x = rms_norm(x, g_norm1[layer]) * (1.0 + sc1) + sh1
        h_c = rms_norm(ctx, g_norm1[layer]) * (1.0 + csc1) + csh1
        y_x, y_c = token_mixer(h_x, h_c, w_in[layer], w_gate2[layer], b_gate2[layer], gla_norm_g[layer],
                               sgu_ln_g[layer], sgu_ln_b[layer], sgu_w[layer], sgu_b[layer],
                               w_branch_a[layer], w_branch_b[layer], b_branch[layer], w_out[layer], with_ctx)
        x = x + gt1 * y_x

        tokens = (rms_norm(x, g_norm2[layer]) * (1.0 + sc2) + sh2).reshape(-1, d)
        if with_ctx:
            ctx = ctx + cgt1 * y_c
            h_c2 = rms_norm(ctx, g_norm2[layer]) * (1.0 + csc2) + csh2
            tokens = jnp.concatenate([tokens, h_c2.reshape(-1, d)], axis=0)
        y = moe_ffn(tokens, w_router, b_router, w_exp_gate[layer], w_exp_up[layer], w_exp_down[layer])
        x = x + gt2 * y[:n_lat].reshape(bsz, seq, d)
        if with_ctx:
            ctx = ctx + cgt2 * y[n_lat:].reshape(ctx.shape)
    return rms_norm(x, g_final)


DEPTH_2 = 2

N_MIXERS = 2
S5_GROUP = 16
S5_GROUPS = D_MODEL // S5_GROUP
S5_STATE = 64
N_HEADS = 16
HEAD_DIM = D_MODEL // N_HEADS
IDX_HEADS = 8
IDX_DIM = 64
TOPK_MAX = 256
Q_BLOCK = 128
ROPE_THETA = 10000.0
D_FF = ((8 * D_MODEL // 3 + 255) // 256) * 256
N_S5 = (DEPTH_2 + 1) // 2
N_DSA = DEPTH_2 // 2
DSA_PROJ = 3 * D_MODEL + IDX_HEADS * IDX_DIM + IDX_DIM + IDX_HEADS


def rmsnorm(x, gain):
    xf = x.astype(jnp.float32)
    y = xf * lax.rsqrt(jnp.mean(xf * xf, axis=-1, keepdims=True) + EPS)
    if gain is not None:
        y = y * gain.astype(jnp.float32)
    return y.astype(x.dtype)

def rope_tables(length):
    inv_freq = ROPE_THETA ** (-jnp.arange(0, HEAD_DIM, 2, dtype=jnp.float32) / HEAD_DIM)
    ang = jnp.arange(length, dtype=jnp.float32)[:, None] * inv_freq[None, :]
    return jnp.cos(ang), jnp.sin(ang)

def apply_rope(t, cos, sin):
    tf = t.astype(jnp.float32)
    t1, t2 = jnp.split(tf, 2, axis=-1)
    c = cos[None, :, None, :]
    s = sin[None, :, None, :]
    out = jnp.concatenate([t1 * c - t2 * s, t2 * c + t1 * s], axis=-1)
    return out.astype(t.dtype)

def _ssm_combine(e1, e2):
    a1, b1 = e1
    a2, b2 = e2
    return a1 * a2, a2 * b1 + b2

def s5_mixer(u, lam_re, lam_im, log_dt, b_re, b_im, c_re, c_im, d_skip, w_glu):
    bsz, length, _ = u.shape
    f32 = jnp.float32
    lam = lax.complex(lam_re.astype(f32), lam_im.astype(f32))
    dt = jnp.exp(log_dt.astype(f32))[:, None]
    a_bar = jnp.exp(lam * dt)
    b_bar = ((a_bar - 1.0) / lam)[..., None] * lax.complex(b_re.astype(f32), b_im.astype(f32))
    ug = u.astype(f32).reshape(bsz, length, S5_GROUPS, S5_GROUP).astype(jnp.complex64)
    bu = jnp.einsum('blgh,gph->blgp', ug, b_bar)
    a_seq = jnp.broadcast_to(a_bar, bu.shape)
    _, states = lax.associative_scan(_ssm_combine, (a_seq, bu), axis=1)
    c = lax.complex(c_re.astype(f32), c_im.astype(f32))
    y = jnp.einsum('blgp,ghp->blgh', states, c).real.reshape(bsz, length, D_MODEL)
    y = y + d_skip.astype(f32) * u.astype(f32)
    y = jax.nn.gelu(y).astype(u.dtype)
    val, gate = jnp.split(y @ w_glu, 2, axis=-1)
    return val * jax.nn.sigmoid(gate)

def dsa_mixer(h, w_in, q_gain, k_gain, w_o, cos, sin, topk):
    bsz, length, _ = h.shape
    f32 = jnp.float32
    proj = h @ w_in
    cuts = [D_MODEL, 2 * D_MODEL, 3 * D_MODEL, 3 * D_MODEL + IDX_HEADS * IDX_DIM,
            3 * D_MODEL + IDX_HEADS * IDX_DIM + IDX_DIM]
    q, k, v, qi, ki, wi = jnp.split(proj, cuts, axis=-1)
    q = q.reshape(bsz, length, N_HEADS, HEAD_DIM)
    k = k.reshape(bsz, length, N_HEADS, HEAD_DIM)
    v = v.reshape(bsz, length, N_HEADS, HEAD_DIM)
    qi = qi.reshape(bsz, length, IDX_HEADS, IDX_DIM)
    q = apply_rope(rmsnorm(q, q_gain), cos, sin)
    k = apply_rope(rmsnorm(k, k_gain), cos, sin)
    qi = apply_rope(qi, cos, sin)
    ki = apply_rope(rmsnorm(ki, None)[:, :, None, :], cos, sin)[:, :, 0, :]
    wi = wi.astype(f32) * (IDX_HEADS ** -0.5)
    nb = length // Q_BLOCK
    kpos = jnp.arange(length, dtype=jnp.int32)
    qpos_blocks = kpos.reshape(nb, Q_BLOCK)
    att_scale = HEAD_DIM ** -0.5
    idx_scale = IDX_DIM ** -0.5

    def to_blocks(t):
        return t.reshape(bsz, nb, Q_BLOCK, *t.shape[2:]).swapaxes(0, 1)

    def attend_block(args):
        qb, qib, wb, qpos = args
        s_idx = jnp.einsum('bqhd,bkd->bqhk', qib, ki).astype(f32) * idx_scale
        score = jnp.einsum('bqhk,bqh->bqk', jax.nn.relu(s_idx), wb)
        causal = kpos[None, None, :] <= qpos[None, :, None]
        score = jnp.where(causal, score, -jnp.inf)
        _, sel = lax.top_k(score, topk)
        kg = jax.vmap(lambda kb, ib: kb[ib])(k, sel)
        vg = jax.vmap(lambda vb, ib: vb[ib])(v, sel)
        logits = jnp.einsum('bqhd,bqkhd->bhqk', qb, kg).astype(f32) * att_scale
        valid = (sel <= qpos[None, :, None])[:, None, :, :]
        logits = jnp.where(valid, logits, -jnp.inf)
        p = jax.nn.softmax(logits, axis=-1).astype(vg.dtype)
        return jnp.einsum('bhqk,bqkhd->bqhd', p, vg)

    out = lax.map(attend_block, (to_blocks(q), to_blocks(qi), to_blocks(wi), qpos_blocks))
    out = out.swapaxes(0, 1).reshape(bsz, length, D_MODEL)
    return out @ w_o

def swiglu(h, w_gate_up, w_down):
    gate, up = jnp.split(h @ w_gate_up, 2, axis=-1)
    return (jax.nn.silu(gate) * up) @ w_down

def second_inputs(seed: int = 0) -> dict:
    key = jax.random.key(seed)
    ks = jax.random.split(key, 20)
    f32 = jnp.float32
    nrm = lambda k, shape, s: jax.random.normal(k, shape, f32) * s
    x = jax.random.normal(ks[0], (BATCH, SEQ, D_MODEL), f32)
    n_idx = jnp.arange(S5_STATE, dtype=f32)
    s5_lambda_re = -0.5 + nrm(ks[1], (N_S5, S5_GROUPS, S5_STATE), 0.01)
    s5_lambda_im = math.pi * n_idx[None, None, :] + nrm(ks[2], (N_S5, S5_GROUPS, S5_STATE), 0.01)
    s5_log_dt = jax.random.uniform(ks[3], (N_S5, S5_GROUPS), f32, math.log(1e-3), math.log(1e-1))
    s5_b_re = nrm(ks[4], (N_S5, S5_GROUPS, S5_STATE, S5_GROUP), (2 * S5_GROUP) ** -0.5)
    s5_b_im = nrm(ks[5], (N_S5, S5_GROUPS, S5_STATE, S5_GROUP), (2 * S5_GROUP) ** -0.5)
    s5_c_re = nrm(ks[6], (N_S5, S5_GROUPS, S5_GROUP, S5_STATE), (2 * S5_STATE) ** -0.5)
    s5_c_im = nrm(ks[7], (N_S5, S5_GROUPS, S5_GROUP, S5_STATE), (2 * S5_STATE) ** -0.5)
    s5_d = nrm(ks[8], (N_S5, D_MODEL), 1.0)
    s5_w_glu = nrm(ks[9], (N_S5, D_MODEL, 2 * D_MODEL), D_MODEL ** -0.5)
    dsa_w_in = nrm(ks[10], (N_DSA, D_MODEL, DSA_PROJ), D_MODEL ** -0.5)
    dsa_q_norm = 1.0 + nrm(ks[11], (N_DSA, HEAD_DIM), 0.02)
    dsa_k_norm = 1.0 + nrm(ks[12], (N_DSA, HEAD_DIM), 0.02)
    dsa_w_o = nrm(ks[13], (N_DSA, D_MODEL, D_MODEL), D_MODEL ** -0.5)
    ffn_w_gate_up = nrm(ks[14], (DEPTH_2, D_MODEL, 2 * D_FF), D_MODEL ** -0.5)
    ffn_w_down = nrm(ks[15], (DEPTH_2, D_FF, D_MODEL), D_FF ** -0.5)
    norm_mix = 1.0 + nrm(ks[16], (DEPTH_2, D_MODEL), 0.02)
    norm_ffn = 1.0 + nrm(ks[17], (DEPTH_2, D_MODEL), 0.02)
    return {'x': x, 's5_lambda_re': s5_lambda_re, 's5_lambda_im': s5_lambda_im, 's5_log_dt': s5_log_dt,
            's5_b_re': s5_b_re, 's5_b_im': s5_b_im, 's5_c_re': s5_c_re, 's5_c_im': s5_c_im,
            's5_d': s5_d, 's5_w_glu': s5_w_glu, 'dsa_w_in': dsa_w_in, 'dsa_q_norm': dsa_q_norm,
            'dsa_k_norm': dsa_k_norm, 'dsa_w_o': dsa_w_o, 'ffn_w_gate_up': ffn_w_gate_up,
            'ffn_w_down': ffn_w_down, 'norm_mix': norm_mix, 'norm_ffn': norm_ffn}

def second_block(x, s5_lambda_re, s5_lambda_im, s5_log_dt, s5_b_re, s5_b_im, s5_c_re, s5_c_im,
              s5_d, s5_w_glu, dsa_w_in, dsa_q_norm, dsa_k_norm, dsa_w_o, ffn_w_gate_up,
              ffn_w_down, norm_mix, norm_ffn):
    length = x.shape[1]
    topk = min(TOPK_MAX, length // 4)
    cos, sin = rope_tables(length)
    for i in range(DEPTH_2):
        h = rmsnorm(x, norm_mix[i])
        j = i // N_MIXERS
        if i % N_MIXERS == 0:
            mix = s5_mixer(h, s5_lambda_re[j], s5_lambda_im[j], s5_log_dt[j], s5_b_re[j], s5_b_im[j],
                           s5_c_re[j], s5_c_im[j], s5_d[j], s5_w_glu[j])
        else:
            mix = dsa_mixer(h, dsa_w_in[j], dsa_q_norm[j], dsa_k_norm[j], dsa_w_o[j], cos, sin, topk)
        x = x + mix.astype(x.dtype)
        x = x + swiglu(rmsnorm(x, norm_ffn[i]), ffn_w_gate_up[i], ffn_w_down[i]).astype(x.dtype)
    return x


def setup_inputs(seed=0):
    out = dict(first_inputs(seed))
    for name, value in second_inputs(seed + 1).items():
        if name != "x":
            out[name + "_2"] = value
    return out


def reference(
    x, c, ctx, c_ctx, w_mod, b_mod, g_norm1, g_norm2, w_in, w_gate2, b_gate2, gla_norm_g,
    sgu_ln_g, sgu_ln_b, sgu_w, sgu_b, w_branch_a, w_branch_b, b_branch, w_out, w_router,
    b_router, w_exp_gate, w_exp_up, w_exp_down, g_final, s5_lambda_re_2, s5_lambda_im_2,
    s5_log_dt_2, s5_b_re_2, s5_b_im_2, s5_c_re_2, s5_c_im_2, s5_d_2, s5_w_glu_2, dsa_w_in_2,
    dsa_q_norm_2, dsa_k_norm_2, dsa_w_o_2, ffn_w_gate_up_2, ffn_w_down_2, norm_mix_2,
    norm_ffn_2,
):
    x = first_block(
        x, c, ctx, c_ctx, w_mod, b_mod, g_norm1, g_norm2, w_in, w_gate2, b_gate2, gla_norm_g,
        sgu_ln_g, sgu_ln_b, sgu_w, sgu_b, w_branch_a, w_branch_b, b_branch, w_out, w_router,
        b_router, w_exp_gate, w_exp_up, w_exp_down, g_final,
    )
    return second_block(
        x, s5_lambda_re_2, s5_lambda_im_2, s5_log_dt_2, s5_b_re_2, s5_b_im_2, s5_c_re_2,
        s5_c_im_2, s5_d_2, s5_w_glu_2, dsa_w_in_2, dsa_q_norm_2, dsa_k_norm_2, dsa_w_o_2,
        ffn_w_gate_up_2, ffn_w_down_2, norm_mix_2, norm_ffn_2,
    )


_drawn_inputs = setup_inputs


def setup_inputs(seed=0):
    import zlib

    import numpy as np

    out = dict(_drawn_inputs(seed))
    spreads = {}
    factors = {'g_norm1': 4.681,
     'g_norm2': 2.763,
     'gla_norm_g': 8.0,
     'sgu_ln_g': 4.347,
     'sgu_ln_b': 8.0,
     'sgu_b': 8.0,
     'b_branch': 8.0,
     'g_final': 3.181,
     's5_lambda_re_2': 8.0,
     'dsa_q_norm_2': 8.0,
     'dsa_k_norm_2': 8.0,
     'norm_mix_2': 2.796}
    for name, (base, spread) in spreads.items():
        noise = np.random.default_rng([zlib.crc32(name.encode()), seed]).standard_normal(out[name].shape)
        drawn = base * np.exp(spread * noise) if base else spread * noise
        out[name] = jnp.asarray(drawn.astype(out[name].dtype))
    for name, factor in factors.items():
        out[name] = (out[name] * factor).astype(out[name].dtype)
    return out
```

```python
from contextlib import ExitStack

import numpy as np
import concourse.bass as bass
from concourse import mybir

F32 = mybir.dt.float32
F32R = mybir.dt.float32r
I32 = mybir.dt.int32
U32 = mybir.dt.uint32
ALU = mybir.AluOpType
ACT = mybir.ActivationFunctionType
AX = mybir.AxisListType

P = 128
D = 1024
KT = D // P
T = 512
TC = 256
TA = T + TC
NTX, NTC = T // P, TC // P
EPS = 1e-6
HEADS, HK, HV = 4, 128, 256
RANK = 16
GC = 64
NE, NG, EG = 16, 4, 4
FE = 1536
FET = FE // P
BLK = 128
NBLK = 2 * T // BLK + NE
FF = 2816
FFT = FF // P
S5G, S5H, S5P, S5T = 64, 16, 64, 8
S5C = T // S5T
AH, HD = 16, 64
IH = 8
TOPK = 128
UNIT = P
CH = 16
MASKED, TAKEN = -1.0e30, -3.0e38
TURN = (6.28125, 0.0019350051879882812, 3.0199159795074593e-07)
KF = 1024

COLS = {}
_at = 0
for _name, _n in (("b_mod", 48), ("g_norm1", 8), ("g_norm2", 8), ("gla_g", 8), ("b_branch", 16),
                  ("g_final", 8), ("b_gate2", 8), ("s5_d", 8), ("norm_mix", 16), ("norm_ffn", 16),
                  ("c", 16), ("qk_gain", 2)):
    COLS[_name] = (_at, _at + _n)
    _at += _n
NCOL = _at

STREAM_A = [("mod", "row", 0, 4), ("lr", "col", 0, 1), ("k", "col", 0, 4), ("q", "col", 0, 4),
            ("v", "row", 0, 2), ("r", "col", 0, 8), ("zv", "row", 0, 2),
            ("zu", "col", 0, 8), ("gb", "col", 0, 8), ("ga", "col", 0, 8), ("wb", "col", 0, 8),
            ("wa", "col", 0, 8), ("wout", "col", 0, 8)]
"""A stream's unit numbers by (matrix, block)."""


def unit_table(stream, depth):
    at, table = 0, {}
    for name, kind, b0, b1 in stream:
        rows = depth.get(name, KT)
        for b in range(b0, b1):
            table[name, b] = at
            at += rows * (1 if kind == "col" else 4)
    return table, -(-at // CH)


DEPTH = {"down0": FFT, "down1": FFT}
UNITS_A, CHUNKS_A = unit_table(STREAM_A, DEPTH)
STREAM_B = [("glu", "col", 0, 16), ("gu0", "col", 0, 2 * FFT), ("down0", "col", 0, 8),
            ("dq", "col", 0, 8), ("dk", "col", 0, 8), ("dv", "row", 0, 2), ("dqi", "col", 0, 4),
            ("dki", "col", 0, 1), ("wo", "col", 0, 8), ("gu1", "col", 0, 2 * FFT), ("down1", "col", 0, 8)]
UNITS_B, CHUNKS_B = unit_table(STREAM_B, DEPTH)
RING_PAGES = 8
HALF = 8
CHUNKS_E = 18
RING_A, RING_E = 4, 6

JOBS_A = ["ssx", "ssc"] + [f"modrow{n}" for n in range(4)] + ["mod1", "lrx", "lrc"]
JOBS_A += [f"k{s}{h}" for h in range(HEADS) for s in "xc"] + ["mod2"]
JOBS_A += [f"la{s}{d}{h}" for d in range(2) for h in range(HEADS) for s in "xc"]
JOBS_A += [f"q{h}" for h in range(HEADS)]
JOBS_A += [f"v{n}{t}" for n in range(2) for t in range(NTX + NTC)]


def gla_steps():
    for i in range(NTC + NTX):
        for d in range(2):
            x = i >= NTC
            n, m = (NTX, i - NTC) if x else (NTC, i)
            yield d, (m if d == 0 else n - 1 - m), x, ((0, 1) if d == 0 else (1, 0)), i == NTC + NTX - 1


for _d, _m, _x, _cs, _last in gla_steps():
    JOBS_A += [f"kT{_d}{_x}{_m}"] + ([f"att{_d}{_m}"] if _x else [])
    for _n, _c in enumerate(_cs):
        JOBS_A += ([f"o{_d}{_m}{_c}"] if _x else [])
        JOBS_A += [] if _last and _n == 1 else [f"st{_d}{_x}{_m}{_c}{_i}" for _i in range(2)]
JOBS_A += [f"on{h}" for h in range(HEADS)] + [f"r{j}" for j in range(KT)]
JOBS_A += [f"zv{n}{t}" for n in range(2) for t in range(NTX)]
JOBS_A += [f"{w}{j}" for w in ("zu", "gb", "ga", "wb") for j in range(KT)]
JOBS_A += [f"mix{j}" for j in range(KT)] + [f"wa{j}" for j in range(KT)] + [f"wout{j}" for j in range(KT)]
JOBS_A += ["ss2"] + [f"tok{t}{n}" for t in range(NTX) for n in range(2)] + ["route", "rank"]
JA = {name: n for n, name in enumerate(JOBS_A)}
assert len(JA) == len(JOBS_A)

JOBS_B = [f"y{j}" for j in range(KT)] + ["sn0", "sn1"]
for _t in range(KT):
    JOBS_B += [f"qt{_t}{i}" for i in range(4)] + [f"kk{_t}{i}" for i in range(2)] + [f"s{_t}{i}" for i in range(2)]
JOBS_B += [f"ys{t}" for t in range(KT)]
JOBS_B += [f"glu{b}" for b in range(2 * KT)] + ["sn2"]
JOBS_B += [f"gu0{b}" for b in range(2 * FFT)] + [f"down0{j}" for j in range(KT)] + ["sn3"]
ROPED = [("dq", j, True, 0) for j in range(KT)] + [("dk", j, True, 1) for j in range(KT)]
ROPED += [("dqi", j, False, None) for j in range(4)] + [("dki", 0, True, None)]
NR = len(ROPED)
for _s in range(NR + 2):
    if _s < NR:
        JOBS_B += [f"pr{_s}"]
    if 1 <= _s <= NR and ROPED[_s - 1][2]:
        JOBS_B += [f"pn{_s - 1}"]
    if 2 <= _s:
        JOBS_B += [f"rot{_s - 2}"]
_k = JOBS_B.index(f"pr{2 * KT}")
JOBS_B[_k:_k] = [f"dv{n}{t}" for n in range(2) for t in range(NTX)]
JOBS_B += ["wi"]
PAIRS = [(t, h) for t in range(NTX) for h in range(AH)]
NPAIR = len(PAIRS)
for _s in range(NPAIR + 3):
    if 2 <= _s < NPAIR + 2:
        JOBS_B += [f"pt{_s - 2}"]
    if 3 <= _s and (_s - 3) % 2 == 0:
        JOBS_B += [f"av{_s - 3}"]
    if _s < NPAIR:
        if PAIRS[_s][1] == 0 and PAIRS[_s][0] > 0:
            JOBS_B += [f"ix{PAIRS[_s][0]}{h}" for h in range(IH)]
        JOBS_B += [f"lg{_s}"]
JOBS_B += [f"wo{j}" for j in range(KT)] + ["sn4"]
JOBS_B += [f"gu1{b}" for b in range(2 * FFT)] + [f"down1{j}" for j in range(KT)]
JB = {name: n + len(JA) for n, name in enumerate(JOBS_B)}
JOBS = {**JA, **JB}
assert len(JOBS) == len(JOBS_A) + len(JOBS_B)
UNITS = {**UNITS_A, **{key: u + CHUNKS_A * CH for key, u in UNITS_B.items()}}


def dram_scratch(nc):
    def dram(name, *shape):
        return nc.dram_tensor(name, shape, F32, kind="Internal").ap()

    return dict(xbuf=dram("xbuf", (NBLK + 1) * BLK, D), ybuf=dram("ybuf", NBLK * BLK, D),
                ud=dram("ud", S5G, S5H, S5T, S5C), kd=dram("kd", S5G, S5H, 2 * S5T, S5H),
                yd=dram("yd", S5G, S5H, S5T, S5C))


def layouts_more(g, io):
    def wide(w):
        return w.reshape(NE, KT, P, 3, 512).transpose(0, 3, 2, 1, 4).reshape(NE, 3, P, 2, CH * P)

    up = np.stack([wide(g["w_exp_gate"][0]), wide(g["w_exp_up"][0])], axis=2)
    up = up.transpose(0, 1, 2, 4, 3, 5).reshape(NE, 12, P, CH * P)
    down = g["w_exp_down"][0].reshape(NE, 6, 2, P, D).transpose(0, 1, 3, 2, 4).reshape(NE, 6, P, CH * P)
    io["we_stream"] = np.concatenate([up, down], axis=1)

    def paired(a, b):
        return np.stack([a.reshape(a.shape[0], -1, P), b.reshape(b.shape[0], -1, P)], axis=2).reshape(a.shape[0], -1)

    dsa = g["dsa_w_in_2"][0]
    dq, dk, dv = (dsa[:, i * D:(i + 1) * D] for i in range(3))
    dqi, dki, dwi = dsa[:, 3 * D:3 * D + 512], dsa[:, 3 * D + 512:3 * D + 576], dsa[:, 3 * D + 576:]
    ffn, glu = g["ffn_w_gate_up_2"], g["s5_w_glu_2"][0]
    io["wb_stream"] = _stream(STREAM_B, dict(
        glu=paired(glu[:, :D], glu[:, D:]), gu0=paired(ffn[0, :, :FF], ffn[0, :, FF:]), down0=g["ffn_w_down_2"][0],
        dq=dq, dk=dk, dv=dv, dqi=dqi, dki=np.concatenate([dki, dki], axis=1), wo=g["dsa_w_o_2"][0],
        gu1=paired(ffn[1, :, :FF], ffn[1, :, FF:]), down1=g["ffn_w_down_2"][1]))
    io["wiw"] = np.ascontiguousarray(dwi.reshape(KT, P, IH).transpose(1, 0, 2))
    twice = lambda a: np.ascontiguousarray(np.concatenate([a, a], axis=0))
    io["s5_lam"] = twice(np.stack([g["s5_lambda_re_2"][0].T, g["s5_lambda_im_2"][0].T,
                                   np.broadcast_to(g["s5_log_dt_2"][0][None, :], (S5P, S5G))], axis=1))
    io["s5_b"] = twice(np.stack([g[n][0].transpose(1, 0, 2) for n in ("s5_b_re_2", "s5_b_im_2")], axis=1))
    io["s5_c"] = twice(np.stack([g[n][0].transpose(2, 0, 1) for n in ("s5_c_re_2", "s5_c_im_2")], axis=1))
    half = np.pi / 2
    phase = np.zeros((2, 4), np.float32)
    phase[0], phase[1] = (half, np.pi, half, 0.0), (0.0, half, half, 0.0)
    io["s5_phase"] = np.ascontiguousarray(np.repeat(phase, S5P, axis=0).reshape(P, 4))
    freq = np.float32(10000.0) ** (-np.arange(0, HD, 2, dtype=np.float32) / np.float32(HD))
    angle = (np.arange(T, dtype=np.float32)[:, None] * freq[None, :]).astype(np.float32).T
    io["cossin"] = np.ascontiguousarray(np.stack([np.tile(np.cos(angle), (4, 1)), np.tile(np.sin(angle), (4, 1))],
                                                 axis=1).astype(np.float32))
    rope = np.zeros((P, P), np.float32)
    for b in range(0, P, HD):
        for i in range(HD // 2):
            rope[b + HD // 2 + i, b + i] = -1.0
            rope[b + i, b + HD // 2 + i] = 1.0
    io["rope"] = rope
    i = np.arange(P)
    io["half1"] = (i[:, None] // HD == i[None, :] // HD).astype(np.float32)


def products(pe, psum, phase):
    ring, used, jobs = phase["ring"], phase["weights_used"], phase["jobs"]
    chunk, order = [-1, False], phase["order"]

    def reach(key, n):
        u = phase["units"][key] + n
        c = u // CH
        if c > chunk[0]:
            pe.wait_ge(phase["weights_in"][c % len(ring)], 16 * (c // len(ring) + 1))
            chunk[:] = [c, c > 0]
        return ring[c % len(ring)], u % CH

    def unit(key, n):
        slot, at = reach(key, n)
        return slot[:, at, :]

    def wide(key, n):
        slot, at = reach(key, n)
        return slot[:, at:at + 4, :].rearrange("p a b -> p (a b)")

    def mm(o, lhsT, rhs, start, stop):
        ins = pe.matmul(o, lhsT, rhs, start=start, stop=stop)
        if chunk[1]:
            ins.then_inc(used, 1)
            chunk[1] = False
        return ins

    def opened(name):
        n = jobs[name]
        assert n == order[0], name
        order[0] += 1
        if n >= 8:
            pe.wait_ge(phase["bank_free"][n % 8], n // 8)
        return psum[n % 8]

    def by_columns(name, key, rhs, n, m=P, depth=KT):
        ps = opened(name)
        for kt in range(depth):
            ins = mm(ps[0:m, 0:n], unit(key, kt)[:, 0:m], rhs(kt), kt == 0, kt == depth - 1)
        ins.then_inc(phase["bank_done"], 1)

    def by_rows(names, key, h, tiles):
        banks = [opened(n) for n in names]
        for kt in range(KT):
            for i, t in enumerate(tiles):
                ins = mm(banks[i][:], h[:, kt, t * P:(t + 1) * P], wide(key, 4 * kt), kt == 0, kt == KT - 1)
                if kt == KT - 1:
                    ins.then_inc(phase["bank_done"], 1)

    return unit, wide, mm, opened, by_columns, by_rows


def half_of(name, block, rows, wide=False):
    return (UNITS_B[name, block] + rows * (4 if wide else 1) - 1) // HALF


def split_products(pe, psum, phase):
    parts, jobs, order, half = phase["parts"], phase["jobs"], phase["order"], [-1, False]

    def reach(key, n):
        u = UNITS_B[key] + n
        c = u // HALF
        if c > half[0]:
            pe.wait_ge(phase["weights_split"], c + 1)
            half[:] = [c, c > 0]
        return parts[c % 2], u % HALF

    def mm(o, lhsT, rhs, start, stop):
        ins = pe.matmul(o, lhsT, rhs, start=start, stop=stop)
        if half[1]:
            ins.then_inc(phase["split_used"], 1)
            half[1] = False
        return ins

    def opened(name):
        n = jobs[name]
        assert n == order[0], name
        order[0] += 1
        pe.wait_ge(phase["bank_free"][n % 8], n // 8)
        return psum[n % 8]

    def by_columns(name, key, moving, depth=KT):
        ps = opened(name)
        for kt in range(depth):
            (whigh, wlow), at = reach(key, kt)
            high, low = moving(kt)
            mm(ps[:], wlow[:, at, :], high, kt == 0, False)
            mm(ps[:], whigh[:, at, :], high, False, False)
            ins = mm(ps[:], whigh[:, at, :], low, False, kt == depth - 1)
        ins.then_inc(phase["bank_done"], 1)

    def by_rows(names, key, high, low):
        banks = [opened(n) for n in names]
        for kt in range(KT):
            (whigh, wlow), at = reach(key, 4 * kt)
            whigh, wlow = (w[:, at:at + 4, :].rearrange("p a b -> p (a b)") for w in (whigh, wlow))
            for t in range(NTX):
                tokens = slice(t * P, (t + 1) * P)
                mm(banks[t][:], low[:, kt, tokens], whigh, kt == 0, False)
                mm(banks[t][:], high[:, kt, tokens], whigh, False, False)
                ins = mm(banks[t][:], high[:, kt, tokens], wlow, False, kt == KT - 1)
                if kt == KT - 1:
                    ins.then_inc(phase["bank_done"], 1)

    return by_columns, by_rows


def block_kernel(nc, io, out, scratch):
    with ExitStack() as ctx:
        def sb(name, shape, dt=F32):
            return ctx.enter_context(nc.sbuf_tensor(name, shape, dt))

        def sem(name):
            return ctx.enter_context(nc.semaphore(name))

        ring_pages = sb("ring_pages", [P, RING_PAGES * KF])

        def parts_page(name, first, *shape):
            with nc.sbuf_tensor(name + "_below", [P, int((first - RING_PAGES) * KF)], F32):
                with nc.sbuf_tensor(name, [P] + list(shape), F32R) as t:
                    return t

        weight_parts = parts_page("weight_parts", 44.5, 2, 2, HALF, P)
        high_b, low_b = parts_page("high_b", 12, KT, T), parts_page("low_b", 16, KT, T)
        high_g = parts_page("high_g", 20, KT, T)
        low_p = parts_page("low_p", 38, KT, T)
        hid_parts = [parts_page(f"hidden_parts_{i}", 20 + 11 * i, 2, FFT // 2, T) for i in range(2)]
        arena = sb("arena", [P, (49 - RING_PAGES) * KF])
        psum = [ctx.enter_context(nc.psum_tensor(f"bank{b}", [P, 512], F32)) for b in range(8)]

        def page(first, *shape):
            n = int(np.prod(shape))
            of, base = (ring_pages, 0) if first < RING_PAGES else (arena, RING_PAGES)
            at = int((first - base) * KF)
            view = of[:, at:at + n]
            names = "abcde"[:len(shape)]
            if len(shape) == 1:
                return view
            return view.rearrange(f"p ({' '.join(names)}) -> p {' '.join(names)}",
                                  **{k: v for k, v in zip(names[1:], shape[1:])})

        ident = sb("ident", [P, P])
        ones = sb("ones", [P, P])
        tri = sb("tri", [P, P])
        gmask = sb("gmask", [P, 2, P], U32)
        cols = sb("cols", [P, NCOL])
        csilu = sb("csilu", [P, KT, 2])
        modc = sb("modc", [P, 48, 2])
        scale1 = sb("scale1", [P, KT, 2])
        scale2 = sb("scale2", [P, KT])
        blast = sb("blast", [P, 2, 48])
        decay = sb("decay", [P, 2, 48])
        wgate = sb("wgate", [64, 2, 4 * P])
        stats = sb("stats", [P, 2, 6])
        meanvar = sb("meanvar", [P, NTX, 2])
        varz = sb("varz", [P, NTX])
        prob, etmp, hot = (page(27 + i / 16, NTX, NE) for i in range(3))
        rsum = sb("rsum", [P, NTX])
        hit1, hit2, rest = (page(27.25 + i / 16, NTX * NG, EG) for i in range(3))
        best1, best2, gscore, before = (sb(n, [P, NTX * NG]) for n in ("best1", "best2", "gscore", "before"))
        ghit = sb("ghit", [P, NTX, NG])
        rank = sb("rank", [P, NTX + 1, NE])
        nblk, ends = sb("nblk", [P, NE]), sb("ends", [P, NE])
        slotf = sb("slotf", [P, 2, NTX])
        planf = sb("planf", [1, 32])
        wrt = sb("wrt", [P, KT, NE])
        brow = sb("brow", [1, NE])
        wiw = sb("wiw", [P, KT, IH])
        rs_b = page(48.5, T)
        plan = sb("plan", [1, 32], I32)
        slot = sb("slot", [P, 2 * NTX], I32)
        tokw = sb("tokw", [P, 2, NTX])

        def col(name, j=0):
            return cols[:, COLS[name][0] + j:COLS[name][0] + j + 1]

        def colspan(name):
            return cols[:, COLS[name][0]:COLS[name][1]]

        ring_a = [page(2 * r, CH, P) for r in range(RING_A)]
        x = page(8, KT, T)
        h1 = page(12, KT, TA)
        kk = page(18, HEADS, TA)
        qq = page(21, HEADS, T)
        vv = page(23, NTX + NTC, D)
        la = [page(29, HEADS, TA), page(32, HEADS, TA)]
        qin = [page(35, HEADS, T), qq]
        kin = [page(37, HEADS, T), kk[:, :, 0:T]]
        ctxt = page(29, KT, TC)
        sqx, sqc = page(39, KT, T), page(43, KT, TC)
        rs1 = page(45, TA)
        lr = page(46, TA)
        eb = page(39, HEADS * TA)
        restart = page(42, TA)
        oo = page(39, KT, T)
        state = page(43, 2, HEADS, HV)
        kst = page(45, 2, HEADS * P)
        att = page(46, 2, HEADS * P)
        wsp = page(47, KT, P)
        lng, lnb = page(48, D), page(36, D)
        bsp = page(30, KT, P)
        sqo = page(31, KT, T)
        rso = page(37, HEADS, T)
        rtmp = page(35, 2, T)
        zv = page(18, NTX, D)
        zu = page(22, KT, T)
        sgb, sga = page(26, KT, T), page(43, KT, T)
        yy = page(12, KT, T)
        mtmp = page(35, 2, T)
        rs2 = page(37, T)
        h2 = page(18, KT, T)
        tok = page(22, NTX, D)
        zero = page(42.75, D // 4)
        modrow = page(33, 4, 512)
        ring_m = [page(23 + 2 * r, CH * P) for r in range(2)]
        modacc = page(35, 4 * D)
        ends_le = page(26, NBLK, NE)

        weights_in = [sem(f"weights_in_{r}") for r in range(RING_A)]
        weights_used = sem("weights_used")
        bank_done = sem("bank_done")
        bank_free = [sem(f"bank_free_{b}") for b in range(8)]
        s_const, s_cols, s_x, s_ctx, s_late = (sem(n) for n in ("s_const", "s_cols", "s_x", "s_ctx", "s_late"))
        dve_step, act_step, pool_step = sem("dve_step"), sem("act_step"), sem("pool_step")
        names = ("csilu_ready", "mod1_ready", "squares", "variance", "root", "normed1", "h1_ready", "lr_ready",
                 "v_ready", "z_ready", "softplus", "b_ready", "eb_full", "eb_used", "kexp_in", "kexp_out",
                 "decay_ready", "gla_in", "kst_ready", "att_ready", "state_zero", "o_first", "o_done",
                 "sqo_ready", "silu_r", "ob_ready", "gelu_done", "zv_ready",
                 "sgb_ready", "sga_ready", "zu_ready", "y_ready", "x1_ready", 
                 "normed2", "h2_ready", "tok_ready", "logit_max", "logit_exp", "onehot", "plan_ready",
                 "mod_used", "modrow_ready", "zeros_stored", "rows_stored", "slots_ready")
        S = {n: sem(n) for n in names}
        state_sem = [sem(f"state_ready_{d}") for d in range(2)]
        kst_made, le_made = sem("kst_made"), sem("le_made")
        mod_in = [sem(f"mod_weights_in_{r}") for r in range(2)]
        att_flat = att.rearrange("p a b -> p (a b)")

        phase_a = dict(ring=ring_a, weights_in=weights_in, weights_used=weights_used, units=UNITS,
                       bank_done=bank_done, bank_free=bank_free, jobs=JOBS, order=[0])

        def result(eng, name):
            eng.wait_ge(bank_done, JOBS[name] + 1)
            return psum[JOBS[name] % 8]

        def free(name):
            return bank_free[JOBS[name] % 8]

        ring_e = [page(29 + 2 * r, CH * P) for r in range(RING_E)]
        xrow = page(12, D)
        xcol = page(13, KT, BLK)
        hs = page(14, 3, 512)
        hh = page(15.5, FE)
        hcol = page(17, FET, BLK)
        yrow = page(19, D)
        yg = page(29, 2, NTX, D)
        jobs_e = ["g0", "u0", "g1", "u1", "h0", "g2", "u2", "h1", "xa", "xb", "h2", "d0", "d1"]
        JE = {n: i for i, n in enumerate(jobs_e)}
        bank_e = dict(g0=(0, 0), u0=(1, 0), g1=(2, 0), u1=(3, 0), g2=(4, 0), u2=(5, 0), h0=(6, 0), h1=(7, 0),
                      xa=(0, 1), xb=(1, 1), h2=(6, 1), d0=(2, 1), d1=(3, 1))
        uses_e = [sum(b == n for b, _ in bank_e.values()) for n in range(8)]
        weights_in_e = [sem(f"expert_weights_in_{r}") for r in range(RING_E)]
        weights_used_e = sem("expert_weights_used")
        bank_done_e = sem("expert_bank_done")
        bank_free_e = [sem(f"expert_bank_free_{b}") for b in range(8)]
        for n in ("x_row_in", "x_turned", "sig_ready", "h_made", "h_turned", "y_copied", "y_stored", "moe_stored",
                  "moe_dve_done", "moe_gathered", "moe_summed"):
            S[n] = sem(n)

        def load_plan(eng):
            eng.wait_ge(S["plan_ready"], 1)
            return eng.value_load(plan[0:1, 0:1], min_val=2 * T // BLK, max_val=NBLK)

        def result_e(eng, i, name):
            eng.wait_ge(bank_done_e, i * len(JE) + (2 + JE[name] + 1))
            return psum[bank_e[name][0]]

        hb = page(12, KT, T)
        sqb = page(16, KT, T)
        u_s = page(37.5, KT, S5T, S5C)
        u2 = page(16, S5G, S5C)
        xs = page(20, S5C + 1, 2, S5G)
        cp = page(28.25, S5G, S5T + 1, S5H)
        qb = page(37.5, 2, 8, S5T, S5H)
        qt = page(39.5, 8, 2, P)
        mt = [page(37.5, 8, P), page(38.5, 8, P)]
        ksb = page(42.5, 8, 2 * S5T, S5H)
        pw = page(44.5, S5T + 1, 2, S5G)
        bb = page(45.75, 2, S5G, S5H)
        ys2 = page(47.75, 8, S5C)
        ab8 = page(48.25, 2, 2, S5G)
        cc = page(20, 2, S5G, S5H)
        bri = page(22, 2, S5G, S5H)
        tmp = page(24, 9 * 8 * S5H)
        phase = sb("phase", [P, 4])
        tmpq = page(41.5, 8 * P)
        sp5 = page(25.25, 24, S5G)
        yn = page(39.5, KT, S5T, S5C)
        st = page(42, 2, T)
        product = page(43, 3, T)
        parts = [[weight_parts[:, i, k] for k in range(2)] for i in range(2)]

        def hid(kt):
            half = hid_parts[kt // (FFT // 2)]
            return half[:, 0, kt % (FFT // 2), :], half[:, 1, kt % (FFT // 2), :]

        raw = page(20, KT, T)
        qT, kT = page(16, KT, T), page(20, KT, T)
        vt = page(24, NTX, D)
        qiT, kiT = page(28, 4, T), page(30, T)
        wi = page(30.5, NTX, IH)
        cossin = page(31, 2, T)
        bias = page(32, T)
        score = page(32.5, T)
        rl = page(33, 2, T)
        pp = page(34, 4, T)
        pT = page(36, 2, T)
        diag = page(37, 4, P)
        rope = page(37.5, P)
        half1 = page(37.625, P)
        oT = page(38, KT, T)
        sqt = page(42, 2, T)
        rst = page(43, 2, T)
        rt = page(44, 1, T)
        m8, mx, nmx, sm, rsm = (sb(n, [P, k]) for n, k in (("m8", 8), ("mx", 4), ("nmx", 4), ("sm", 4), ("rsm", 4)))
        for n in ("sq_full",   "h_full", "x2_ready", "s5_in", "s5_u_made", "s5_u_out",
                 "u2_in", "coef_exp", "coef_ready", "cp_ready", "qb_ready", "qt_ready", "ksb_ready",
                 "k_stored", "s_copied", "scanned", "ys_copied", "ys_stored", "yn_in", "y5_ready", "g5_ready",
                 "sig_b", "st_used", "x_ready", "raw_ready", "sqt_ready", "rvar", "rroot",
                 "normed_q", "rope_in", "rotated", "v_rows", "relu_ready", "score_ready", "masked", "bias0",
                 "logits", "exped", "diag_ready", "pt_ready", "o_ready", "stored"):
            S["b_" + n] = sem("b_" + n)
        RS = rs_b
        mt_sem = [sem(f"b_mt_in_{i}") for i in range(2)]
        av_done, relu_used, scan_part = sem("b_av_done"), sem("b_relu_used"), sem("b_scan_part")
        high_ready, split_ready, product_ready = sem("b_high_ready"), sem("b_split_ready"), sem("b_product_ready")
        weights_high, weights_split, split_used = sem("b_weights_high"), sem("b_weights_split"), sem("b_split_used")
        phase_b = dict(phase_a, parts=parts, weights_split=weights_split, split_used=split_used)
        NORMS_A = 3 + HEADS + NTX
        h_count = {1: KT, 2: 2 * KT, 3: 3 * KT, 4: 4 * KT}
        norm_of = [s for s in range(NR) if ROPED[s][2]]
        norm_index = {s: k for k, s in enumerate(norm_of)}

        def roped_tile(s):
            name, j = ROPED[s][0], ROPED[s][1]
            return {"dq": qT, "dk": kT, "dqi": qiT}[name][:, j, :] if name != "dki" else kiT

        def weights_high_part(act, upto, done):
            for h in range(done[0], upto + 1):
                c = CHUNKS_A + h // 2
                if h % 2 == 0:
                    act.wait_ge(weights_in[c % RING_A], 16 * (c // RING_A + 1))
                if h >= 2:
                    act.wait_ge(split_used, h - 1)
                src = ring_a[c % RING_A][:, h % 2 * HALF:(h % 2 + 1) * HALF, :]
                nc.scalar.activation(parts[h % 2][0], src, ACT.Copy).then_inc(weights_high, 1)
            done[0] = max(done[0], upto + 1)

        def weights_low_part(dve, upto, done):
            for h in range(done[0], upto + 1):
                c = CHUNKS_A + h // 2
                dve.wait_ge(weights_high, h + 1)
                src = ring_a[c % RING_A][:, h % 2 * HALF:(h % 2 + 1) * HALF, :]
                nc.vector.tensor_tensor(parts[h % 2][1], src, parts[h % 2][0].bitcast(F32), ALU.subtract) \
                    .then_inc(weights_split, 1)
                if h % 2:
                    dve.wait_ge(weights_split, h + 1)
                    dve.sem_inc(weights_used, 1)
            done[0] = max(done[0], upto + 1)

        END = dict(glu=half_of("glu", 15, KT), down0=half_of("down0", 7, FFT), dki=half_of("dki", 0, KT),
                   wo=half_of("wo", 7, KT), down1=half_of("down1", 7, FFT))

        def ahead(end, name, block, rows=KT, wide=False):
            last = half_of("down1", 7, FFT)
            return min(half_of(name, block, rows, wide) + 2, END[end] + 1, last)

        def copied(eng, ins, done, count, name):
            ins.then_inc(done, 1)
            eng.wait_ge(done, count)
            eng.sem_inc(free(name), 1)

        block = ctx.enter_context(nc.Block())

        @block.sync
        def _(sp):
            sp.dma_start(x, io["xt"].rearrange("k p t -> p k t")).then_inc(s_x, 16)
            sp.dma_start(ctxt, io["ct"].rearrange("k p t -> p k t")).then_inc(s_ctx, 16)
            for c in range(CHUNKS_A):
                if c >= RING_A:
                    sp.wait_ge(weights_used, c - RING_A + 1)
                sp.dma_start(ring_a[c % RING_A], io["wa_stream"][c].rearrange("p (u n) -> p u n", n=P)) \
                    .then_inc(weights_in[c % RING_A], 16)


            n_blocks = load_plan(sp)
            sp.wait_ge(S["rows_stored"], 16 * 2 * NTX)
            sp.wait_ge(S["onehot"], 1)
            sp.dma_start(xrow, scratch["xbuf"][0:BLK, :]).then_inc(S["x_row_in"], 16)
            with sp.Fori(0, n_blocks) as i:
                e = sp.value_load(plan[0:1, bass.ds(i + 1, 1)], min_val=0, max_val=NE - 1)
                for c in range(CHUNKS_E):
                    if c == 8:
                        sp.wait_ge(S["x_turned"], i * 2 + 2)
                        sp.dma_start(xrow, scratch["xbuf"][bass.ds(i * BLK + BLK, BLK), :]).then_inc(S["x_row_in"], 16)
                    sp.wait_ge(weights_used_e, i * CHUNKS_E + (c + 1))
                    sp.dma_start(ring_e[c % RING_E],
                                 io["we_stream"][bass.ds(e, 1), c, :, :].rearrange("a p n -> (a p) n")) \
                        .then_inc(weights_in_e[c % RING_E], 16)

            for c in range(CHUNKS_A, CHUNKS_A + CHUNKS_B):
                if c == CHUNKS_A + RING_A:
                    sp.wait_ge(S["b_k_stored"], 16 * KT)
                    kflat = scratch["kd"].rearrange("g h k c -> h g (k c)")
                    for t in range(KT):
                        if t < 2:
                            sp.wait_ge(S["b_s_copied"], 2 * KT)
                        else:
                            sp.wait_ge(bank_done, JB[f"ys{t - 2}"] + 1)
                        for s in range(S5T):
                            lo = (S5T - s) * S5H
                            sp.dma_start(mt[t % 2][16 * s:16 * s + 16, :, :], kflat[:, 8 * t:8 * t + 8, lo:lo + P]) \
                                .then_inc(mt_sem[t % 2], 16)
                sp.wait_ge(weights_used, c - RING_A + 1)
                sp.dma_start(ring_a[c % RING_A], io["wb_stream"][c - CHUNKS_A].rearrange("p (u n) -> p u n", n=P)) \
                    .then_inc(weights_in[c % RING_A], 16)
            sp.wait_ge(S["b_x_ready"], 4 * KT)
            sp.dma_start(out.rearrange("k p t -> p k t"), x).then_inc(S["b_stored"], 16)
            sp.wait_ge(S["b_stored"], 16)
        @block.gpsimd
        def _(pool):
            for dst, src in ((ident[:], io["ident"]), (tri[:], io["tri"]),
                             (gmask[:], io["gmask"]), (wgate[:], io["wgate"]), (wrt[:], io["wrouter"]),
                             (brow[:], io["b_router"]), (wiw[:], io["wiw"]), (wsp, io["sgu_w"]),
                             (lng, io["sgu_ln_g"].partition_broadcast(P))):
                pool.dma_start(dst, src).then_inc(s_const, 16)
            for c in range(2 * KT):
                if c >= 2:
                    pool.wait_ge(S["mod_used"], c - 1)
                pool.dma_start(ring_m[c % 2], io["mod2"][c]).then_inc(mod_in[c % 2], 16)
            pool.wait_ge(bank_done, JA["ssx"] + 1)
            nc.gpsimd.memset(zero, 0.0).then_inc(pool_step, 1)
            pool.wait_ge(pool_step, 1)
            spread = zero.unsqueeze(1).to_broadcast([P, 4, D // 4])
            for b in range(NBLK + 1):
                pool.dma_start(scratch["xbuf"][b * BLK:(b + 1) * BLK, :].rearrange("r (a b) -> r a b", a=4), spread) \
                    .then_inc(S["zeros_stored"], 16)
            for b in range(NBLK):
                pool.dma_start(scratch["ybuf"][b * BLK:(b + 1) * BLK, :].rearrange("r (a b) -> r a b", a=4), spread) \
                    .then_inc(S["zeros_stored"], 16)
            pool.wait_ge(bank_done, JA["on0"])
            pool.dma_start(lnb, io["sgu_ln_b"].partition_broadcast(P)).then_inc(s_late, 16)
            pool.dma_start(bsp.rearrange("p a b -> p (a b)"), io["sgu_b"].partition_broadcast(P)).then_inc(s_late, 16)
            pool.wait_ge(S["zeros_stored"], 16 * (2 * NBLK + 1))
            pool.wait_ge(S["tok_ready"], 2 * NTX)
            pool.wait_ge(S["slots_ready"], 1)
            for k in range(2):
                for t in range(NTX):
                    pool.indirect_dma_start(scratch["xbuf"],
                                            bass.IndirectOffsetOnAxis(ap=slot[:, k * NTX + t:k * NTX + t + 1], axis=0),
                                            tok[:, t, :], None).then_inc(S["rows_stored"], 16)
            pool.wait_ge(S["rows_stored"], 16 * 2 * NTX)

            pool.wait_ge(S["moe_stored"], 1)
            for k in range(2):
                for t in range(NTX):
                    pool.indirect_dma_start(yg[:, k, t, :], None, scratch["ybuf"],
                                            bass.IndirectOffsetOnAxis(ap=slot[:, k * NTX + t:k * NTX + t + 1], axis=0)) \
                        .then_inc(S["moe_gathered"], 16)
            for dst, src in ((cc, io["s5_c"]), (bri, io["s5_b"]), (sp5[:, 0:3, :], io["s5_lam"]),
                             (phase[:], io["s5_phase"])):
                pool.dma_start(dst, src).then_inc(S["b_s5_in"], 16)
            pool.wait_ge(S["b_s5_u_made"], KT)
            pool.dma_start(scratch["ud"].rearrange("(k g) h s c -> (g h) k (s c)", k=KT),
                           u_s.rearrange("p k s c -> p k (s c)")).then_inc(S["b_s5_u_out"], 16)
            pool.wait_ge(S["b_s5_u_out"], 16)
            for s in range(S5T):
                pool.dma_start(u2[16 * s:16 * s + 16, :, :], scratch["ud"][:, :, s, :].rearrange("g h c -> h g c")) \
                    .then_inc(S["b_u2_in"], 16)
            for t in range(KT):
                pool.wait_ge(S["b_ksb_ready"], 2 * t + 2)
                pool.dma_start(scratch["kd"][8 * t:8 * t + 8].rearrange("g h k c -> h g (k c)"),
                               ksb[0:16].rearrange("p g k c -> p g (k c)")).then_inc(S["b_k_stored"], 16)
            pool.wait_ge(S["b_ys_stored"], 16 * S5T * KT)
            pool.dma_start(yn.rearrange("p k s c -> p k (s c)"),
                           scratch["yd"].rearrange("(k g) h s c -> (g h) k (s c)", k=KT)).then_inc(S["b_yn_in"], 16)
            pool.wait_ge(S["b_x_ready"], 2 * KT)
            for dst, src in ((cossin, io["cossin"]), (rope, io["rope"]), (half1, io["half1"])):
                pool.dma_start(dst, src).then_inc(S["b_rope_in"], 16)
            pool.wait_ge(S["b_bias0"], 1)
            nc.gpsimd.affine_select(out=bias[:, 0:P], in_=bias[:, 0:P], compare_op=ALU.is_ge, fill=MASKED, base=0,
                                    pattern=[[-1, P]], channel_multiplier=1).then_inc(S["b_masked"], 1)
            for t in range(1, NTX):
                pool.wait_ge(S["b_score_ready"], t)
                nc.gpsimd.affine_select(out=score[:, t * P:(t + 1) * P], in_=score[:, t * P:(t + 1) * P],
                                        compare_op=ALU.is_ge, fill=MASKED, base=0, pattern=[[-1, P]],
                                        channel_multiplier=1).then_inc(S["b_masked"], 1)
        @block.tensor
        def _(pe):
            unit, wide, mm, opened, by_columns, by_rows = products(pe, psum, phase_a)
            pe.wait_ge(s_cols, 32)
            for i, (name, sq, n) in enumerate((("ssx", sqx, T), ("ssc", sqc, TC))):
                pe.wait_ge(S["squares"], i + 1)
                ps = opened(name)
                for kt in range(KT):
                    ins = mm(ps[:, 0:n], ones[:], sq[:, kt, :], kt == 0, kt == KT - 1)
                ins.then_inc(bank_done, 1)
            pe.wait_ge(S["csilu_ready"], 1)
            for n in range(4):
                ps = opened(f"modrow{n}")
                for kt in range(KT):
                    ins = mm(ps[0:2, :], csilu[:, kt, :], wide(("mod", n), 4 * kt), kt == 0, kt == KT - 1)
                ins.then_inc(bank_done, 1)
            pe.wait_ge(s_const, 16 * 9)
            pe.wait_ge(S["modrow_ready"], 4)
            ps = opened("mod1")
            for b in range(16):
                ins = pe.transpose(ps[:, 2 * b:2 * b + 2], modrow[0:2, b // 4, (b % 4) * P:(b % 4 + 1) * P],
                                   ident[0:2, 0:2])
            ins.then_inc(bank_done, 1)
            hx = lambda kt: h1[:, kt, 0:T]
            hc = lambda kt: h1[:, kt, T:TA]
            pe.wait_ge(S["h1_ready"], 2 * KT)
            by_columns("lrx", ("lr", 0), hx, T, 64)
            by_columns("lrc", ("lr", 0), hc, TC, 64)
            for h in range(HEADS):
                by_columns(f"kx{h}", ("k", h), hx, T)
                by_columns(f"kc{h}", ("k", h), hc, TC)
            pe.wait_ge(S["mod_used"], 2 * KT)
            ps = opened("mod2")
            for b in range(32):
                ins = pe.matmul(ps[:, b:b + 1], modacc[:, b * P:(b + 1) * P], ones[:, 0:1], start=True, stop=True)
            ins.then_inc(bank_done, 1)
            pe.wait_ge(S["lr_ready"], 2)
            for d in range(2):
                for h in range(HEADS):
                    for s, a, b in (("x", 0, T), ("c", T, TA)):
                        ps = opened(f"la{s}{d}{h}")
                        pe.matmul(ps[:, 0:b - a], wgate[32 * d:32 * d + RANK, d, h * P:(h + 1) * P],
                                  lr[32 * d:32 * d + RANK, a:b], start=True, stop=True).then_inc(bank_done, 1)
            for h in range(HEADS):
                by_columns(f"q{h}", ("q", h), hx, T)

            for n in range(2):
                by_rows([f"v{n}{t}" for t in range(NTX + NTC)], ("v", n), h1, range(NTX + NTC))

            pe.wait_ge(S["v_ready"], 2 * (NTX + NTC))
            pe.wait_ge(S["state_zero"], 1)
            n_kst, n_att, n_state = 0, 0, [0, 0]
            for d, m, is_x, cs, last in gla_steps():
                at = (0 if is_x else T) + m * P
                tile = m if is_x else NTX + m
                pe.wait_ge(S["gla_in"], d + 1)
                ps = opened(f"kT{d}{is_x}{m}")
                for h in range(HEADS):
                    ins = pe.transpose(ps[:, h * P:(h + 1) * P], la[d][:, h, at:at + P], ident[:])
                ins.then_inc(bank_done, 1)
                if is_x:
                    ps = opened(f"att{d}{m}")
                    for h in range(HEADS):
                        ins = pe.matmul(ps[:, h * P:(h + 1) * P], kin[d][:, h, at:at + P], qin[d][:, h, at:at + P],
                                        start=True, stop=True)
                    ins.then_inc(bank_done, 1)
                    n_att += 1
                    pe.wait_ge(S["att_ready"], n_att)
                n_kst += 1
                pe.wait_ge(S["kst_ready"], n_kst)
                for n, c in enumerate(cs):
                    lo = 64 * c
                    if is_x:
                        ps = opened(f"o{d}{m}{c}")
                        pe.wait_ge(state_sem[d], n_state[d])
                        for h in range(HEADS):
                            for half in range(2):
                                o = ps[:, (2 * h + half) * GC:(2 * h + half + 1) * GC]
                                f = h * HV + half * P
                                pe.matmul(o, vv[lo:lo + 64, tile, f:f + P],
                                          att[lo:lo + 64, d, h * P + lo:h * P + lo + 64], start=True, stop=False)
                                ins = pe.matmul(o, state[:, d, h, half * P:(half + 1) * P],
                                                qin[d][:, h, at + lo:at + lo + GC], start=False, stop=True)
                        ins.then_inc(bank_done, 1)
                    if last and n == 1:
                        continue
                    for i in range(2):
                        ps = opened(f"st{d}{is_x}{m}{c}{i}")
                        for h in (2 * i, 2 * i + 1):
                            ins = pe.matmul(ps[:, (h % 2) * HV:(h % 2 + 1) * HV],
                                            kst[lo:lo + 64, d, h * P:(h + 1) * P],
                                            vv[lo:lo + 64, tile, h * HV:(h + 1) * HV], start=True, stop=True)
                        ins.then_inc(bank_done, 1)
                    n_state[d] += 4

            pe.wait_ge(S["sqo_ready"], 1)
            for h in range(HEADS):
                ps = opened(f"on{h}")
                for i in range(2):
                    ins = pe.matmul(ps[:], ones[:], sqo[:, 2 * h + i, :], start=(i == 0), stop=(i == 1))
                ins.then_inc(bank_done, 1)
            for j in range(KT):
                by_columns(f"r{j}", ("r", j), hx, T)
            for n in range(2):
                by_rows([f"zv{n}{t}" for t in range(NTX)], ("zv", n), h1, range(NTX))
            for w in ("zu", "gb", "ga"):
                for j in range(KT):
                    by_columns(f"{w}{j}", (w, j), hx, T)
            pe.wait_ge(S["ob_ready"], KT)
            for j in range(KT):
                by_columns(f"wb{j}", ("wb", j), lambda kt: oo[:, kt, :], T)
            pe.wait_ge(S["zv_ready"], NTX)
            for j in range(KT):
                ps = opened(f"mix{j}")
                for t in range(NTX):
                    ins = pe.matmul(ps[:, t * P:(t + 1) * P], zv[:, t, j * P:(j + 1) * P], wsp[:, j, :],
                                    start=True, stop=True)
                ins.then_inc(bank_done, 1)
            pe.wait_ge(S["zu_ready"], KT)
            for j in range(KT):
                by_columns(f"wa{j}", ("wa", j), lambda kt: zu[:, kt, :], T)
            pe.wait_ge(S["y_ready"], KT)
            for j in range(KT):
                by_columns(f"wout{j}", ("wout", j), lambda kt: yy[:, kt, :], T)
            pe.wait_ge(S["squares"], 3)
            ps = opened("ss2")
            for kt in range(KT):
                ins = pe.matmul(ps[:], ones[:], sqo[:, kt, :], start=(kt == 0), stop=(kt == KT - 1))
            ins.then_inc(bank_done, 1)
            pe.wait_ge(S["h2_ready"], KT)
            for t in range(NTX):
                for n in range(2):
                    ps = opened(f"tok{t}{n}")
                    for i in range(4):
                        ins = pe.transpose(ps[:, i * P:(i + 1) * P], h2[:, 4 * n + i, t * P:(t + 1) * P], ident[:])
                    ins.then_inc(bank_done, 1)
            ps = opened("route")
            for t in range(NTX):
                o = ps[:, t * NE:(t + 1) * NE]
                pe.matmul(o, ones[0:1, :], brow[:], start=True, stop=False)
                for kt in range(KT):
                    ins = pe.matmul(o, h2[:, kt, t * P:(t + 1) * P], wrt[:, kt, :], start=False, stop=(kt == KT - 1))
            ins.then_inc(bank_done, 1)
            pe.wait_ge(S["onehot"], 1)
            ps = opened("rank")
            for t in range(NTX + 1):
                o = ps[:, t * NE:(t + 1) * NE]
                for u in range(t):
                    ins = pe.matmul(o, ones[:], hot[:, u, :], start=(u == 0), stop=(t == NTX and u == NTX - 1))
                if t < NTX:
                    ins = pe.matmul(o, tri[:], hot[:, t, :], start=(t == 0), stop=True)
            ins.then_inc(bank_done, 1)

            n_blocks = load_plan(pe)
            for b in range(8):
                pe.wait_ge(bank_free[b], sum(n % 8 == b for n in JA.values()))
                pe.sem_inc(bank_free_e[b], 1)
            pe.sem_inc(weights_used_e, RING_E - 1)

            def turn(ps, src, n):
                for q in range(4):
                    ins = pe.transpose(ps[:, q * P:(q + 1) * P], src[:, (4 * n + q) * P:(4 * n + q + 1) * P], ident[:])
                ins.then_inc(bank_done_e, 1)

            pe.wait_ge(S["x_row_in"], 16)
            for n in range(2):
                pe.wait_ge(bank_free_e[n], 1)
                turn(psum[n], xrow, n)
            with pe.Fori(0, n_blocks) as i:
                def opened_e(name):
                    bank, use = bank_e[name]
                    before = 1 if bank < 2 else 0
                    pe.wait_ge(bank_free_e[bank], i * uses_e[bank] + (before + use + 1))
                    return psum[bank]

                def chunk_e(c):
                    pe.wait_ge(weights_in_e[c % RING_E], i * (16 * CHUNKS_E // RING_E) + 16 * (c // RING_E + 1))
                    return ring_e[c % RING_E]

                def up_half(name, n, c0):
                    ps = opened_e(name)
                    for kt in range(KT):
                        if kt % 4 == 0:
                            slot_e = chunk_e(c0 + kt // 4)
                        ins = pe.matmul(ps[:], xcol[:, kt, :], slot_e[:, (kt % 4) * 512:(kt % 4 + 1) * 512],
                                        start=(kt == 0), stop=(kt == KT - 1))
                        if kt % 4 == 0:
                            ins.then_inc(weights_used_e, 1)
                    ins.then_inc(bank_done_e, 1)

                def turn_h(n):
                    pe.wait_ge(S["h_made"], i * 3 + (n + 1))
                    turn(opened_e(f"h{n}"), hh, n)

                pe.wait_ge(S["x_turned"], i * 2 + 2)
                for n in range(2):
                    up_half(f"g{n}", n, 4 * n)
                    up_half(f"u{n}", n, 4 * n + 2)
                turn_h(0)
                up_half("g2", 2, 8)
                up_half("u2", 2, 10)
                turn_h(1)
                pe.wait_ge(S["x_row_in"], i * 16 + 32)
                turn(opened_e("xa"), xrow, 0)
                turn(opened_e("xb"), xrow, 1)
                turn_h(2)
                down = [opened_e("d0"), opened_e("d1")]
                for kt in range(FET):
                    if kt % 4 == 0:
                        pe.wait_ge(S["h_turned"], i * 3 + (kt // 4 + 1))
                    if kt % 2 == 0:
                        slot_e = chunk_e(12 + kt // 2)
                    for n in range(2):
                        ins = pe.matmul(down[n][:], hcol[:, kt, :],
                                        slot_e[:, (kt % 2) * D + n * 512:(kt % 2) * D + (n + 1) * 512],
                                        start=(kt == 0), stop=(kt == FET - 1))
                        if kt % 2 == 0 and n == 0:
                            ins.then_inc(weights_used_e, 1)
                        if kt == FET - 1:
                            ins.then_inc(bank_done_e, 1)

            pe.wait_ge(S["moe_stored"], 1)
            pe.wait_ge(S["moe_dve_done"], 1)
            pe.wait_ge(S["moe_summed"], NTX)
            for j in range(KT):
                ps = opened(f"y{j}")
                for t in range(NTX):
                    ins = pe.transpose(ps[:, t * P:(t + 1) * P], yg[:, 0, t, j * P:(j + 1) * P], ident[:])
                ins.then_inc(bank_done, 1)

            def squares(n):
                pe.wait_ge(S["b_sq_full"], n + 1)
                ps = opened(f"sn{n}")
                for kt in range(KT):
                    ins = pe.matmul(ps[:], ones[:], sqb[:, kt, :], start=(kt == 0), stop=(kt == KT - 1))
                ins.then_inc(bank_done, 1)

            squares(0)
            squares(1)
            for t in range(KT):
                pe.wait_ge(S["b_qb_ready"], 2 * t + 2)
                for i in range(4):
                    ps = opened(f"qt{t}{i}")
                    for n in range(4):
                        g, f = 2 * i + n // 2, n % 2
                        ins = pe.transpose(ps[:, n * P:(n + 1) * P],
                                           qb[:, f, g, :, :].rearrange("p s h -> p (s h)"), ident[:])
                    ins.then_inc(bank_done, 1)
                pe.wait_ge(S["b_cp_ready"], KT)
                for i in range(2):
                    ps = opened(f"kk{t}{i}")
                    for n in range(4):
                        g = 4 * i + n
                        ins = pe.matmul(ps[0:16, n * P:(n + 1) * P], qb[:, 0, g, S5T - 1, :],
                                        cp[:, 8 * t + g, 0:S5T, :].rearrange("p k h -> p (k h)"),
                                        start=True, stop=True)
                    ins.then_inc(bank_done, 1)
                pe.wait_ge(S["b_qt_ready"], 4 * t + 4)
                if t == 0:
                    pe.wait_ge(S["b_u2_in"], 16 * S5T)
                for i in range(2):
                    ps = opened(f"s{t}{i}")
                    for n in range(4):
                        for f in range(2):
                            g = 4 * i + n
                            o = (2 * n + f) * S5C
                            ins = pe.matmul(ps[:, o:o + S5C], qt[:, g, f, :], u2[:, 8 * t + g, :],
                                            start=True, stop=True)
                    ins.then_inc(bank_done, 1)
            pe.wait_ge(S["b_scanned"], 1)
            for t in range(KT):
                pe.wait_ge(mt_sem[t % 2], 16 * S5T * (t // 2 + 1))
                ps = opened(f"ys{t}")
                for n in range(8):
                    g = 8 * t + n
                    pe.matmul(ps[:, n * S5C:(n + 1) * S5C], mt[t % 2][:, n, :], u2[:, g, :], start=True, stop=False)
                    ins = pe.matmul(ps[:, n * S5C:(n + 1) * S5C],
                                    cp[:, g, 1:S5T + 1, :].rearrange("p k h -> p (k h)"), xs[:, 0:S5C, 0, g],
                                    start=False, stop=True)
                ins.then_inc(bank_done, 1)
            by_columns, by_rows = split_products(pe, psum, phase_b)
            pe.wait_ge(split_ready, KT)
            for b in range(2 * KT):
                by_columns(f"glu{b}", ("glu", b), lambda kt: (high_g[:, kt, :], low_b[:, kt, :]))

            def dense(n):
                squares(2 + 2 * n)
                pe.wait_ge(split_ready, (2 + 3 * n) * KT + n * FFT)
                for b in range(2 * FFT):
                    by_columns(f"gu{n}{b}", (f"gu{n}", b), lambda kt: (high_b[:, kt, :], low_b[:, kt, :]))
                pe.wait_ge(split_ready, (2 + 3 * n) * KT + (n + 1) * FFT)
                for j in range(KT):
                    by_columns(f"down{n}{j}", (f"down{n}", j), hid, depth=FFT)

            dense(0)
            squares(3)
            pe.wait_ge(split_ready, 3 * KT + FFT)
            pe.wait_ge(S["b_rope_in"], 48)
            for s in range(NR + 2):
                if s < NR:
                    if s == 2 * KT:
                        for n in range(2):
                            by_rows([f"dv{n}{t}" for t in range(NTX)], ("dv", n), high_b, low_p)
                    by_columns(f"pr{s}", (ROPED[s][0], ROPED[s][1]), lambda kt: (high_b[:, kt, :], low_p[:, kt, :]))
                if 1 <= s <= NR and ROPED[s - 1][2]:
                    pe.wait_ge(S["b_sqt_ready"], norm_index[s - 1] + 1)
                    ps = opened(f"pn{s - 1}")
                    pe.matmul(ps[:], half1, sqt[:, norm_index[s - 1] % 2, :], start=True, stop=True) \
                        .then_inc(bank_done, 1)
                if s >= 2:
                    if ROPED[s - 2][2]:
                        pe.wait_ge(S["b_normed_q"], norm_index[s - 2] + 1)
                    else:
                        pe.wait_ge(S["b_raw_ready"], s - 1)
                    ps = opened(f"rot{s - 2}")
                    pe.matmul(ps[:], rope, roped_tile(s - 2), start=True, stop=True).then_inc(bank_done, 1)
            ps = opened("wi")
            for t in range(NTX):
                for kt in range(KT):
                    for part in (high_b, low_p):
                        ins = pe.matmul(ps[:, t * IH:(t + 1) * IH], part[:, kt, t * P:(t + 1) * P].bitcast(F32),
                                        wiw[:, kt, :], start=(kt == 0 and part is high_b),
                                        stop=(kt == KT - 1 and part is low_p))
            ins.then_inc(bank_done, 1)
            pe.wait_ge(S["b_rotated"], NR)
            pe.wait_ge(S["b_v_rows"], 2 * NTX)
            for s in range(NPAIR + 3):
                if 2 <= s < NPAIR + 2:
                    t, h = PAIRS[s - 2]
                    pe.wait_ge(S["b_diag_ready"], s - 1)
                    ps = opened(f"pt{s - 2}")
                    for b in range(t + 1):
                        ins = pe.matmul(ps[:, b * P:(b + 1) * P], pp[:, (s - 2) % 4, b * P:(b + 1) * P],
                                        diag[:, (s - 2) % 4, :], start=True, stop=True)
                    ins.then_inc(bank_done, 1)
                if s >= 3:
                    t, h = PAIRS[s - 3]
                    pe.wait_ge(S["b_pt_ready"], s - 2)
                    if h % 2 == 0:
                        ps = opened(f"av{s - 3}")
                        av = ps
                    r = 64 * (h % 2)
                    for b in range(t + 1):
                        ins = pe.matmul(av[r:r + 64, 0:P], vt[:, b, h * HD:(h + 1) * HD],
                                        pT[:, (s - 3) % 2, b * P:(b + 1) * P], start=(b == 0), stop=(b == t))
                    ins.then_inc(av_done if h % 2 else bank_done, 1)
                if s < NPAIR:
                    t, h = PAIRS[s]
                    if h == 0 and t > 0:
                        for i in range(IH):
                            ps = opened(f"ix{t}{i}")
                            r = 64 * (i % 2)
                            pe.matmul(ps[:, 0:(t + 1) * P], qiT[r:r + 64, i // 2, t * P:(t + 1) * P],
                                      kiT[r:r + 64, 0:(t + 1) * P], start=True, stop=True).then_inc(bank_done, 1)
                    ps = opened(f"lg{s}")
                    r = 64 * (h % 2)
                    pe.matmul(ps[:, 0:(t + 1) * P], qT[r:r + 64, h // 2, t * P:(t + 1) * P],
                              kT[r:r + 64, h // 2, 0:(t + 1) * P], start=True, stop=True).then_inc(bank_done, 1)
            pe.wait_ge(split_ready, 4 * KT + FFT)
            for j in range(KT):
                by_columns(f"wo{j}", ("wo", j), lambda kt: (high_b[:, kt, :], low_b[:, kt, :]))
            dense(1)

        @block.scalar
        def _(act):
            steps = [0]

            def link(ins):
                steps[0] += 1
                ins.then_inc(act_step, 1)
                act.wait_ge(act_step, steps[0])

            act.dma_start(cols[:], io["cols"]).then_inc(s_cols, 16)
            act.dma_start(ones[:], io["ones"]).then_inc(s_cols, 16)
            act.wait_ge(s_cols, 32)
            cc = colspan("c").rearrange("p (s k) -> p k s", s=2)
            nc.scalar.activation(csilu[:], cc, ACT.Silu).then_inc(S["csilu_ready"], 1)
            act.wait_ge(s_x, 16)
            nc.scalar.activation(sqx, x, ACT.Square).then_inc(S["squares"], 1)
            act.wait_ge(s_ctx, 16)
            nc.scalar.activation(sqc, ctxt, ACT.Square).then_inc(S["squares"], 1)
            act.wait_ge(S["variance"], 2)
            nc.scalar.activation(rs1, rs1, ACT.Sqrt).then_inc(S["root"], 1)
            for n in range(4):
                ps = result(act, f"modrow{n}")
                nc.scalar.activation(modrow[0:2, n, :], ps[0:2, :], ACT.Copy).then_inc(S["modrow_ready"], 1)
                act.wait_ge(S["modrow_ready"], n + 1)
                act.sem_inc(free(f"modrow{n}"), 1)
            act.wait_ge(S["mod1_ready"], 3)
            act.wait_ge(S["normed1"], 2)
            for kt in range(KT):
                for s, (a, b) in enumerate(((0, T), (T, TA))):
                    nc.scalar.activation(h1[:, kt, a:b], h1[:, kt, a:b], ACT.Identity, bias=modc[:, kt, s:s + 1],
                                         scale=scale1[:, kt, s:s + 1]).then_inc(S["h1_ready"], 1)
            for name, a, b in (("lrx", 0, T), ("lrc", T, TA)):
                ps = result(act, name)
                nc.scalar.activation(lr[0:64, a:b], ps[0:64, 0:b - a], ACT.Copy).then_inc(S["lr_ready"], 1)
                act.wait_ge(S["lr_ready"], 1 + (a > 0))
                act.sem_inc(free(name), 1)
            for h in range(HEADS):
                for s, a, b in (("x", 0, T), ("c", T, TA)):
                    ps = result(act, f"k{s}{h}")
                    nc.scalar.activation(kk[:, h, a:b], ps[:, 0:b - a], ACT.Copy).then_inc(free(f"k{s}{h}"), 1)
            for d in range(2):
                act.wait_ge(S["z_ready"], d + 1)
                zf = la[d].rearrange("p a b -> p (a b)")
                link(nc.scalar.activation(eb, zf, ACT.Abs))
                link(nc.scalar.activation(eb, eb, ACT.Exp, scale=-1.0))
                nc.scalar.activation(eb, eb, ACT.Ln, bias=1.0).then_inc(S["softplus"], 1)
                act.wait_ge(S["b_ready"], d + 1)
                nc.scalar.activation(decay[:, d, :], blast[:, d, :], ACT.Exp, scale=1.0 / 16).then_inc(S["decay_ready"], 1)
                ebx = eb[:, 0:HEADS * T].rearrange("p (a b) -> p a b", a=HEADS)
                if d == 0:
                    for h in range(HEADS):
                        ps = result(act, f"q{h}")
                        nc.scalar.activation(qq[:, h, :], ps[:], ACT.Copy, scale=float(HK) ** -0.5) \
                            .then_inc(free(f"q{h}"), 1)
                nc.scalar.activation(ebx, la[d][:, :, 0:T], ACT.Exp, scale=1.0 / 16).then_inc(S["eb_full"], 1)
                act.wait_ge(S["eb_used"], 2 * d + 1)
                nc.scalar.activation(ebx, la[d][:, :, 0:T], ACT.Exp, scale=-1.0 / 16).then_inc(S["eb_full"], 1)
                act.wait_ge(S["kexp_in"], d + 1)
                nc.scalar.activation(zf, zf, ACT.Exp, scale=1.0 / 16).then_inc(S["kexp_out"], 1)
            n_v = 0
            for n in range(2):
                for t in range(NTX + NTC):
                    ps = result(act, f"v{n}{t}")
                    nc.scalar.activation(vv[:, t, n * 512:(n + 1) * 512], ps[:], ACT.Copy).then_inc(S["v_ready"], 1)
                    n_v += 1
                    act.wait_ge(S["v_ready"], n_v)
                    act.sem_inc(free(f"v{n}{t}"), 1)
            step = [0, 0]
            n_kst = n_first = 0
            for d, m, is_x, cs, last in gla_steps():
                ps = result(act, f"kT{d}{is_x}{m}")
                nc.scalar.activation(kst[:, d, :], ps[:], ACT.Copy).then_inc(S["kst_ready"], 1)
                n_kst += 1
                act.wait_ge(S["kst_ready"], n_kst)
                act.sem_inc(free(f"kT{d}{is_x}{m}"), 1)
                for c in cs:
                    if is_x:
                        if step[d] < 4:
                            if n_first == 0:
                                act.wait_ge(S["zeros_stored"], 16 * (2 * NBLK + 1))
                            ps = result(act, f"o{d}{m}{c}")
                            nc.scalar.activation(oo[:, :, m * P + c * GC:m * P + c * GC + GC],
                                                 ps.rearrange("p (f t) -> p f t", t=GC), ACT.Copy) \
                                .then_inc(S["o_first"], 1)
                            n_first += 1
                            act.wait_ge(S["o_first"], n_first)
                            act.sem_inc(free(f"o{d}{m}{c}"), 1)
                        step[d] += 1
            act.wait_ge(S["o_done"], 8)
            nc.scalar.activation(sqo, oo, ACT.Square).then_inc(S["sqo_ready"], 1)
            act.wait_ge(S["variance"], 2 + HEADS)
            nc.scalar.activation(rso, rso, ACT.Sqrt).then_inc(S["root"], 1)
            for j in range(KT):
                ps = result(act, f"r{j}")
                if j >= 2:
                    act.wait_ge(S["ob_ready"], j - 1)
                nc.scalar.activation(rtmp[:, j % 2, :], ps[:], ACT.Silu).then_inc(S["silu_r"], 1)
                act.wait_ge(S["silu_r"], j + 1)
                act.sem_inc(free(f"r{j}"), 1)
            n_z = 0
            for n in range(2):
                for t in range(NTX):
                    ps = result(act, f"zv{n}{t}")
                    nc.scalar.activation(zv[:, t, n * 512:(n + 1) * 512], ps[:], ACT.Gelu_apprx_tanh) \
                        .then_inc(S["gelu_done"], 1)
                    n_z += 1
                    act.wait_ge(S["gelu_done"], n_z)
                    act.sem_inc(free(f"zv{n}{t}"), 1)
            for j in range(KT):
                ps = result(act, f"zu{j}")
                nc.scalar.activation(zu[:, j, :], ps[:], ACT.Gelu_apprx_tanh).then_inc(S["gelu_done"], 1)
                act.wait_ge(S["gelu_done"], 2 * NTX + j + 1)
                act.sem_inc(free(f"zu{j}"), 1)
            act.wait_ge(S["variance"], 2 + HEADS + NTX)
            nc.scalar.activation(varz[:], varz[:], ACT.Sqrt).then_inc(S["root"], 1)
            for w, dst, key, first in (("gb", sgb, "sgb_ready", KT), ("ga", sga, "sga_ready", 0)):
                for j in range(KT):
                    ps = result(act, f"{w}{j}")
                    nc.scalar.activation(dst[:, j, :], ps[:], ACT.Sigmoid, bias=col("b_branch", first + j)) \
                        .then_inc(S[key], 1)
                    act.wait_ge(S[key], j + 1)
                    act.sem_inc(free(f"{w}{j}"), 1)
            act.wait_ge(S["x1_ready"], KT)
            nc.scalar.activation(sqo, x, ACT.Square).then_inc(S["squares"], 1)
            act.wait_ge(S["variance"], 3 + HEADS + NTX)
            nc.scalar.activation(rs2, rs2, ACT.Sqrt).then_inc(S["root"], 1)
            act.wait_ge(S["normed2"], 1)
            for kt in range(KT):
                nc.scalar.activation(h2[:, kt, :], h2[:, kt, :], ACT.Identity, bias=modc[:, 24 + kt, 0:1],
                                     scale=scale2[:, kt:kt + 1]).then_inc(S["h2_ready"], 1)
            for t in range(NTX):
                for n in range(2):
                    ps = result(act, f"tok{t}{n}")
                    nc.scalar.activation(tok[:, t, n * 512:(n + 1) * 512], ps[:], ACT.Copy).then_inc(S["tok_ready"], 1)
                    act.wait_ge(S["tok_ready"], 2 * t + n + 1)
                    act.sem_inc(free(f"tok{t}{n}"), 1)
            act.wait_ge(S["logit_max"], 1)
            nc.scalar.activation(prob[:], prob[:], ACT.Exp).then_inc(S["logit_exp"], 1)


            n_blocks = load_plan(act)

            def turned(name, dst, ps, done, count):
                nc.scalar.activation(dst, ps, ACT.Copy).then_inc(done, 1)
                act.wait_ge(done, count)
                act.sem_inc(bank_free_e[bank_e[name][0]], 1)

            for n in range(2):
                act.wait_ge(bank_done_e, n + 1)
                turned(f"x{'ab'[n]}", xcol[:, 4 * n:4 * n + 4, :].rearrange("p a b -> p (a b)"), psum[n][:],
                       S["x_turned"], n + 1)
            act.sem_inc(S["y_stored"], 16)
            with act.Fori(0, n_blocks) as i:
                for n in range(3):
                    ps = result_e(act, i, f"g{n}")
                    nc.scalar.activation(hs[:, n, :], ps[:], ACT.Silu).then_inc(S["sig_ready"], 1)
                    act.wait_ge(S["sig_ready"], i * 3 + (n + 1))
                    act.sem_inc(bank_free_e[bank_e[f"g{n}"][0]], 1)
                    if n:
                        turned(f"h{n - 1}", hcol[:, 4 * n - 4:4 * n, :].rearrange("p a b -> p (a b)"),
                               result_e(act, i, f"h{n - 1}")[:], S["h_turned"], i * 3 + n)
                for n in range(2):
                    turned(f"x{'ab'[n]}", xcol[:, 4 * n:4 * n + 4, :].rearrange("p a b -> p (a b)"),
                           result_e(act, i, f"x{'ab'[n]}")[:], S["x_turned"], i * 2 + (3 + n))
                turned("h2", hcol[:, 8:12, :].rearrange("p a b -> p (a b)"), result_e(act, i, "h2")[:],
                       S["h_turned"], i * 3 + 3)
                act.wait_ge(S["y_stored"], i * 16 + 16)
                for n in range(2):
                    turned(f"d{n}", yrow[:, n * 512:(n + 1) * 512], result_e(act, i, f"d{n}")[:],
                           S["y_copied"], i * 2 + (n + 1))
                act.dma_start(scratch["ybuf"][bass.ds(i * BLK, BLK), :], yrow).then_inc(S["y_stored"], 16)
            act.wait_ge(S["y_stored"], n_blocks * 16 + 16)
            act.sem_inc(S["moe_stored"], 1)

            def squared(n, wait, count):
                act.wait_ge(wait, count)
                nc.scalar.activation(sqb, x, ACT.Square).then_inc(S["b_sq_full"], 1)
                act.wait_ge(S["variance"], NORMS_A + n + 1)
                nc.scalar.activation(RS[:], RS[:], ACT.Sqrt).then_inc(S["root"], 1)

            act.wait_ge(S["b_s5_in"], 64)
            link(nc.scalar.activation(sp5[:, 3, :], sp5[:, 2, :], ACT.Exp))
            act.sem_inc(S["b_coef_exp"], 1)
            act.wait_ge(S["b_coef_ready"], 1)
            link(nc.scalar.activation(sp5[:, 4, :], sp5[:, 4, :], ACT.Exp))
            nc.scalar.activation(sp5[:, 8:12, :], sp5[:, 8:12, :], ACT.Sin).then_inc(S["b_coef_exp"], 1)
            squared(0, S["b_x2_ready"], KT)
            squared(1, S["b_x2_ready"], 2 * KT)
            for t in range(KT):
                for i in range(4):
                    ps = result(act, f"qt{t}{i}")
                    copied(act, nc.scalar.activation(qt[:, 2 * i:2 * i + 2, :, :].rearrange("p g f n -> p (g f n)"),
                                                     ps[:], ACT.Copy), S["b_qt_ready"], 4 * t + i + 1, f"qt{t}{i}")
                if t:
                    act.wait_ge(S["b_k_stored"], 16 * t)
                for i in range(2):
                    ps = result(act, f"kk{t}{i}")
                    copied(act, nc.scalar.activation(ksb[0:16, 4 * i:4 * i + 4, S5T:2 * S5T, :],
                                                     ps[0:16, :].rearrange("p (g k h) -> p g k h", g=4, h=S5H),
                                                     ACT.Copy), S["b_ksb_ready"], 2 * t + i + 1, f"kk{t}{i}")
                for i in range(2):
                    ps = result(act, f"s{t}{i}")
                    g = 8 * t + 4 * i
                    copied(act, nc.scalar.activation(xs[:, 1:S5C + 1, :, g:g + 4],
                                                     ps.rearrange("p (g f c) -> p c f g", g=4, f=2), ACT.Copy),
                           S["b_s_copied"], 2 * t + i + 1, f"s{t}{i}")
            for t in range(KT):
                ps = result(act, f"ys{t}")
                if t:
                    act.wait_ge(S["b_ys_stored"], 16 * S5T * t)
                copied(act, nc.scalar.activation(ys2, ps.rearrange("p (g c) -> p g c", g=8), ACT.Copy),
                       S["b_ys_copied"], t + 1, f"ys{t}")
                for s in range(S5T):
                    act.dma_start(scratch["yd"][8 * t:8 * t + 8, :, s, :].rearrange("g h c -> h g c"),
                                  ys2[16 * s:16 * s + 16, :, :]).then_inc(S["b_ys_stored"], 16)
            for kt in range(KT):
                act.wait_ge(S["b_y5_ready"], kt + 1)
                nc.scalar.activation(hb[:, kt, :], hb[:, kt, :], ACT.Gelu_apprx_tanh).then_inc(S["b_g5_ready"], 1)
            split_to = [0]
            weights_high_part(act, 1, split_to)

            def high_part(dst, src, ready, first):
                for kt in range(KT):
                    act.wait_ge(ready, first + kt + 1)
                    nc.scalar.activation(dst[:, kt, :], src[:, kt, :], ACT.Copy).then_inc(high_ready, 1)

            high_part(high_g, hb, S["b_g5_ready"], 0)
            n_sig = 0
            for j in range(KT):
                for i in range(2):
                    weights_high_part(act, ahead("glu", "glu", 2 * j + i), split_to)
                ps = result(act, f"glu{2 * j + 1}")
                if n_sig >= 2:
                    act.wait_ge(S["b_st_used"], n_sig - 1)
                n_sig += 1
                copied(act, nc.scalar.activation(st[:, j % 2, :], ps[:], ACT.Sigmoid), S["b_sig_b"], n_sig,
                       f"glu{2 * j + 1}")

            def dense_act(n, n_sig):
                high_part(high_b, raw, S["b_h_full"], h_count[2 + 2 * n] - KT)
                for j in range(FFT):
                    weights_high_part(act, ahead(f"down{n}", f"gu{n}", 2 * j), split_to)
                    ps = result(act, f"gu{n}{2 * j}")
                    act.wait_ge(S["b_st_used"], n_sig - 1)
                    n_sig += 1
                    copied(act, nc.scalar.activation(st[:, j % 2, :], ps[:], ACT.Silu), S["b_sig_b"], n_sig,
                           f"gu{n}{2 * j}")
                    if j < FFT - 1:
                        weights_high_part(act, ahead(f"down{n}", f"gu{n}", 2 * j + 1), split_to)
                    act.wait_ge(product_ready, FFT * n + j + 1)
                    nc.scalar.activation(hid(j)[0], product[:, j % 3, :], ACT.Copy).then_inc(high_ready, 1)
                for j in range(KT):
                    weights_high_part(act, ahead(f"down{n}", f"down{n}", j, FFT), split_to)
                return n_sig

            squared(2, S["b_x_ready"], KT)
            n_sig = dense_act(0, n_sig)
            squared(3, S["b_x_ready"], 2 * KT)
            high_part(high_b, raw, S["b_h_full"], h_count[3] - KT)
            n_row = 0
            for s in range(NR + 1):
                if s == 2 * KT:
                    for n in range(2):
                        weights_high_part(act, ahead("dki", "dv", n, KT, True), split_to)
                        for t in range(NTX):
                            ps = result(act, f"dv{n}{t}")
                            n_row += 1
                            copied(act, nc.scalar.activation(vt[:, t, n * 512:(n + 1) * 512], ps[:], ACT.Copy),
                                   S["b_v_rows"], n_row, f"dv{n}{t}")
                if s < NR:
                    weights_high_part(act, ahead("dki", ROPED[s][0], ROPED[s][1]), split_to)
                    ps = result(act, f"pr{s}")
                    if ROPED[s][2]:
                        k = norm_index[s]
                        if k >= 2:
                            act.wait_ge(bank_done, JB[f"pn{norm_of[k - 2]}"] + 1)
                        nc.scalar.activation(sqt[:, k % 2, :], ps[:], ACT.Square).then_inc(S["b_sqt_ready"], 1)
                    copied(act, nc.scalar.activation(roped_tile(s), ps[:], ACT.Copy), S["b_raw_ready"], s + 1, f"pr{s}")
                if s >= 1 and ROPED[s - 1][2]:
                    k = norm_index[s - 1]
                    act.wait_ge(S["b_rvar"], k + 1)
                    nc.scalar.activation(rst[:, k % 2, :], rst[:, k % 2, :], ACT.Sqrt).then_inc(S["b_rroot"], 1)
            n_relu = 0
            for s in range(NPAIR + 3):
                if 1 <= s <= NPAIR:
                    t, h = PAIRS[s - 1]
                    b = (s - 1) % 4
                    act.wait_ge(S["b_logits"], s)
                    nc.scalar.activation(pp[:, b, 0:(t + 1) * P], pp[:, b, 0:(t + 1) * P], ACT.Exp,
                                         bias=nmx[:, b:b + 1], scale=float(HD) ** -0.5,
                                         accum_out=sm[:, b:b + 1]).then_inc(S["b_exped"], 1)
                if 2 <= s < NPAIR + 2:
                    t, h = PAIRS[s - 2]
                    ps = result(act, f"pt{s - 2}")
                    if s >= 4 and (s - 4) % 2 == 1:
                        act.wait_ge(av_done, (s - 4) // 2 + 1)
                    elif s >= 4:
                        act.wait_ge(bank_done, JB[f"pt{s - 2}"] + 1)
                    copied(act, nc.scalar.activation(pT[:, (s - 2) % 2, 0:(t + 1) * P], ps[:, 0:(t + 1) * P],
                                                     ACT.Copy), S["b_pt_ready"], s - 1, f"pt{s - 2}")
                if s >= 3 and (s - 3) % 2 == 1:
                    t, h = PAIRS[s - 3]
                    name = f"av{s - 4}"
                    act.wait_ge(av_done, (s - 3) // 2 + 1)
                    copied(act, nc.scalar.activation(oT[:, h // 2, t * P:(t + 1) * P], psum[JB[name] % 8][:, 0:P],
                                                     ACT.Copy), S["b_o_ready"], (s - 3) // 2 + 1, name)
                if s < NPAIR:
                    t, h = PAIRS[s]
                    if h == 0 and t > 0:
                        for i in range(IH):
                            ps = result(act, f"ix{t}{i}")
                            if n_relu >= 2:
                                act.wait_ge(relu_used, n_relu - 1)
                            n_relu += 1
                            copied(act, nc.scalar.activation(rl[:, i % 2, 0:(t + 1) * P], ps[:, 0:(t + 1) * P],
                                                             ACT.Relu), S["b_relu_ready"], n_relu, f"ix{t}{i}")
            act.wait_ge(S["b_o_ready"], NPAIR // 2)
            high_part(high_b, oT, S["b_o_ready"], NPAIR // 2 - KT)
            for j in range(KT):
                weights_high_part(act, ahead("wo", "wo", j), split_to)
            squared(4, S["b_x_ready"], 3 * KT)
            dense_act(1, n_sig)
        @block.vector
        def _(dve):
            steps = [0]

            def link(ins):
                steps[0] += 1
                ins.then_inc(dve_step, 1)
                dve.wait_ge(dve_step, steps[0])

            dve.wait_ge(s_cols, 32)
            for i, (name, a, b) in enumerate((("ssx", 0, T), ("ssc", T, TA))):
                ps = result(dve, name)
                nc.vector.tensor_scalar(rs1[:, a:b], ps[:, 0:b - a], 1.0 / D, EPS, ALU.mult, ALU.add) \
                    .then_inc(S["variance"], 1)
                dve.wait_ge(S["variance"], i + 1)
                dve.sem_inc(free(name), 1)
            dve.wait_ge(S["root"], 1)
            link(nc.vector.reciprocal(rs1, rs1))
            nc.vector.tensor_tensor(h1[:, :, 0:T], x, rs1[:, 0:T].unsqueeze(1).to_broadcast([P, KT, T]), ALU.mult) \
                .then_inc(S["normed1"], 1)
            nc.vector.tensor_tensor(h1[:, :, T:TA], ctxt, rs1[:, T:TA].unsqueeze(1).to_broadcast([P, KT, TC]),
                                    ALU.mult).then_inc(S["normed1"], 1)
            dve.wait_ge(S["normed1"], 2)
            ps = result(dve, "mod1")
            link(nc.vector.tensor_tensor(modc[:, 0:16, :], ps[:, 0:32].rearrange("p (b s) -> p b s", s=2),
                                         colspan("b_mod")[:, 0:16].unsqueeze(2).to_broadcast([P, 16, 2]), ALU.add))
            dve.sem_inc(free("mod1"), 1)
            link(nc.vector.tensor_scalar(scale1[:], modc[:, 8:16, :], 1.0, None, ALU.add))
            link(nc.vector.tensor_tensor(scale1[:], scale1[:],
                                         colspan("g_norm1").unsqueeze(2).to_broadcast([P, KT, 2]), ALU.mult))
            dve.sem_inc(S["mod1_ready"], 3)
            dve.wait_ge(S["csilu_ready"], 1)
            for c in range(2 * KT):
                kt, half = c // 2, modacc[:, c % 2 * 2 * D:(c % 2 + 1) * 2 * D]
                dve.wait_ge(mod_in[c % 2], 16 * (c // 2 + 1))
                if kt == 0:
                    ins = nc.vector.tensor_scalar(half, ring_m[c % 2], csilu[:, kt, 0:1], None, ALU.mult)
                else:
                    ins = nc.vector.scalar_tensor_tensor(out=half, in0=ring_m[c % 2], scalar=csilu[:, kt, 0:1], in1=half,
                                                         op0=ALU.mult, op1=ALU.add)
                ins.then_inc(S["mod_used"], 1)
                dve.wait_ge(S["mod_used"], c + 1)
            ps = result(dve, "mod2")
            link(nc.vector.tensor_tensor(modc[:, 16:48, 0], ps[:, 0:32], colspan("b_mod")[:, 16:48], ALU.add))
            dve.sem_inc(free("mod2"), 1)
            link(nc.vector.tensor_scalar(scale2[:], modc[:, 32:40, 0], 1.0, None, ALU.add))
            link(nc.vector.tensor_tensor(scale2[:], scale2[:], colspan("g_norm2"), ALU.mult))
            link(nc.vector.memset(state, 0.0))
            link(nc.vector.memset(restart, 1.0))
            link(nc.vector.memset(restart[:, 0::GC], 0.0))
            dve.sem_inc(S["state_zero"], 1)
            for d in range(2):
                for h in range(HEADS):
                    for s, a, b in (("x", 0, T), ("c", T, TA)):
                        name = f"la{s}{d}{h}"
                        ps = result(dve, name)
                        link(nc.vector.tensor_scalar(la[d][:, h, a:b], ps[:, 0:b - a], col("b_gate2", 4 * d + h), None,
                                                     ALU.add))
                        dve.sem_inc(free(name), 1)
                dve.sem_inc(S["z_ready"], 1)
            link(nc.vector.memset(att_flat, 0.0))
            for d in range(2):
                zf = la[d].rearrange("p a b -> p (a b)")
                dve.wait_ge(S["softplus"], d + 1)
                link(nc.vector.scalar_tensor_tensor(out=zf, in0=zf, scalar=0.0, in1=eb, op0=ALU.min, op1=ALU.subtract))
                for h in range(HEADS):
                    row = la[d][:, h, :] if d == 0 else la[d][:, h, ::-1]
                    link(nc.vector.tensor_tensor_scan(row, restart, row, 0.0, ALU.mult, ALU.add))
                chunks = la[d].rearrange("p h (n t) -> p h n t", t=GC)
                end = chunks[:, :, :, GC - 1] if d == 0 else chunks[:, :, :, 0]
                nc.vector.tensor_copy(blast[:, d, :].rearrange("p (h n) -> p h n", h=HEADS), end) \
                    .then_inc(S["b_ready"], 1)
                ebx = eb[:, 0:HEADS * T].rearrange("p (a b) -> p a b", a=HEADS)
                dve.wait_ge(S["eb_full"], 2 * d + 1)
                if d == 0:
                    dve.wait_ge(free("q3"), JA["q3"] // 8 + 1)
                    dve.wait_ge(free("q2"), JA["q2"] // 8 + 1)
                    dve.wait_ge(free("q1"), JA["q1"] // 8 + 1)
                    dve.wait_ge(free("q0"), JA["q0"] // 8 + 1)
                    for h in range(HEADS):
                        for s in "xc":
                            dve.wait_ge(free(f"k{s}{h}"), JA[f"k{s}{h}"] // 8 + 1)
                nc.vector.tensor_tensor(qin[d], qq, ebx, ALU.mult).then_inc(S["eb_used"], 1)
                dve.wait_ge(S["eb_full"], 2 * d + 2)

                def keys_in():
                    nc.vector.tensor_tensor(kin[d], kk[:, :, 0:T], ebx, ALU.mult).then_inc(S["eb_used"], 1)
                    dve.wait_ge(S["eb_used"], 2 * d + 2)

                if d == 0:
                    keys_in()
                end = blast[:, d, :].rearrange("p (c o) -> p c o", o=1).to_broadcast([P, 48, GC])
                ch = zf.rearrange("p (c t) -> p c t", t=GC)
                nc.vector.tensor_tensor(ch, end, ch, ALU.subtract).then_inc(S["kexp_in"], 1)
                dve.wait_ge(S["kexp_out"], d + 1)
                nc.vector.tensor_tensor(zf, kk.rearrange("p a b -> p (a b)"), zf, ALU.mult).then_inc(kst_made, 1)
                dve.wait_ge(kst_made, d + 1)
                if d == 1:
                    keys_in()
                dve.sem_inc(S["gla_in"], 1)
            step = [0, 0]
            n_state = [0, 0]
            dve.wait_ge(s_const, 16 * 9)
            dve.wait_ge(S["decay_ready"], 2)
            for d, m, is_x, cs, last in gla_steps():
                if is_x:
                    name = f"att{d}{m}"
                    ps = result(dve, name)
                    nc.vector.copy_predicated(att[:, d, :].rearrange("p (h t) -> p h t", h=HEADS),
                                              gmask[:, d, :].unsqueeze(1).to_broadcast([P, HEADS, P]),
                                              ps.rearrange("p (h t) -> p h t", h=HEADS)).then_inc(S["att_ready"], 1)
                    dve.wait_ge(S["att_ready"], 2 * (m if d == 0 else NTX - 1 - m) + d + 1)
                    dve.sem_inc(free(name), 1)
                for n, c in enumerate(cs):
                    if is_x:
                        at = m * P + c * GC
                        if step[d] >= 4:
                            name = f"o{d}{m}{c}"
                            ps = result(dve, name)
                            dve.wait_ge(S["o_first"], 8)
                            link(nc.vector.tensor_tensor(oo[:, :, at:at + GC], oo[:, :, at:at + GC],
                                                         ps.rearrange("p (f t) -> p f t", t=GC), ALU.add))
                            dve.sem_inc(free(name), 1)
                            dve.sem_inc(S["o_done"], 1)
                        step[d] += 1
                    if last and n == 1:
                        continue
                    chunk = (0 if is_x else 8) + 2 * m + c
                    for i in range(2):
                        name = f"st{d}{is_x}{m}{c}{i}"
                        ps = result(dve, name)
                        for h in (2 * i, 2 * i + 1):
                            nc.vector.scalar_tensor_tensor(
                                out=state[:, d, h, :], in0=state[:, d, h, :],
                                scalar=decay[:, d, h * 12 + chunk:h * 12 + chunk + 1],
                                in1=ps[:, (h % 2) * HV:(h % 2 + 1) * HV], op0=ALU.mult, op1=ALU.add) \
                                .then_inc(state_sem[d], 1)
                            n_state[d] += 1
                            dve.wait_ge(state_sem[d], n_state[d])
                        dve.sem_inc(free(name), 1)
            for h in range(HEADS):
                ps = result(dve, f"on{h}")
                nc.vector.tensor_scalar(rso[:, h, :], ps[:], 1.0 / HV, EPS, ALU.mult, ALU.add).then_inc(S["variance"], 1)
                dve.wait_ge(S["variance"], 2 + h + 1)
                dve.sem_inc(free(f"on{h}"), 1)
            dve.wait_ge(S["root"], 2)
            link(nc.vector.reciprocal(rso, rso))
            for j in range(KT):
                link(nc.vector.scalar_tensor_tensor(out=oo[:, j, :], in0=oo[:, j, :], scalar=col("gla_g", j),
                                                    in1=rso[:, j // 2, :], op0=ALU.mult, op1=ALU.mult))
            for j in range(KT):
                dve.wait_ge(S["silu_r"], j + 1)
                nc.vector.tensor_tensor(oo[:, j, :], oo[:, j, :], rtmp[:, j % 2, :], ALU.mult) \
                    .then_inc(S["ob_ready"], 1)
            for t in range(NTX):
                dve.wait_ge(S["gelu_done"], NTX + t + 1)
                link(nc.vector.bn_stats(stats[:, 0, :], zv[:, t, 0:512]))
                link(nc.vector.bn_stats(stats[:, 1, :], zv[:, t, 512:D]))
                link(nc.vector.bn_aggr(meanvar[:, t, :], stats[:]))
                nc.vector.tensor_scalar(varz[:, t:t + 1], meanvar[:, t, 1:2], EPS, None, ALU.add) \
                    .then_inc(S["variance"], 1)
            dve.wait_ge(S["root"], 3)
            link(nc.vector.reciprocal(varz[:], varz[:]))
            dve.wait_ge(s_late, 32)
            for t in range(NTX):
                link(nc.vector.tensor_scalar(zv[:, t, :], zv[:, t, :], meanvar[:, t, 0:1], varz[:, t:t + 1],
                                             ALU.subtract, ALU.mult))
                link(nc.vector.tensor_tensor(zv[:, t, :], zv[:, t, :], lng, ALU.mult))
                nc.vector.tensor_tensor(zv[:, t, :], zv[:, t, :], lnb, ALU.add).then_inc(S["zv_ready"], 1)
            for j in range(KT):
                ps = result(dve, f"wb{j}")
                dve.wait_ge(S["sgb_ready"], j + 1)
                link(nc.vector.tensor_tensor(yy[:, j, :], ps[:], sgb[:, j, :], ALU.mult))
                dve.sem_inc(free(f"wb{j}"), 1)
            dve.wait_ge(S["gelu_done"], 2 * NTX + KT)
            for j in range(KT):
                ps = result(dve, f"mix{j}")
                link(nc.vector.tensor_tensor(mtmp[:, 0, :].rearrange("p (t s) -> p t s", t=NTX),
                                             ps.rearrange("p (t s) -> p t s", t=NTX),
                                             bsp[:, j, :].unsqueeze(1).to_broadcast([P, NTX, P]), ALU.add))
                dve.sem_inc(free(f"mix{j}"), 1)
                nc.vector.tensor_tensor(zu[:, j, :], zu[:, j, :], mtmp[:, 0, :], ALU.mult).then_inc(S["zu_ready"], 1)
                dve.wait_ge(S["zu_ready"], j + 1)
            for j in range(KT):
                ps = result(dve, f"wa{j}")
                dve.wait_ge(S["sga_ready"], j + 1)
                link(nc.vector.tensor_tensor(sga[:, j, :], ps[:], sga[:, j, :], ALU.mult))
                dve.sem_inc(free(f"wa{j}"), 1)
                nc.vector.tensor_tensor(yy[:, j, :], yy[:, j, :], sga[:, j, :], ALU.add).then_inc(S["y_ready"], 1)
            for j in range(KT):
                ps = result(dve, f"wout{j}")
                nc.vector.scalar_tensor_tensor(out=x[:, j, :], in0=ps[:], scalar=modc[:, 16 + j, 0:1], in1=x[:, j, :],
                                               op0=ALU.mult, op1=ALU.add).then_inc(S["x1_ready"], 1)
                dve.wait_ge(S["x1_ready"], j + 1)
                dve.sem_inc(free(f"wout{j}"), 1)
            dve.sem_inc(weights_used, 1)
            ps = result(dve, "ss2")
            nc.vector.tensor_scalar(rs2, ps[:], 1.0 / D, EPS, ALU.mult, ALU.add).then_inc(S["variance"], 1)
            dve.wait_ge(S["root"], 4)
            dve.sem_inc(free("ss2"), 1)
            link(nc.vector.reciprocal(rs2, rs2))
            nc.vector.tensor_tensor(h2, x, rs2.unsqueeze(1).to_broadcast([P, KT, T]), ALU.mult) \
                .then_inc(S["normed2"], 1)

            ps = result(dve, "route")
            link(nc.vector.tensor_copy(prob[:], ps[:, 0:NTX * NE].rearrange("p (t e) -> p t e", t=NTX)))
            dve.sem_inc(free("route"), 1)
            link(nc.vector.tensor_reduce(rsum[:], prob[:], AX.X, ALU.max))
            nc.vector.tensor_tensor(prob[:], prob[:], rsum[:].unsqueeze(2).to_broadcast([P, NTX, NE]), ALU.subtract) \
                .then_inc(S["logit_max"], 1)
            dve.wait_ge(S["logit_exp"], 1)
            link(nc.vector.tensor_reduce(rsum[:], prob[:], AX.X, ALU.add))
            link(nc.vector.reciprocal(rsum[:], rsum[:]))
            link(nc.vector.tensor_tensor(prob[:], prob[:], rsum[:].unsqueeze(2).to_broadcast([P, NTX, NE]), ALU.mult))
            TG = NTX * NG
            pg = prob[:].rearrange("p t (g e) -> p (t g) e", e=EG)

            def first_max(v, best, hit, n):
                link(nc.vector.tensor_reduce(best, v, AX.X, ALU.max))
                link(nc.vector.tensor_tensor(hit, v, best.unsqueeze(2).to_broadcast([P, n, 4]), ALU.is_equal))
                b = before[:, 0:n]
                link(nc.vector.tensor_copy(b, hit[:, :, 0]))
                for i in range(1, 4):
                    link(nc.vector.tensor_tensor(hit[:, :, i], hit[:, :, i], b, ALU.is_gt))
                    if i < 3:
                        link(nc.vector.tensor_tensor(b, hit[:, :, i], b, ALU.max))

            first_max(pg, best1[:], hit1[:], TG)
            link(nc.vector.tensor_tensor(rest[:], pg, hit1[:], ALU.mult))
            link(nc.vector.tensor_tensor(rest[:], pg, rest[:], ALU.subtract))
            link(nc.vector.tensor_tensor(rest[:], rest[:], hit1[:], ALU.subtract))
            first_max(rest[:], best2[:], hit2[:], TG)
            link(nc.vector.tensor_tensor(gscore[:], best1[:], best2[:], ALU.add))
            gs = gscore[:].rearrange("p (t g) -> p t g", g=NG)
            first_max(gs, rsum[:], ghit[:], NTX)
            gh = ghit[:].rearrange("p t g -> p (t g)").unsqueeze(2).to_broadcast([P, TG, EG])
            link(nc.vector.tensor_tensor(hit1[:], hit1[:], gh, ALU.mult))
            link(nc.vector.tensor_tensor(hit2[:], hit2[:], gh, ALU.mult))
            link(nc.vector.tensor_tensor(hot[:].rearrange("p t (g e) -> p (t g) e", e=EG), hit1[:], hit2[:], ALU.add))
            dve.sem_inc(S["onehot"], 1)
            h16 = [h[:].rearrange("p (t g) e -> p t (g e)", g=NG) for h in (hit1, hit2)]
            for k in range(2):
                link(nc.vector.tensor_tensor(etmp[:], prob[:], h16[k], ALU.mult))
                link(nc.vector.tensor_reduce(tokw[:, k, :], etmp[:], AX.X, ALU.add))
            link(nc.vector.tensor_tensor(rsum[:], tokw[:, 0, :], tokw[:, 1, :], ALU.add))
            link(nc.vector.reciprocal(rsum[:], rsum[:]))
            for k in range(2):
                link(nc.vector.tensor_tensor(tokw[:, k, :], tokw[:, k, :], rsum[:], ALU.mult))
            ps = result(dve, "rank")
            link(nc.vector.tensor_copy(rank[:], ps[:, 0:(NTX + 1) * NE].rearrange("p (t e) -> p t e", e=NE)))
            dve.sem_inc(free("rank"), 1)
            count = rank[:, NTX, :]
            link(nc.vector.tensor_scalar(nblk[:], count, 0.5, None, ALU.is_gt))
            for i in range(1, T // BLK):
                link(nc.vector.scalar_tensor_tensor(out=nblk[:], in0=count, scalar=i * BLK + 0.5, in1=nblk[:],
                                                    op0=ALU.is_gt, op1=ALU.add))
            link(nc.vector.tensor_tensor_scan(ends[:], ones[:, 0:NE], nblk[:], 0.0, ALU.mult, ALU.add))
            link(nc.vector.tensor_tensor(nblk[:], ends[:], nblk[:], ALU.subtract))
            link(nc.vector.tensor_scalar(nblk[:], nblk[:], float(BLK), None, ALU.mult))
            link(nc.vector.tensor_tensor(rank[:, 0:NTX, :], rank[:, 0:NTX, :],
                                         nblk[:].unsqueeze(1).to_broadcast([P, NTX, NE]), ALU.add))
            for k in range(2):
                link(nc.vector.tensor_tensor(etmp[:], rank[:, 0:NTX, :], h16[k], ALU.mult))
                link(nc.vector.tensor_reduce(slotf[:, k, :], etmp[:], AX.X, ALU.add))
            nc.vector.tensor_copy(slot[:], slotf[:].rearrange("p k t -> p (k t)")).then_inc(S["slots_ready"], 1)
            for b in range(NBLK):
                nc.vector.tensor_scalar(ends_le[0:1, b, :], ends[0:1, :], float(b) + 0.5, None, ALU.is_lt) \
                    .then_inc(le_made, 1)
            dve.wait_ge(le_made, NBLK)
            link(nc.vector.tensor_reduce(planf[0:1, 1:1 + NBLK], ends_le[0:1, :, :], AX.X, ALU.add))
            link(nc.vector.tensor_copy(planf[0:1, 0:1], ends[0:1, NE - 1:NE]))
            link(nc.vector.tensor_scalar(planf[0:1, 1:1 + NBLK], planf[0:1, 1:1 + NBLK], NE - 1.0, None, ALU.min))
            nc.vector.tensor_copy(plan[0:1, 0:1 + NBLK], planf[0:1, 0:1 + NBLK]).then_inc(S["plan_ready"], 1)

            n_blocks = load_plan(dve)
            with dve.Fori(0, n_blocks) as i:
                for n in range(3):
                    ps = result_e(dve, i, f"u{n}")
                    dve.wait_ge(S["sig_ready"], i * 3 + (n + 1))
                    nc.vector.tensor_tensor(hh[:, n * 512:(n + 1) * 512], ps[:], hs[:, n, :], ALU.mult) \
                        .then_inc(S["h_made"], 1)
                    dve.wait_ge(S["h_made"], i * 3 + (n + 1))
                    dve.sem_inc(bank_free_e[bank_e[f"u{n}"][0]], 1)
            dve.sem_inc(S["moe_dve_done"], 1)
            dve.wait_ge(S["moe_gathered"], 16 * 2 * NTX)
            for t in range(NTX):
                link(nc.vector.tensor_scalar(yg[:, 0, t, :], yg[:, 0, t, :], tokw[:, 0, t:t + 1], None, ALU.mult))
                nc.vector.scalar_tensor_tensor(out=yg[:, 0, t, :], in0=yg[:, 1, t, :], scalar=tokw[:, 1, t:t + 1],
                                               in1=yg[:, 0, t, :], op0=ALU.mult, op1=ALU.add) \
                    .then_inc(S["moe_summed"], 1)

            lre, lim, dt, size, ang = (sp5[:, i, :] for i in (0, 1, 3, 4, 5))
            sin4, n4 = sp5[:, 8:12, :], sp5[:, 12:16, :]
            dve.wait_ge(S["b_coef_exp"], 1)
            link(nc.vector.tensor_tensor(size, lre, dt, ALU.mult))
            link(nc.vector.tensor_tensor(ang, lim, dt, ALU.mult))
            for i in range(4):
                link(nc.vector.tensor_scalar(n4[:, i, :], ang, phase[:, i:i + 1], 0.5 / np.pi, ALU.add, ALU.mult))
            link(nc.vector.tensor_scalar(n4, n4, 12582912.0, -12582912.0, ALU.add, ALU.add))
            for i in range(4):
                link(nc.vector.scalar_tensor_tensor(out=sin4[:, i, :], in0=n4[:, i, :], scalar=-TURN[0], in1=ang,
                                                    op0=ALU.mult, op1=ALU.add))
                link(nc.vector.scalar_tensor_tensor(out=sin4[:, i, :], in0=n4[:, i, :], scalar=-TURN[1],
                                                    in1=sin4[:, i, :], op0=ALU.mult, op1=ALU.add))
                link(nc.vector.scalar_tensor_tensor(out=sin4[:, i, :], in0=n4[:, i, :], scalar=-TURN[2],
                                                    in1=sin4[:, i, :], op0=ALU.mult, op1=ALU.add))
                link(nc.vector.tensor_scalar(sin4[:, i, :], sin4[:, i, :], phase[:, i:i + 1], None, ALU.add))
            link(nc.vector.tensor_scalar(sin4, sin4, 3.14159250, -3.14159250, ALU.min, ALU.max))
            dve.sem_inc(S["b_coef_ready"], 1)
            dve.wait_ge(S["b_coef_exp"], 2)
            link(nc.vector.tensor_tensor(sin4, sin4, size.unsqueeze(1).to_broadcast([P, 4, S5G]), ALU.mult))
            are, aim = sin4[:, 2, :], sin4[:, 3, :]
            link(nc.vector.memset(pw[:, 0, :, :], 0.0))
            link(nc.vector.memset(pw[0:64, 0, 0, :], 1.0))
            link(nc.vector.memset(pw[64:128, 0, 1, :], 1.0))
            link(nc.vector.tensor_copy(pw[:, 1, :, :], sin4[:, 0:2, :]))
            t2 = sp5[:, 12:14, :]
            ai2 = sp5[:, 14:16, :]
            link(nc.vector.tensor_copy(ai2[:, 0, :], aim))
            link(nc.vector.tensor_scalar(ai2[:, 1, :], aim, -1.0, None, ALU.mult))
            ar2 = are.unsqueeze(1).to_broadcast([P, 2, S5G])
            for k in range(1, S5T):
                link(nc.vector.tensor_tensor(t2, pw[:, k, ::-1, :], ai2, ALU.mult))
                link(nc.vector.tensor_tensor(pw[:, k + 1, :, :], pw[:, k, :, :], ar2, ALU.mult))
                link(nc.vector.tensor_tensor(pw[:, k + 1, :, :], pw[:, k + 1, :, :], t2, ALU.add))
            r8, i8 = ab8[:, 0, 0, :], ab8[:, 1, 0, :]
            link(nc.vector.tensor_copy(r8, are))
            link(nc.vector.tensor_copy(i8, aim))
            ta, tb = sp5[:, 6, :], sp5[:, 7, :]
            for _ in range(3):
                link(nc.vector.tensor_tensor(ta, r8, r8, ALU.mult))
                link(nc.vector.tensor_tensor(tb, i8, i8, ALU.mult))
                link(nc.vector.scalar_tensor_tensor(out=i8, in0=i8, scalar=2.0, in1=r8, op0=ALU.mult, op1=ALU.mult))
                link(nc.vector.tensor_tensor(r8, ta, tb, ALU.subtract))
            link(nc.vector.tensor_copy(ab8[:, 0, 1, :], r8))
            link(nc.vector.tensor_scalar(ab8[:, 1, 1, :], i8, -1.0, None, ALU.mult))
            am, wre, wim, den = (sp5[:, i, :] for i in (16, 17, 18, 19))
            link(nc.vector.tensor_scalar(am, are, -1.0, None, ALU.add))
            link(nc.vector.tensor_tensor(ta, lre, lre, ALU.mult))
            link(nc.vector.tensor_tensor(tb, lim, lim, ALU.mult))
            link(nc.vector.tensor_tensor(den, ta, tb, ALU.add))
            link(nc.vector.reciprocal(den, den))
            link(nc.vector.tensor_tensor(ta, am, lre, ALU.mult))
            link(nc.vector.tensor_tensor(tb, aim, lim, ALU.mult))
            link(nc.vector.tensor_tensor(wre, ta, tb, ALU.add))
            link(nc.vector.tensor_tensor(wre, wre, den, ALU.mult))
            link(nc.vector.tensor_tensor(ta, aim, lre, ALU.mult))
            link(nc.vector.tensor_tensor(tb, am, lim, ALU.mult))
            link(nc.vector.tensor_tensor(wim, ta, tb, ALU.subtract))
            link(nc.vector.tensor_tensor(wim, wim, den, ALU.mult))
            bt = tmp[:, 0:S5G * S5H].rearrange("p (g h) -> p g h", h=S5H)
            wr = wre.unsqueeze(2).to_broadcast([P, S5G, S5H])
            wm = wim.unsqueeze(2).to_broadcast([P, S5G, S5H])
            link(nc.vector.tensor_tensor(bb[:, 0], bri[:, 0], wr, ALU.mult))
            link(nc.vector.tensor_tensor(bt, bri[:, 1], wm, ALU.mult))
            link(nc.vector.tensor_tensor(bb[:, 0], bb[:, 0], bt, ALU.subtract))
            link(nc.vector.tensor_tensor(bb[:, 1], bri[:, 1], wr, ALU.mult))
            link(nc.vector.tensor_tensor(bt, bri[:, 0], wm, ALU.mult))
            link(nc.vector.tensor_tensor(bb[:, 1], bb[:, 1], bt, ALU.add))
            link(nc.vector.tensor_scalar(cc[64:128], cc[64:128], -1.0, None, ALU.mult))

            def power(k0, k1, form, t, step=1):
                ks = pw[:, k0:k1, form, 8 * t:8 * t + 8] if step == 1 else pw[:, k1 - 1::-1, form, 8 * t:8 * t + 8]
                return ks.rearrange("p k g -> p g k").unsqueeze(3).to_broadcast([P, 8, k1 - k0, S5H])

            n_x2 = 0
            for j in range(KT):
                ps = result(dve, f"y{j}")
                n_x2 += 1
                copied(dve, nc.vector.scalar_tensor_tensor(out=x[:, j, :], in0=ps[:], scalar=modc[:, 40 + j, 0:1],
                                                           in1=x[:, j, :], op0=ALU.mult, op1=ALU.add),
                       S["b_x2_ready"], n_x2, f"y{j}")

            for t in range(KT):
                g = slice(8 * t, 8 * t + 8)
                o = cp[:, g, :, :]
                tv = tmp.rearrange("p (g k h) -> p g k h", g=8, h=S5H)
                c0, c1 = (cc[:, i, g, :].unsqueeze(2).to_broadcast([P, 8, S5T + 1, S5H]) for i in range(2))
                link(nc.vector.tensor_tensor(o, c0, power(0, S5T + 1, 0, t), ALU.mult))
                link(nc.vector.tensor_tensor(tv, c1, power(0, S5T + 1, 1, t), ALU.mult))
                nc.vector.tensor_tensor(o, o, tv, ALU.add).then_inc(S["b_cp_ready"], 1)
                dve.wait_ge(S["b_cp_ready"], t + 1)

            def rms(n):
                ps = result(dve, f"sn{n}")
                copied(dve, nc.vector.tensor_scalar(RS[:], ps[:], 1.0 / D, EPS, ALU.mult, ALU.add),
                       S["variance"], NORMS_A + n + 1, f"sn{n}")
                dve.wait_ge(S["root"], 4 + n + 1)
                link(nc.vector.reciprocal(RS[:], RS[:]))

            def normed(dst, kt, gain, done, count):
                nc.vector.scalar_tensor_tensor(out=dst[:, kt, :], in0=x[:, kt, :], scalar=gain, in1=RS[:],
                                               op0=ALU.mult, op1=ALU.mult).then_inc(done, 1)
                dve.wait_ge(done, count)

            rms(0)
            for kt in range(KT):
                normed(x, kt, col("g_final", kt), S["b_x2_ready"], KT + kt + 1)
            rms(1)
            for kt in range(KT):
                normed(hb, kt, col("norm_mix", kt), S["b_h_full"], kt + 1)
                nc.vector.tensor_copy(u_s[:, kt, :, :], hb[:, kt, :].rearrange("p (c s) -> p s c", s=S5T)) \
                    .then_inc(S["b_s5_u_made"], 1)
            link(nc.vector.memset(ksb[0:16], 0.0))
            dve.wait_ge(S["b_s5_u_out"], 16)
            for t in range(KT):
                g = slice(8 * t, 8 * t + 8)
                tv = tmpq.rearrange("p (g k h) -> p g k h", g=8, h=S5H)
                b0, b1 = (bb[:, i, g, :].unsqueeze(2).to_broadcast([P, 8, S5T, S5H]) for i in range(2))
                if t:
                    dve.wait_ge(bank_done, JB[f"kk{t - 1}1"] + 1)
                for f, op, pa, pb in ((0, ALU.add, 0, 1), (1, ALU.subtract, 1, 0)):
                    link(nc.vector.tensor_tensor(qb[:, f], b0, power(0, S5T, pa, t, -1), ALU.mult))
                    link(nc.vector.tensor_tensor(tv, b1, power(0, S5T, pb, t, -1), ALU.mult))
                    nc.vector.tensor_tensor(qb[:, f], qb[:, f], tv, op).then_inc(S["b_qb_ready"], 1)
                    dve.wait_ge(S["b_qb_ready"], 2 * t + f + 1)
            dve.wait_ge(S["b_s_copied"], 2 * KT)
            link(nc.vector.memset(xs[:, 0, :, :], 0.0))
            ts = tmpq[:, 0:4 * S5G].rearrange("p (w f g) -> p w f g", w=2, f=2)
            for c in range(1, S5C - 1):
                nc.vector.tensor_tensor(ts[:, 0], xs[:, c, :, :], ab8[:, 0], ALU.mult).then_inc(scan_part, 1)
                nc.vector.tensor_tensor(ts[:, 1], xs[:, c, ::-1, :], ab8[:, 1], ALU.mult).then_inc(scan_part, 1)
                dve.wait_ge(scan_part, 2 * c)
                link(nc.vector.tensor_tensor(ts[:, 0], ts[:, 0], ts[:, 1], ALU.add))
                link(nc.vector.tensor_tensor(xs[:, c + 1], xs[:, c + 1], ts[:, 0], ALU.add))
            dve.sem_inc(S["b_scanned"], 1)
            dve.wait_ge(S["b_yn_in"], 16)
            for kt in range(KT):
                hv = hb[:, kt, :].rearrange("p (c s) -> p c s", s=S5T)
                nc.vector.scalar_tensor_tensor(out=hv, in0=hv, scalar=col("s5_d", kt),
                                               in1=yn[:, kt].rearrange("p s c -> p c s"), op0=ALU.mult, op1=ALU.add) \
                    .then_inc(S["b_y5_ready"], 1)
            split_to, n_high = [0], [0]
            weights_low_part(dve, 1, split_to)

            def low_part(dst, high, src):
                for kt in range(KT):
                    n_high[0] += 1
                    dve.wait_ge(high_ready, n_high[0])
                    nc.vector.tensor_tensor(dst[:, kt, :], src[:, kt, :], high[:, kt, :].bitcast(F32), ALU.subtract) \
                        .then_inc(split_ready, 1)

            low_part(low_b, high_g, hb)
            n_sig, n_x, n_hid = 0, 0, 0
            for j in range(KT):
                for i in range(2):
                    weights_low_part(dve, ahead("glu", "glu", 2 * j + i), split_to)
                ps = result(dve, f"glu{2 * j}")
                n_sig += 1
                dve.wait_ge(S["b_sig_b"], n_sig)
                link(nc.vector.tensor_tensor(st[:, j % 2, :], ps[:], st[:, j % 2, :], ALU.mult))
                dve.sem_inc(free(f"glu{2 * j}"), 1)
                link(nc.vector.tensor_tensor(x[:, j, :], x[:, j, :], st[:, j % 2, :], ALU.add))
                dve.sem_inc(S["b_st_used"], 1)
                dve.sem_inc(S["b_x_ready"], 1)
            n_x = KT

            def normed_all(n, gain, first):
                rms(n)
                for kt in range(KT):
                    normed(raw, kt, col(gain, first + kt), S["b_h_full"], h_count[n] - KT + kt + 1)

            def dense_dve(n, n_sig, n_x):
                normed_all(2 + 2 * n, "norm_ffn", KT * n)
                low_part(low_b, high_b, raw)
                for j in range(FFT):
                    name = f"gu{n}{2 * j + 1}"
                    for i in range(2 if j < FFT - 1 else 1):
                        weights_low_part(dve, ahead(f"down{n}", f"gu{n}", 2 * j + i), split_to)
                    ps = result(dve, name)
                    n_sig += 1
                    dve.wait_ge(S["b_sig_b"], n_sig)
                    copied(dve, nc.vector.tensor_tensor(product[:, j % 3, :], ps[:], st[:, j % 2, :], ALU.mult),
                           product_ready, FFT * n + j + 1, name)
                    dve.sem_inc(S["b_st_used"], 1)
                    n_high[0] += 1
                    dve.wait_ge(high_ready, n_high[0])
                    nc.vector.tensor_tensor(hid(j)[1], product[:, j % 3, :], hid(j)[0].bitcast(F32),
                                            ALU.subtract).then_inc(split_ready, 1)
                for j in range(KT):
                    weights_low_part(dve, ahead(f"down{n}", f"down{n}", j, FFT), split_to)
                    name = f"down{n}{j}"
                    ps = result(dve, name)
                    n_x += 1
                    copied(dve, nc.vector.tensor_tensor(x[:, j, :], x[:, j, :], ps[:], ALU.add), S["b_x_ready"], n_x,
                           name)
                return n_sig, n_x

            n_sig, n_x = dense_dve(0, n_sig, n_x)
            normed_all(3, "norm_mix", KT)
            low_part(low_p, high_b, raw)
            dve.wait_ge(S["b_rope_in"], 48)
            for s in range(NR + 2):
                if s == 2 * KT:
                    for n in range(2):
                        weights_low_part(dve, ahead("dki", "dv", n, KT, True), split_to)
                if s < NR:
                    weights_low_part(dve, ahead("dki", ROPED[s][0], ROPED[s][1]), split_to)
                if 1 <= s <= NR and ROPED[s - 1][2]:
                    k = norm_index[s - 1]
                    ps = result(dve, f"pn{s - 1}")
                    copied(dve, nc.vector.tensor_scalar(rst[:, k % 2, :], ps[:], 1.0 / HD, EPS, ALU.mult, ALU.add),
                           S["b_rvar"], k + 1, f"pn{s - 1}")
                    dve.wait_ge(S["b_rroot"], k + 1)
                    link(nc.vector.reciprocal(rst[:, k % 2, :], rst[:, k % 2, :]))
                    gain = ROPED[s - 1][3]
                    dve.wait_ge(S["b_raw_ready"], s)
                    nc.vector.scalar_tensor_tensor(out=roped_tile(s - 1), in0=roped_tile(s - 1),
                                                   scalar=1.0 if gain is None else col("qk_gain", gain),
                                                   in1=rst[:, k % 2, :], op0=ALU.mult, op1=ALU.mult) \
                        .then_inc(S["b_normed_q"], 1)
                    dve.wait_ge(S["b_normed_q"], k + 1)
                if s >= 2:
                    name = f"rot{s - 2}"
                    ps = result(dve, name)
                    v = roped_tile(s - 2)
                    link(nc.vector.tensor_tensor(rt[:, 0, :], ps[:], cossin[:, 1, :], ALU.mult))
                    dve.sem_inc(free(name), 1)
                    link(nc.vector.tensor_tensor(v, v, cossin[:, 0, :], ALU.mult))
                    nc.vector.tensor_tensor(v, v, rt[:, 0, :], ALU.add).then_inc(S["b_rotated"], 1)
                    dve.wait_ge(S["b_rotated"], s - 1)
            ps = result(dve, "wi")
            link(nc.vector.tensor_scalar(wi, ps[:, 0:NTX * IH].rearrange("p (t h) -> p t h", h=IH),
                                         float(IH) ** -0.5, float(HD) ** -0.5, ALU.mult, ALU.mult))
            dve.sem_inc(free("wi"), 1)
            link(nc.vector.memset(bias[:, 0:P], 0.0))
            dve.sem_inc(S["b_bias0"], 1)
            dve.wait_ge(S["b_masked"], 1)
            n_relu = 0

            def scale_rows(s):
                b = s % 4
                dve.wait_ge(S["b_exped"], s + 1)
                link(nc.vector.reciprocal(rsm[:, b:b + 1], sm[:, b:b + 1]))
                nc.vector.tensor_scalar(diag[:, b, :], ident[:], rsm[:, b:b + 1], None, ALU.mult) \
                    .then_inc(S["b_diag_ready"], 1)

            for s in range(NPAIR + 1):
                opens = s < NPAIR and PAIRS[s][1] == 0 and PAIRS[s][0] > 0
                if s < NPAIR:
                    t, h = PAIRS[s]
                    w = (t + 1) * P
                    if opens:
                        scale_rows(s - 1)
                        for i in range(IH):
                            n_relu += 1
                            dve.wait_ge(S["b_relu_ready"], n_relu)
                            if i == 0:
                                ins = nc.vector.tensor_scalar(score[:, 0:w], rl[:, i % 2, 0:w], wi[:, t, i:i + 1], None,
                                                              ALU.mult)
                            else:
                                ins = nc.vector.scalar_tensor_tensor(out=score[:, 0:w], in0=rl[:, i % 2, 0:w],
                                                                     scalar=wi[:, t, i:i + 1], in1=score[:, 0:w],
                                                                     op0=ALU.mult, op1=ALU.add)
                            ins.then_inc(relu_used, 1)
                            dve.wait_ge(relu_used, n_relu)
                        dve.sem_inc(S["b_score_ready"], 1)
                        dve.wait_ge(S["b_masked"], t + 1)
                        for _ in range(TOPK // 8):
                            link(nc.vector.max(m8[:], score[:, 0:w]))
                            link(nc.vector.match_replace(score[:, 0:w], m8[:], score[:, 0:w], TAKEN))
                        link(nc.vector.tensor_scalar(bias[:, 0:w], score[:, 0:w], TAKEN / 2, MASKED, ALU.is_gt,
                                                     ALU.mult))
                    b = s % 4
                    name = f"lg{s}"
                    ps = result(dve, name)
                    if s >= 4:
                        dve.wait_ge(bank_done, JB[f"pt{s - 4}"] + 1)
                    link(nc.vector.tensor_tensor_reduce(pp[:, b, 0:w], ps[:, 0:w], bias[:, 0:w], 1.0, -3.0e38,
                                                        ALU.add, ALU.max, mx[:, b:b + 1]))
                    dve.sem_inc(free(name), 1)
                    nc.vector.tensor_scalar(nmx[:, b:b + 1], mx[:, b:b + 1], -float(HD) ** -0.5, None, ALU.mult) \
                        .then_inc(S["b_logits"], 1)
                if s >= 1 and not opens:
                    scale_rows(s - 1)
            low_part(low_b, high_b, oT)
            for j in range(KT):
                weights_low_part(dve, ahead("wo", "wo", j), split_to)
                name = f"wo{j}"
                ps = result(dve, name)
                n_x += 1
                copied(dve, nc.vector.tensor_tensor(x[:, j, :], x[:, j, :], ps[:], ALU.add), S["b_x_ready"], n_x, name)
            dense_dve(1, n_sig, n_x)


def _tiles(w, b, width=P):
    return w[:, b * width:(b + 1) * width].reshape(-1, P, width).transpose(1, 0, 2)


def _stream(stream, parts):
    units = []
    for name, kind, b0, b1 in stream:
        for b in range(b0, b1):
            if kind == "col":
                units.append(_tiles(parts[name], b))
            else:
                t = _tiles(parts[name], b, 4 * P)
                units.append(t.reshape(P, -1, P))
    a = np.concatenate(units, axis=1)
    n = -(-a.shape[1] // CH)
    pad = np.zeros((P, n * CH - a.shape[1], P), np.float32)
    a = np.concatenate([a, pad], axis=1) if pad.shape[1] else a
    return np.ascontiguousarray(a.reshape(P, n, CH * P).transpose(1, 0, 2))


def _columns(v):
    return np.asarray(v, np.float32).reshape(-1, P).T


def layouts(inputs):
    g = {k: np.asarray(v) for k, v in inputs.items()}
    io = {}
    io["xt"] = np.ascontiguousarray(g["x"][0].T.reshape(KT, P, T))
    io["ct"] = np.ascontiguousarray(g["ctx"][0].T.reshape(KT, P, TC))
    w = g["w_in"][0]
    cut = np.cumsum([0, D, D, 512, 512, D, D, RANK, RANK, D, D])
    zu, zv, q, k, v, r, lf, lb, ga, gb = (w[:, a:b] for a, b in zip(cut[:-1], cut[1:]))
    lr = np.zeros((D, P), np.float32)
    lr[:, 0:RANK] = lf
    lr[:, 32:32 + RANK] = lb
    io["wa_stream"] = _stream(STREAM_A, dict(mod=g["w_mod"][0], lr=lr, k=k, q=q, v=v, r=r, zv=zv, zu=zu, ga=ga, gb=gb,
                                             wb=g["w_branch_b"][0], wa=g["w_branch_a"][0], wout=g["w_out"][0]))
    io["mod2"] = np.ascontiguousarray(g["w_mod"][0][:, 2 * D:].reshape(KT, P, 2, 2 * D).transpose(0, 2, 1, 3)) \
        .reshape(2 * KT, P, 2 * D)
    packed = dict(b_mod=g["b_mod"], g_norm1=g["g_norm1"], g_norm2=g["g_norm2"], gla_g=g["gla_norm_g"],
                  b_branch=g["b_branch"], g_final=g["g_final"], b_gate2=g["b_gate2"], s5_d=g["s5_d_2"],
                  norm_mix=g["norm_mix_2"], norm_ffn=g["norm_ffn_2"])
    parts = [_columns(packed[n]) for n in packed] + [_columns(g["c"]), _columns(g["c_ctx"])]
    parts += [np.tile(g[n][0], 2)[:, None] for n in ("dsa_q_norm_2", "dsa_k_norm_2")]
    io["cols"] = np.ascontiguousarray(np.concatenate(parts, axis=1))
    assert io["cols"].shape[1] == NCOL
    io["ident"] = np.eye(P, dtype=np.float32)
    io["ones"] = np.ones((P, P), np.float32)
    i = np.arange(P)
    io["tri"] = (i[:, None] < i[None, :]).astype(np.float32)
    same = (i[:, None] // GC) == (i[None, :] // GC)
    io["gmask"] = np.ascontiguousarray(np.stack([same & (i[:, None] <= i[None, :]), same & (i[:, None] >= i[None, :])],
                                                axis=1).astype(np.uint32))
    wg = np.zeros((64, 2, 512), np.float32)
    wg[0:RANK, 0] = g["w_gate2"][0, 0]
    wg[32:32 + RANK, 1] = g["w_gate2"][0, 1]
    io["wgate"] = wg
    io["wrouter"] = np.ascontiguousarray(g["w_router"].reshape(KT, P, NE).transpose(1, 0, 2))
    io["b_router"] = g["b_router"].reshape(1, NE)
    io["sgu_w"] = np.ascontiguousarray(g["sgu_w"][0].transpose(2, 0, 1))
    io["sgu_ln_g"] = g["sgu_ln_g"][0]
    io["sgu_ln_b"] = g["sgu_ln_b"][0]
    io["sgu_b"] = g["sgu_b"][0].reshape(-1)
    layouts_more(g, io)
    return io


def kernel(**inputs):
    import concourse.bacc as bacc
    from concourse.bass_utils import run_bass_kernel_spmd as run

    arrays = {f"in_{n}": a for n, a in layouts(inputs).items()}
    nc = bacc.Bacc("TRN2", target_bir_lowering=False, num_devices=1)
    io = {n[3:]: nc.dram_tensor(n, a.shape, mybir.dt.from_np(a.dtype), kind="ExternalInput").ap()
          for n, a in arrays.items()}
    out = nc.dram_tensor("out_dram", (KT, P, T), F32, kind="ExternalOutput").ap()
    block_kernel(nc, io, out, dram_scratch(nc))
    r = run(nc, [arrays], core_ids=[0])
    return np.ascontiguousarray(r.results[0]["out_dram"].reshape(D, T).T).reshape(1, T, D)
```

```python
from contextlib import ExitStack

import numpy as np
import concourse.bass as bass
from concourse import mybir

F32 = mybir.dt.float32
F32R = mybir.dt.float32r
I32 = mybir.dt.int32
U32 = mybir.dt.uint32
ALU = mybir.AluOpType
ACT = mybir.ActivationFunctionType
AX = mybir.AxisListType

P = 128
D = 1024
KT = D // P
T = 512
TC = 256
TA = T + TC
NTX, NTC = T // P, TC // P
EPS = 1e-6
HEADS, HK, HV = 4, 128, 256
RANK = 16
GC = 64
NE, NG, EG = 16, 4, 4
FE = 1536
FET = FE // P
BLK = 128
NBLK = 2 * T // BLK + NE
FF = 2816
FFT = FF // P
S5G, S5H, S5P, S5T = 64, 16, 64, 8
S5C = T // S5T
AH, HD = 16, 64
IH = 8
TOPK = 128
CH = 16
MASKED, TAKEN = -1.0e30, -3.0e38
TURN = (6.28125, 0.0019350051879882812, 3.0199159795074593e-07)
KF = 1024

COLS = {}
_at = 0
for _name, _n in (("b_mod", 48), ("g_norm1", 8), ("g_norm2", 8), ("gla_g", 8), ("b_branch", 16),
                  ("g_final", 8), ("b_gate2", 8), ("s5_d", 8), ("norm_mix", 16), ("norm_ffn", 16),
                  ("c", 16), ("qk_gain", 2)):
    COLS[_name] = (_at, _at + _n)
    _at += _n
NCOL = _at

STREAM_A = [("mod", "row", 0, 4), ("lr", "col", 0, 1), ("k", "col", 0, 4), ("q", "col", 0, 4),
            ("v", "row", 0, 2), ("r", "col", 0, 8), ("zv", "row", 0, 2),
            ("zu", "col", 0, 8), ("gb", "col", 0, 8), ("ga", "col", 0, 8), ("wb", "col", 0, 8),
            ("wa", "col", 0, 8), ("wout", "col", 0, 8)]


def unit_table(stream, depth):
    at, table = 0, {}
    for name, kind, b0, b1 in stream:
        rows = depth.get(name, KT)
        for b in range(b0, b1):
            table[name, b] = at
            at += rows * (1 if kind == "col" else 4)
    return table, -(-at // CH)


DEPTH = {"down0": FFT, "down1": FFT}
UNITS_A, CHUNKS_A = unit_table(STREAM_A, DEPTH)
STREAM_B = [("glu", "col", 0, 16), ("gu0", "col", 0, 2 * FFT), ("down0", "col", 0, 8),
            ("dq", "col", 0, 8), ("dk", "col", 0, 8), ("dv", "row", 0, 2), ("dqi", "col", 0, 4),
            ("dki", "col", 0, 1), ("wo", "col", 0, 8), ("gu1", "col", 0, 2 * FFT), ("down1", "col", 0, 8)]
UNITS_B, CHUNKS_B = unit_table(STREAM_B, DEPTH)
RING_PAGES = 8
HALF = 8
CHUNKS_E = 18
RING_A, RING_E, RING_M = 4, 6, 3

JOBS_A = ["ssx", "ssc"] + [f"modrow{n}" for n in range(4)] + ["mod1", "lrx", "lrc"]
JOBS_A += [f"k{s}{h}" for h in range(HEADS) for s in "xc"] + ["mod2"]
JOBS_A += [f"la{s}{d}{h}" for d in range(2) for h in range(HEADS) for s in "xc"]
JOBS_A += [f"q{h}" for h in range(HEADS)]
JOBS_A += [f"v{n}{t}" for n in range(2) for t in range(NTX + NTC)]


def gla_steps():
    for i in range(NTC + NTX):
        for d in range(2):
            x = i >= NTC
            n, m = (NTX, i - NTC) if x else (NTC, i)
            yield d, (m if d == 0 else n - 1 - m), x, ((0, 1) if d == 0 else (1, 0)), i == NTC + NTX - 1


GLA = list(gla_steps())
for _i in range(-1, len(GLA)):
    if _i + 1 < len(GLA):
        _d, _m, _x, _, _ = GLA[_i + 1]
        JOBS_A += [f"kT{_d}{_x}{_m}"] + ([f"att{_d}{_m}"] if _x else [])
    if _i < 0:
        continue
    _d, _m, _x, _cs, _last = GLA[_i]
    for _n, _c in enumerate(_cs):
        JOBS_A += ([f"o{_d}{_m}{_c}"] if _x else [])
        JOBS_A += [] if _last and _n == 1 else [f"st{_d}{_x}{_m}{_c}{_i}" for _i in range(2)]
JOBS_A += [f"on{h}" for h in range(HEADS)] + [f"r{j}" for j in range(KT)]
JOBS_A += [f"zv{n}{t}" for n in range(2) for t in range(NTX)]
JOBS_A += [f"{w}{j}" for w in ("zu", "gb", "ga") for j in range(KT)]
JOBS_A += [f"{w}{j}" for w in ("mix", "wb") for j in range(KT)] + [f"wa{j}" for j in range(KT)] + [f"wout{j}" for j in range(KT)]
JOBS_A += ["ss2", "route"] + [f"tok{t}{n}" for t in range(NTX) for n in range(2)] + ["rank"]
JA = {name: n for n, name in enumerate(JOBS_A)}
assert len(JA) == len(JOBS_A)

JOBS_B = [f"y{j}" for j in range(KT)] + ["sn0", "sn1"]
for _t in range(KT):
    JOBS_B += [f"qt{_t}{i}" for i in range(2)] + [f"kk{_t}{i}" for i in range(2)] + [f"s{_t}{i}" for i in range(2)]
JOBS_B += [f"yu{t}" for t in range(KT)] + [f"ys{t}" for t in range(KT)]
JOBS_B += [f"glu{b}" for b in range(2 * KT)] + ["sn2"]
JOBS_B += [f"gu0{b}" for b in range(2 * FFT)] + [f"down0{j}" for j in range(KT)] + ["sn3"]
ROPED = [("dq", j, True, 0) for j in range(KT)] + [("dk", j, True, 1) for j in range(KT)]
ROPED += [("dqi", j, False, None) for j in range(4)] + [("dki", 0, True, None)]
NR = len(ROPED)
for _s in range(NR + 2):
    if _s < NR:
        JOBS_B += [f"pr{_s}"]
    if 1 <= _s <= NR and ROPED[_s - 1][2]:
        JOBS_B += [f"pn{_s - 1}"]
    if 2 <= _s:
        JOBS_B += [f"rot{_s - 2}"]
_k = JOBS_B.index(f"pr{2 * KT}")
JOBS_B[_k:_k] = [f"dv{n}{t}" for n in range(2) for t in range(NTX)]
JOBS_B += ["wi"]
PAIRS = [(t, h) for t in range(NTX) for h in range(AH)]
NPAIR = len(PAIRS)
TURN_LAG, VALUE_LAG = 3, 4
for _s in range(NPAIR + VALUE_LAG):
    if TURN_LAG <= _s < NPAIR + TURN_LAG:
        JOBS_B += [f"pt{_s - TURN_LAG}"]
    if VALUE_LAG <= _s and (_s - VALUE_LAG) % 2 == 0:
        JOBS_B += [f"av{_s - VALUE_LAG}"]
    if _s < NPAIR:
        JOBS_B += [f"lg{_s}"]
        if PAIRS[_s][1] == 1 and PAIRS[_s][0] < NTX - 1:
            JOBS_B += [f"ix{PAIRS[_s][0] + 1}{h}" for h in range(IH)]
JOBS_B += [f"wo{j}" for j in range(KT)] + ["sn4"]
JOBS_B += [f"gu1{b}" for b in range(2 * FFT)] + [f"down1{j}" for j in range(KT)]
JB = {name: n + len(JA) for n, name in enumerate(JOBS_B)}
JOBS = {**JA, **JB}
assert len(JOBS) == len(JOBS_A) + len(JOBS_B)
UNITS = {**UNITS_A, **{key: u + CHUNKS_A * CH for key, u in UNITS_B.items()}}


def dram_scratch(nc):
    def dram(name, *shape):
        return nc.dram_tensor(name, shape, F32, kind="Internal").ap()

    return dict(xbuf=dram("xbuf", (NBLK + 1) * BLK, D), ybuf=dram("ybuf", NBLK * BLK, D),
                ud=dram("ud", S5G, S5H, S5T, S5C), kd=dram("kd", S5G, S5H, 2 * S5T, S5H),
                yd=dram("yd", S5G, S5H, S5T, S5C))


def layouts_more(g, io):
    def wide(w):
        return w.reshape(NE, KT, P, 3, 512).transpose(0, 3, 2, 1, 4).reshape(NE, 3, P, 2, CH * P)

    up = np.stack([wide(g["w_exp_gate"][0]), wide(g["w_exp_up"][0])], axis=2)
    up = up.transpose(0, 1, 2, 4, 3, 5).reshape(NE, 12, P, CH * P)
    down = g["w_exp_down"][0].reshape(NE, 6, 2, P, D).transpose(0, 1, 3, 2, 4).reshape(NE, 6, P, CH * P)
    io["we_stream"] = np.concatenate([up, down], axis=1)

    def paired(a, b):
        return np.stack([a.reshape(a.shape[0], -1, P), b.reshape(b.shape[0], -1, P)], axis=2).reshape(a.shape[0], -1)

    dsa = g["dsa_w_in_2"][0]
    dq, dk, dv = (dsa[:, i * D:(i + 1) * D] for i in range(3))
    dqi, dki, dwi = dsa[:, 3 * D:3 * D + 512], dsa[:, 3 * D + 512:3 * D + 576], dsa[:, 3 * D + 576:]
    ffn, glu = g["ffn_w_gate_up_2"], g["s5_w_glu_2"][0]
    io["wb_stream"] = _stream(STREAM_B, dict(
        glu=paired(glu[:, :D], glu[:, D:]), gu0=paired(ffn[0, :, :FF], ffn[0, :, FF:]), down0=g["ffn_w_down_2"][0],
        dq=dq, dk=dk, dv=dv, dqi=dqi, dki=np.concatenate([dki, dki], axis=1), wo=g["dsa_w_o_2"][0],
        gu1=paired(ffn[1, :, :FF], ffn[1, :, FF:]), down1=g["ffn_w_down_2"][1]))
    io["wiw"] = np.ascontiguousarray(dwi.reshape(KT, P, IH).transpose(1, 0, 2))
    twice = lambda a: np.ascontiguousarray(np.concatenate([a, a], axis=0))
    io["s5_lam"] = twice(np.stack([g["s5_lambda_re_2"][0].T, g["s5_lambda_im_2"][0].T,
                                   np.broadcast_to(g["s5_log_dt_2"][0][None, :], (S5P, S5G))], axis=1))
    io["s5_b"] = twice(np.stack([g[n][0].transpose(1, 0, 2) for n in ("s5_b_re_2", "s5_b_im_2")], axis=1))
    io["s5_c"] = twice(np.stack([g[n][0].transpose(2, 0, 1) for n in ("s5_c_re_2", "s5_c_im_2")], axis=1))
    half = np.pi / 2
    phase = np.zeros((2, 4), np.float32)
    phase[0], phase[1] = (half, np.pi, half, 0.0), (0.0, half, half, 0.0)
    io["s5_phase"] = np.ascontiguousarray(np.repeat(phase, S5P, axis=0).reshape(P, 4))
    freq = np.float32(10000.0) ** (-np.arange(0, HD, 2, dtype=np.float32) / np.float32(HD))
    angle = (np.arange(T, dtype=np.float32)[:, None] * freq[None, :]).astype(np.float32).T
    io["cossin"] = np.ascontiguousarray(np.stack([np.tile(np.cos(angle), (4, 1)), np.tile(np.sin(angle), (4, 1))],
                                                 axis=1).astype(np.float32))
    rope = np.zeros((P, P), np.float32)
    for b in range(0, P, HD):
        for i in range(HD // 2):
            rope[b + HD // 2 + i, b + i] = -1.0
            rope[b + i, b + HD // 2 + i] = 1.0
    io["rope"] = rope
    i = np.arange(P)
    io["half1"] = (i[:, None] // HD == i[None, :] // HD).astype(np.float32)


def products(pe, psum, phase):
    ring, used, jobs = phase["ring"], phase["weights_used"], phase["jobs"]
    chunk, order = [-1, False], phase["order"]

    def reach(key, n):
        u = phase["units"][key] + n
        c = u // CH
        if c > chunk[0]:
            pe.wait_ge(phase["weights_in"][c % len(ring)], 16 * (c // len(ring) + 1))
            chunk[:] = [c, c > 0]
        return ring[c % len(ring)], u % CH

    def unit(key, n):
        slot, at = reach(key, n)
        return slot[:, at, :]

    def wide(key, n):
        slot, at = reach(key, n)
        return slot[:, at:at + 4, :].rearrange("p a b -> p (a b)")

    def mm(o, lhsT, rhs, start, stop):
        ins = pe.matmul(o, lhsT, rhs, start=start, stop=stop)
        if chunk[1]:
            ins.then_inc(used, 1)
            chunk[1] = False
        return ins

    def opened(name):
        n = jobs[name]
        assert n == order[0], name
        order[0] += 1
        if n >= 8:
            pe.wait_ge(phase["bank_free"][n % 8], n // 8)
        return psum[n % 8]

    def by_columns(name, key, rhs, n, m=P, depth=KT):
        ps = opened(name)
        for kt in range(depth):
            ins = mm(ps[0:m, 0:n], unit(key, kt)[:, 0:m], rhs(kt), kt == 0, kt == depth - 1)
        ins.then_inc(phase["bank_done"], 1)

    def by_rows(names, key, h, tiles):
        banks = [opened(n) for n in names]
        for kt in range(KT):
            for i, t in enumerate(tiles):
                ins = mm(banks[i][:], h[:, kt, t * P:(t + 1) * P], wide(key, 4 * kt), kt == 0, kt == KT - 1)
                if kt == KT - 1:
                    ins.then_inc(phase["bank_done"], 1)

    return unit, wide, mm, opened, by_columns, by_rows


def half_of(name, block, rows, wide=False):
    return (UNITS_B[name, block] + rows * (4 if wide else 1) - 1) // HALF


def split_products(pe, psum, phase):
    parts, jobs, order, half = phase["parts"], phase["jobs"], phase["order"], [-1, False]

    def reach(key, n):
        u = UNITS_B[key] + n
        c = u // HALF
        if c > half[0]:
            pe.wait_ge(phase["weights_split"], c + 1)
            half[:] = [c, c > 0]
        return parts[c % 2], u % HALF

    def mm(o, lhsT, rhs, start, stop):
        ins = pe.matmul(o, lhsT, rhs, start=start, stop=stop)
        if half[1]:
            ins.then_inc(phase["split_used"], 1)
            half[1] = False
        return ins

    def opened(name):
        n = jobs[name]
        assert n == order[0], name
        order[0] += 1
        pe.wait_ge(phase["bank_free"][n % 8], n // 8)
        return psum[n % 8]

    def by_columns(name, key, moving, depth=KT, split_before=None):
        ps = opened(name)
        for kt in range(depth):
            (whigh, wlow), at = reach(key, kt)
            if split_before is not None:
                pe.wait_ge(phase["split_ready"], split_before + kt + 1)
            high, low = moving(kt)
            mm(ps[:], wlow[:, at, :], high, kt == 0, False)
            mm(ps[:], whigh[:, at, :], high, False, False)
            ins = mm(ps[:], whigh[:, at, :], low, False, kt == depth - 1)
        ins.then_inc(phase["bank_done"], 1)

    def by_rows(names, key, high, low):
        banks = [opened(n) for n in names]
        for kt in range(KT):
            (whigh, wlow), at = reach(key, 4 * kt)
            whigh, wlow = (w[:, at:at + 4, :].rearrange("p a b -> p (a b)") for w in (whigh, wlow))
            for t in range(NTX):
                tokens = slice(t * P, (t + 1) * P)
                mm(banks[t][:], low[:, kt, tokens], whigh, kt == 0, False)
                mm(banks[t][:], high[:, kt, tokens], whigh, False, False)
                ins = mm(banks[t][:], high[:, kt, tokens], wlow, False, kt == KT - 1)
                if kt == KT - 1:
                    ins.then_inc(phase["bank_done"], 1)

    return by_columns, by_rows


def block_kernel(nc, io, out, scratch):
    with ExitStack() as ctx:
        def sb(name, shape, dt=F32):
            return ctx.enter_context(nc.sbuf_tensor(name, shape, dt))

        def sem(name):
            return ctx.enter_context(nc.semaphore(name))

        ring_pages = sb("ring_pages", [P, RING_PAGES * KF])

        def parts_page(name, first, *shape):
            with nc.sbuf_tensor(name + "_below", [P, int((first - RING_PAGES) * KF)], F32):
                with nc.sbuf_tensor(name, [P] + list(shape), F32R) as t:
                    return t

        weight_parts = parts_page("weight_parts", 44.5, 2, 2, HALF, P)
        high_b, low_b = parts_page("high_b", 12, KT, T), parts_page("low_b", 16, KT, T)
        high_g = parts_page("high_g", 20, KT, T)
        low_p = parts_page("low_p", 38, KT, T)
        hid_parts = [parts_page(f"hidden_parts_{i}", 20 + 11 * i, 2, FFT // 2, T) for i in range(2)]
        arena = sb("arena", [P, (49 - RING_PAGES) * KF])
        psum = [ctx.enter_context(nc.psum_tensor(f"bank{b}", [P, 512], F32)) for b in range(8)]

        def page(first, *shape):
            n = int(np.prod(shape))
            of, base = (ring_pages, 0) if first < RING_PAGES else (arena, RING_PAGES)
            at = int((first - base) * KF)
            view = of[:, at:at + n]
            names = "abcde"[:len(shape)]
            if len(shape) == 1:
                return view
            return view.rearrange(f"p ({' '.join(names)}) -> p {' '.join(names)}",
                                  **{k: v for k, v in zip(names[1:], shape[1:])})

        ident = sb("ident", [P, P])
        ones = sb("ones", [P, P])
        tri = sb("tri", [P, P])
        gmask = sb("gmask", [P, 2, P], U32)
        cols = sb("cols", [P, NCOL])
        csilu = sb("csilu", [P, KT, 2])
        modc = sb("modc", [P, 48, 2])
        scale1 = sb("scale1", [P, KT, 2])
        scale2 = sb("scale2", [P, KT])
        eps = sb("eps", [P, 1])
        blast = sb("blast", [P, 2, 48])
        decay = sb("decay", [P, 2, 48])
        wgate = sb("wgate", [64, 2, 4 * P])
        stats = sb("stats", [P, 2, 6])
        meanvar = sb("meanvar", [P, NTX, 2])
        varz = sb("varz", [P, NTX])
        prob, etmp, hot = (page(27 + i / 16, NTX, NE) for i in range(3))
        rsum = sb("rsum", [P, NTX])
        hit1, hit2, rest = (page(27.25 + i / 16, NTX * NG, EG) for i in range(3))
        best1, best2, gscore, before = (sb(n, [P, NTX * NG]) for n in ("best1", "best2", "gscore", "before"))
        ghit = sb("ghit", [P, NTX, NG])
        rank = sb("rank", [P, NTX + 1, NE])
        nblk, ends = sb("nblk", [P, NE]), sb("ends", [P, NE])
        slotf = sb("slotf", [P, 2, NTX])
        planf = sb("planf", [1, 32])
        wrt = sb("wrt", [P, KT, NE])
        brow = sb("brow", [1, NE])
        wiw = sb("wiw", [P, KT, IH])
        rs_b = page(48.5, T)
        plan = sb("plan", [1, 32], I32)
        slot = sb("slot", [P, 2 * NTX], I32)
        tokw = sb("tokw", [P, 2, NTX])

        def col(name, j=0):
            return cols[:, COLS[name][0] + j:COLS[name][0] + j + 1]

        def colspan(name):
            return cols[:, COLS[name][0]:COLS[name][1]]

        ring_a = [page(2 * r, CH, P) for r in range(RING_A)]
        x = page(8, KT, T)
        h1 = page(12, KT, TA)
        kk = page(18, HEADS, TA)
        qq = page(21, HEADS, T)
        vv = page(23, NTX + NTC, D)
        la = [page(29, HEADS, TA), page(32, HEADS, TA)]
        qin = [page(35, HEADS, T), qq]
        kin = [page(37, HEADS, T), kk[:, :, 0:T]]
        ctxt = page(29, KT, TC)
        sqx, sqc = page(39, KT, T), page(43, KT, TC)
        rs1 = page(45, TA)
        lr = page(46, TA)
        eb = page(39, HEADS * TA)
        restart = page(42, TA)
        oo = page(39, KT, T)
        state = page(43, 2, HEADS, HV)
        kst = page(45, 2, HEADS * P)
        att = page(46, 2, HEADS * P)
        wsp = page(47, KT, P)
        lng, lnb = page(48, D), page(36, D)
        bsp = page(30, KT, P)
        sqo = page(31, KT, T)
        rso = page(37, HEADS, T)
        rtmp = page(35, 2, T)
        zv = page(18, NTX, D)
        zu = page(22, KT, T)
        sgb, sga = page(26, KT, T), page(43, KT, T)
        yy = page(12, KT, T)
        mtmp = page(35, 2, T)
        rs2 = page(37, T)
        h2 = page(18, KT, T)
        tok = page(22, NTX, D)
        zero = page(42.75, D // 4)
        modrow = page(33, 4, 512)
        ring_m = [page(23 + 2 * r, CH * P) for r in range(RING_M)]
        modacc = page(35, 4 * D)
        ends_le = page(26, NBLK, NE)

        weights_in = [sem(f"weights_in_{r}") for r in range(RING_A)]
        weights_used = sem("weights_used")
        bank_done = sem("bank_done")
        bank_free = [sem(f"bank_free_{b}") for b in range(8)]
        s_const, s_cols, s_x, s_ctx, s_late = (sem(n) for n in ("s_const", "s_cols", "s_x", "s_ctx", "s_late"))
        dve_step, act_step, pool_step = sem("dve_step"), sem("act_step"), sem("pool_step")
        names = ("csilu_ready", "mod1_ready", "squares", "variance", "root", "normed1", "h1_ready", "lr_ready",
                 "v_ready", "z_ready", "softplus", "b_ready", "eb_full", "eb_used", "kexp_in", "kexp_out",
                 "decay_ready", "gla_in", "kst_ready", "att_ready", "state_zero", "o_first", "o_done",
                 "sqo_ready", "silu_r", "ob_ready", "gelu_done", "zv_ready",
                 "sgb_ready", "sga_ready", "zu_ready", "y_ready", "x1_ready",
                 "normed2", "h2_ready", "tok_ready", "logit_max", "logit_exp", "onehot", "plan_ready",
                 "mod_used", "modrow_ready", "zeros_stored", "rows_stored", "slots_ready")
        S = {n: sem(n) for n in names}
        state_sem = [sem(f"state_ready_{d}") for d in range(2)]
        kst_made, le_made = sem("kst_made"), sem("le_made")
        mod_in = [sem(f"mod_weights_in_{r}") for r in range(RING_M)]
        att_flat = att.rearrange("p a b -> p (a b)")

        phase_a = dict(ring=ring_a, weights_in=weights_in, weights_used=weights_used, units=UNITS,
                       bank_done=bank_done, bank_free=bank_free, jobs=JOBS, order=[0])

        def result(eng, name):
            eng.wait_ge(bank_done, JOBS[name] + 1)
            return psum[JOBS[name] % 8]

        def free(name):
            return bank_free[JOBS[name] % 8]

        ring_e = [page(29 + 2 * r, CH * P) for r in range(RING_E)]
        xrow = page(12, D)
        xcol = page(13, KT, BLK)
        hs = page(14, 3, 512)
        hh = page(15.5, FE)
        hcol = page(17, FET, BLK)
        yrow = page(19, D)
        yg = page(29, 2, NTX, D)
        jobs_e = ["g0", "u0", "g1", "u1", "h0", "g2", "u2", "h1", "xa", "xb", "h2", "d0", "d1"]
        JE = {n: i for i, n in enumerate(jobs_e)}
        bank_e = dict(g0=(0, 0), u0=(1, 0), g1=(2, 0), u1=(3, 0), g2=(4, 0), u2=(5, 0), h0=(6, 0), h1=(7, 0),
                      xa=(0, 1), xb=(1, 1), h2=(6, 1), d0=(2, 1), d1=(3, 1))
        uses_e = [sum(b == n for b, _ in bank_e.values()) for n in range(8)]
        weights_in_e = [sem(f"expert_weights_in_{r}") for r in range(RING_E)]
        weights_used_e = sem("expert_weights_used")
        bank_done_e = sem("expert_bank_done")
        bank_free_e = [sem(f"expert_bank_free_{b}") for b in range(8)]
        for n in ("x_row_in", "x_turned", "sig_ready", "h_made", "h_turned", "y_copied", "y_stored", "moe_stored",
                  "moe_dve_done", "moe_gathered", "moe_summed"):
            S[n] = sem(n)

        def load_plan(eng):
            eng.wait_ge(S["plan_ready"], 1)
            return eng.value_load(plan[0:1, 0:1], min_val=2 * T // BLK, max_val=NBLK)

        def result_e(eng, i, name):
            eng.wait_ge(bank_done_e, i * len(JE) + (2 + JE[name] + 1))
            return psum[bank_e[name][0]]

        hb = page(12, KT, T)
        sqb = [page(first, KT, T) for first in (16, 16, 24, 16, 20)]
        u_s = page(29, KT, S5T, S5C)
        u2 = page(16, S5G, S5C)
        xs = page(29, S5C + 1, 2, S5G)
        cp = page(20, S5G, S5T + 1, S5H)
        qb = [page(37.25 + i, 8, S5T, S5H) for i in range(2)]
        qt = page(39.25, 8, 2, P)
        tmpq = page(41.25, 8 * P)
        mt = page(37.25, KT, 8, P)
        sp5 = page(41, 20, S5G)
        pw = page(42.25, S5T + 1, 2, S5G)
        bb = page(43.375, 2, S5G, S5H)
        ab8 = page(45.375, 2, 2, S5G)
        ksb = [page(45.625 + i, 8, S5T, S5H) for i in range(2)]
        kzero = page(47.625, P)
        cc = page(46.25, 2, S5G, S5H)
        tmp = page(45.625, 2, 16 * S5H)
        tmpc = page(45.625, 4 * (S5T + 1) * S5H)
        scaled = page(47.75, 2, 2, S5G)
        ys2 = page(37.25, KT, 8, S5C)
        phase = sb("phase", [P, 4])
        yn = page(41.25, KT, S5T, S5C)
        st = page(42, 2, T)
        product = page(43, 3, T)
        parts = [[weight_parts[:, i, k] for k in range(2)] for i in range(2)]

        def hid(kt):
            half = hid_parts[kt // (FFT // 2)]
            return half[:, 0, kt % (FFT // 2), :], half[:, 1, kt % (FFT // 2), :]

        raw = page(20, KT, T)
        qT, kT = page(16, KT, T), page(20, KT, T)
        vt = page(24, NTX, D)
        qiT, kiT = page(28, 4, T), page(30, T)
        wi = page(30.5, NTX, IH)
        cossin = page(31, 2, T)
        bias = [page(32, T), page(43, T)]
        score = page(32.5, T)
        rl = page(33, 2, T)
        pp = page(34, 4, T)
        pT = page(36, 2, T)
        diag = page(37, 4, P)
        rope = page(37.5, P)
        half1 = page(37.625, P)
        oT = page(38, KT, T)
        sqt = page(42, 2, T)
        rst = page(43, 2, T)
        rt = page(44, 1, T)
        m8, mx, nmx, sm, rsm = (sb(n, [P, k]) for n, k in (("m8", 8), ("mx", 4), ("nmx", 4), ("sm", 4), ("rsm", 4)))
        for n in ("sq_full",   "h_full", "x2_ready", "s5_in", "s5_u_made", "s5_u_out",
                 "u2_in", "coef_exp", "coef_ready", "cp_ready", "qb_ready", "qt_ready", "ksb_ready",
                 "s_copied", "scanned", "ys_copied", "ys_added", "ys_stored", "yn_in", "y5_ready", "g5_ready",
                 "sig_b", "st_used", "x_ready", "raw_ready", "sqt_ready", "turned_cos", "rroot",
                 "normed_q", "rope_in", "rotated", "v_rows", "relu_ready", "score_ready", "masked", "bias0",
                 "logits", "exped", "diag_ready", "pt_ready", "o_ready", "stored"):
            S["b_" + n] = sem("b_" + n)
        RS = rs_b
        mt_in = sem("b_mt_in")
        k_stored = [sem(f"b_k_stored_{i}") for i in range(2)]
        av_done, relu_used, scan_part = sem("b_av_done"), sem("b_relu_used"), sem("b_scan_part")
        high_ready, split_ready, product_ready = sem("b_high_ready"), sem("b_split_ready"), sem("b_product_ready")
        weights_high, weights_split, split_used = sem("b_weights_high"), sem("b_weights_split"), sem("b_split_used")
        phase_b = dict(phase_a, parts=parts, weights_split=weights_split, split_used=split_used,
                       split_ready=split_ready)
        h_count = {1: KT, 2: 2 * KT, 3: 3 * KT, 4: 4 * KT}
        norm_of = [s for s in range(NR) if ROPED[s][2]]
        norm_index = {s: k for k, s in enumerate(norm_of)}

        def roped_tile(s):
            name, j = ROPED[s][0], ROPED[s][1]
            return {"dq": qT, "dk": kT, "dqi": qiT}[name][:, j, :] if name != "dki" else kiT

        def weights_high_part(act, upto, done):
            for h in range(done[0], upto + 1):
                c = CHUNKS_A + h // 2
                if h % 2 == 0:
                    act.wait_ge(weights_in[c % RING_A], 16 * (c // RING_A + 1))
                if h >= 2:
                    act.wait_ge(split_used, h - 1)
                src = ring_a[c % RING_A][:, h % 2 * HALF:(h % 2 + 1) * HALF, :]
                nc.scalar.activation(parts[h % 2][0], src, ACT.Copy).then_inc(weights_high, 1)
            done[0] = max(done[0], upto + 1)

        def weights_low_part(dve, upto, done):
            for h in range(done[0], upto + 1):
                c = CHUNKS_A + h // 2
                dve.wait_ge(weights_high, h + 1)
                src = ring_a[c % RING_A][:, h % 2 * HALF:(h % 2 + 1) * HALF, :]
                nc.vector.tensor_tensor(parts[h % 2][1], src, parts[h % 2][0].bitcast(F32), ALU.subtract) \
                    .then_inc(weights_split, 1)
                if h % 2:
                    dve.wait_ge(weights_split, h + 1)
                    dve.sem_inc(weights_used, 1)
            done[0] = max(done[0], upto + 1)

        END = dict(glu=half_of("glu", 15, KT), down0=half_of("down0", 7, FFT), dki=half_of("dki", 0, KT),
                   wo=half_of("wo", 7, KT), down1=half_of("down1", 7, FFT))

        def ahead(end, name, block, rows=KT, wide=False):
            last = half_of("down1", 7, FFT)
            return min(half_of(name, block, rows, wide) + 2, END[end] + 1, last)

        def powers(k0, k1, form, g, n):
            return pw[:, k0:k1, form, g:g + n].rearrange("p k g -> p g k").unsqueeze(3) \
                .to_broadcast([P, n, k1 - k0, S5H])

        def copied(eng, ins, done, count, name):
            ins.then_inc(done, 1)
            eng.wait_ge(done, count)
            eng.sem_inc(free(name), 1)

        block = ctx.enter_context(nc.Block())

        @block.sync
        def _(sp):
            sp.dma_start(x, io["xt"].rearrange("k p t -> p k t")).then_inc(s_x, 16)
            sp.dma_start(ctxt, io["ct"].rearrange("k p t -> p k t")).then_inc(s_ctx, 16)
            for c in range(CHUNKS_A):
                if c >= RING_A:
                    sp.wait_ge(weights_used, c - RING_A + 1)
                sp.dma_start(ring_a[c % RING_A], io["wa_stream"][c].rearrange("p (u n) -> p u n", n=P)) \
                    .then_inc(weights_in[c % RING_A], 16)


            n_blocks = load_plan(sp)
            sp.wait_ge(S["rows_stored"], 16 * 2 * NTX)
            sp.wait_ge(S["onehot"], 1)
            sp.dma_start(xrow, scratch["xbuf"][0:BLK, :]).then_inc(S["x_row_in"], 16)
            with sp.Fori(0, n_blocks) as i:
                e = sp.value_load(plan[0:1, bass.ds(i + 1, 1)], min_val=0, max_val=NE - 1)
                for c in range(CHUNKS_E):
                    if c == 8:
                        sp.wait_ge(S["x_turned"], i * 2 + 2)
                        sp.dma_start(xrow, scratch["xbuf"][bass.ds(i * BLK + BLK, BLK), :]).then_inc(S["x_row_in"], 16)
                    sp.wait_ge(weights_used_e, i * CHUNKS_E + (c + 1))
                    sp.dma_start(ring_e[c % RING_E],
                                 io["we_stream"][bass.ds(e, 1), c, :, :].rearrange("a p n -> (a p) n")) \
                        .then_inc(weights_in_e[c % RING_E], 16)

            for c in range(CHUNKS_A, CHUNKS_A + CHUNKS_B):
                if c == CHUNKS_A + RING_A:
                    sp.wait_ge(S["b_s5_u_made"], KT)
                    sp.dma_start(scratch["ud"].rearrange("(k g) h s c -> (g h) k (s c)", k=KT),
                                 u_s.rearrange("p k s c -> p k (s c)")).then_inc(S["b_s5_u_out"], 16)
                    sp.wait_ge(S["b_s5_u_out"], 16)
                    for s in range(S5T):
                        sp.dma_start(u2[16 * s:16 * s + 16, :, :], scratch["ud"][:, :, s, :].rearrange("g h c -> h g c")) \
                            .then_inc(S["b_u2_in"], 16)
                    for i in range(2):
                        sp.wait_ge(k_stored[i], 16 * (KT // 2 + (i == 0)))
                    sp.wait_ge(S["b_s_copied"], 2 * KT)
                    kflat = scratch["kd"].rearrange("g h k c -> h g (k c)")
                    mflat = mt.rearrange("p t g n -> p (t g) n")
                    for s in range(S5T):
                        lo = (1 + s) * S5H
                        sp.dma_start(mflat[16 * s:16 * s + 16], kflat[:, :, lo:lo + P]).then_inc(mt_in, 16)
                sp.wait_ge(weights_used, c - RING_A + 1)
                sp.dma_start(ring_a[c % RING_A], io["wb_stream"][c - CHUNKS_A].rearrange("p (u n) -> p u n", n=P)) \
                    .then_inc(weights_in[c % RING_A], 16)
            sp.wait_ge(S["b_x_ready"], 4 * KT)
            sp.dma_start(out.rearrange("k p t -> p k t"), x).then_inc(S["b_stored"], 16)
            sp.wait_ge(S["b_stored"], 16)
        @block.gpsimd
        def _(pool):
            for dst, src in ((ident[:], io["ident"]), (tri[:], io["tri"]),
                             (gmask[:], io["gmask"]), (wgate[:], io["wgate"]), (wrt[:], io["wrouter"]),
                             (brow[:], io["b_router"]), (wiw[:], io["wiw"]), (wsp, io["sgu_w"]),
                             (lng, io["sgu_ln_g"].partition_broadcast(P))):
                pool.dma_start(dst, src).then_inc(s_const, 16)
            for c in range(2 * KT):
                if c >= RING_M:
                    pool.wait_ge(S["mod_used"], c - RING_M + 1)
                pool.dma_start(ring_m[c % RING_M], io["mod2"][c]).then_inc(mod_in[c % RING_M], 16)
            pool.wait_ge(bank_done, JA["ssx"] + 1)
            nc.gpsimd.memset(zero, 0.0).then_inc(pool_step, 1)
            pool.wait_ge(pool_step, 1)
            spread = zero.unsqueeze(1).to_broadcast([P, 4, D // 4])
            for b in range(NBLK + 1):
                pool.dma_start(scratch["xbuf"][b * BLK:(b + 1) * BLK, :].rearrange("r (a b) -> r a b", a=4), spread) \
                    .then_inc(S["zeros_stored"], 16)
            for b in range(NBLK):
                pool.dma_start(scratch["ybuf"][b * BLK:(b + 1) * BLK, :].rearrange("r (a b) -> r a b", a=4), spread) \
                    .then_inc(S["zeros_stored"], 16)
            pool.wait_ge(bank_done, JA["on0"])
            pool.dma_start(lnb, io["sgu_ln_b"].partition_broadcast(P)).then_inc(s_late, 16)
            pool.dma_start(bsp.rearrange("p a b -> p (a b)"), io["sgu_b"].partition_broadcast(P)).then_inc(s_late, 16)
            steps = [1]

            def link(ins):
                steps[0] += 1
                ins.then_inc(pool_step, 1)
                pool.wait_ge(pool_step, steps[0])

            pool.wait_ge(bank_done, JA["wb7"] + 1)
            pool.dma_start(phase[:], io["s5_phase"]).then_inc(S["b_s5_in"], 16)
            pool.dma_start(sp5[:, 0:3, :], io["s5_lam"]).then_inc(S["b_s5_in"], 16)
            pool.wait_ge(S["y_ready"], KT)
            pool.dma_start(cc, io["s5_c"]).then_inc(S["b_s5_in"], 16)
            pool.dma_start(bb, io["s5_b"]).then_inc(S["b_s5_in"], 16)
            pool.wait_ge(S["zeros_stored"], 16 * (2 * NBLK + 1))
            pool.wait_ge(S["tok_ready"], 2 * NTX)
            pool.wait_ge(S["slots_ready"], 1)
            for k in range(2):
                for t in range(NTX):
                    pool.indirect_dma_start(scratch["xbuf"],
                                            bass.IndirectOffsetOnAxis(ap=slot[:, k * NTX + t:k * NTX + t + 1], axis=0),
                                            tok[:, t, :], None).then_inc(S["rows_stored"], 16)
            pool.wait_ge(S["rows_stored"], 16 * 2 * NTX)
            pool.wait_ge(S["plan_ready"], 1)
            for n in range(S5G // 4):
                g = slice(4 * n, 4 * n + 4)
                tv = tmpc.rearrange("p (g k h) -> p g k h", g=4, h=S5H)
                c0, c1 = (cc[:, i, g, :].unsqueeze(2).to_broadcast([P, 4, S5T + 1, S5H]) for i in range(2))
                link(nc.gpsimd.tensor_tensor(cp[:, g], c0, powers(0, S5T + 1, 0, 4 * n, 4), ALU.mult))
                link(nc.gpsimd.tensor_tensor(tv, c1, powers(0, S5T + 1, 1, 4 * n, 4), ALU.mult))
                nc.gpsimd.tensor_tensor(cp[:, g], cp[:, g], tv, ALU.add).then_inc(S["b_cp_ready"], 1)
                pool.wait_ge(S["b_cp_ready"], n + 1)
            link(nc.gpsimd.memset(kzero, 0.0))
            pool.dma_start(scratch["kd"][:, :, 0:S5T, :].rearrange("g h k c -> h g (k c)"),
                           kzero[0:16].unsqueeze(1).to_broadcast([16, S5G, P])).then_inc(k_stored[0], 16)

            pool.wait_ge(S["moe_stored"], 1)
            for k in range(2):
                for t in range(NTX):
                    pool.indirect_dma_start(yg[:, k, t, :], None, scratch["ybuf"],
                                            bass.IndirectOffsetOnAxis(ap=slot[:, k * NTX + t:k * NTX + t + 1], axis=0)) \
                        .then_inc(S["moe_gathered"], 16)
            for t in range(KT):
                pool.wait_ge(S["b_ksb_ready"], 2 * t + 2)
                pool.dma_start(scratch["kd"][8 * t:8 * t + 8, :, S5T:, :].rearrange("g h k c -> h g (k c)"),
                               ksb[t % 2][0:16].rearrange("p g k c -> p g (k c)")).then_inc(k_stored[t % 2], 16)
            pool.wait_ge(S["b_ys_stored"], 2 * 16 * S5T)
            pool.dma_start(yn.rearrange("p k s c -> p k (s c)"),
                           scratch["yd"].rearrange("(k g) h s c -> (g h) k (s c)", k=KT)).then_inc(S["b_yn_in"], 16)
            pool.wait_ge(S["b_x_ready"], 2 * KT)
            for dst, src in ((cossin, io["cossin"]), (rope, io["rope"]), (half1, io["half1"])):
                pool.dma_start(dst, src).then_inc(S["b_rope_in"], 16)
            pool.wait_ge(S["b_rope_in"], 48)
            for s in range(NR):
                pool.wait_ge(bank_done, JB[f"rot{s}"] + 1)
                v = roped_tile(s)
                nc.gpsimd.tensor_tensor(v, v, cossin[:, 0, :], ALU.mult).then_inc(S["b_turned_cos"], 1)
            pool.wait_ge(S["b_bias0"], 1)
            nc.gpsimd.affine_select(out=bias[0][:, 0:P], in_=bias[0][:, 0:P], compare_op=ALU.is_ge, fill=MASKED, base=0,
                                    pattern=[[-1, P]], channel_multiplier=1).then_inc(S["b_masked"], 1)
            for t in range(1, NTX):
                pool.wait_ge(S["b_score_ready"], t)
                nc.gpsimd.affine_select(out=score[:, t * P:(t + 1) * P], in_=score[:, t * P:(t + 1) * P],
                                        compare_op=ALU.is_ge, fill=MASKED, base=0, pattern=[[-1, P]],
                                        channel_multiplier=1).then_inc(S["b_masked"], 1)
        @block.tensor
        def _(pe):
            unit, wide, mm, opened, by_columns, by_rows = products(pe, psum, phase_a)
            pe.wait_ge(s_cols, 32)
            for i, (name, sq, n) in enumerate((("ssx", sqx, T), ("ssc", sqc, TC))):
                pe.wait_ge(S["squares"], i + 1)
                ps = opened(name)
                for kt in range(KT):
                    ins = mm(ps[:, 0:n], ones[:], sq[:, kt, :], kt == 0, kt == KT - 1)
                ins.then_inc(bank_done, 1)
            pe.wait_ge(S["csilu_ready"], 1)
            for n in range(4):
                ps = opened(f"modrow{n}")
                for kt in range(KT):
                    ins = mm(ps[0:2, :], csilu[:, kt, :], wide(("mod", n), 4 * kt), kt == 0, kt == KT - 1)
                ins.then_inc(bank_done, 1)
            pe.wait_ge(s_const, 16 * 9)
            pe.wait_ge(S["modrow_ready"], 4)
            ps = opened("mod1")
            for b in range(16):
                ins = pe.transpose(ps[:, 2 * b:2 * b + 2], modrow[0:2, b // 4, (b % 4) * P:(b % 4 + 1) * P],
                                   ident[0:2, 0:2])
            ins.then_inc(bank_done, 1)
            hx = lambda kt: h1[:, kt, 0:T]
            hc = lambda kt: h1[:, kt, T:TA]
            pe.wait_ge(S["h1_ready"], 2 * KT)
            by_columns("lrx", ("lr", 0), hx, T, 64)
            by_columns("lrc", ("lr", 0), hc, TC, 64)
            for h in range(HEADS):
                by_columns(f"kx{h}", ("k", h), hx, T)
                by_columns(f"kc{h}", ("k", h), hc, TC)
            pe.wait_ge(S["mod_used"], 2 * KT)
            ps = opened("mod2")
            for b in range(32):
                ins = pe.matmul(ps[:, b:b + 1], modacc[:, b * P:(b + 1) * P], ones[:, 0:1], start=True, stop=True)
            ins.then_inc(bank_done, 1)
            pe.wait_ge(S["lr_ready"], 2)
            for d in range(2):
                for h in range(HEADS):
                    for s, a, b in (("x", 0, T), ("c", T, TA)):
                        ps = opened(f"la{s}{d}{h}")
                        pe.matmul(ps[:, 0:b - a], wgate[32 * d:32 * d + RANK, d, h * P:(h + 1) * P],
                                  lr[32 * d:32 * d + RANK, a:b], start=True, stop=True).then_inc(bank_done, 1)
            for h in range(HEADS):
                by_columns(f"q{h}", ("q", h), hx, T)

            for n in range(2):
                by_rows([f"v{n}{t}" for t in range(NTX + NTC)], ("v", n), h1, range(NTX + NTC))

            pe.wait_ge(S["v_ready"], 2 * (NTX + NTC))
            pe.wait_ge(S["state_zero"], 1)
            n_kst, n_att, n_state = 0, 0, [0, 0]

            def keys_and_scores(i):
                d, m, is_x, _, _ = GLA[i]
                at = (0 if is_x else T) + m * P
                pe.wait_ge(S["gla_in"], d + 1)
                ps = opened(f"kT{d}{is_x}{m}")
                for h in range(HEADS):
                    ins = pe.transpose(ps[:, h * P:(h + 1) * P], la[d][:, h, at:at + P], ident[:])
                ins.then_inc(bank_done, 1)
                if is_x:
                    ps = opened(f"att{d}{m}")
                    for h in range(HEADS):
                        ins = pe.matmul(ps[:, h * P:(h + 1) * P], kin[d][:, h, at:at + P], qin[d][:, h, at:at + P],
                                        start=True, stop=True)
                    ins.then_inc(bank_done, 1)

            keys_and_scores(0)
            for i, (d, m, is_x, cs, last) in enumerate(GLA):
                at = (0 if is_x else T) + m * P
                tile = m if is_x else NTX + m
                if i + 1 < len(GLA):
                    keys_and_scores(i + 1)
                if is_x:
                    n_att += 1
                    pe.wait_ge(S["att_ready"], n_att)
                n_kst += 1
                pe.wait_ge(S["kst_ready"], n_kst)
                for n, c in enumerate(cs):
                    lo = 64 * c
                    if is_x:
                        ps = opened(f"o{d}{m}{c}")
                        pe.wait_ge(state_sem[d], n_state[d])
                        for h in range(HEADS):
                            for half in range(2):
                                o = ps[:, (2 * h + half) * GC:(2 * h + half + 1) * GC]
                                f = h * HV + half * P
                                pe.matmul(o, vv[lo:lo + 64, tile, f:f + P],
                                          att[lo:lo + 64, d, h * P + lo:h * P + lo + 64], start=True, stop=False)
                                ins = pe.matmul(o, state[:, d, h, half * P:(half + 1) * P],
                                                qin[d][:, h, at + lo:at + lo + GC], start=False, stop=True)
                        ins.then_inc(bank_done, 1)
                    if last and n == 1:
                        continue
                    for i in range(2):
                        ps = opened(f"st{d}{is_x}{m}{c}{i}")
                        for h in (2 * i, 2 * i + 1):
                            ins = pe.matmul(ps[:, (h % 2) * HV:(h % 2 + 1) * HV],
                                            kst[lo:lo + 64, d, h * P:(h + 1) * P],
                                            vv[lo:lo + 64, tile, h * HV:(h + 1) * HV], start=True, stop=True)
                        ins.then_inc(bank_done, 1)
                    n_state[d] += 4

            pe.wait_ge(S["sqo_ready"], 1)
            for h in range(HEADS):
                ps = opened(f"on{h}")
                for i in range(2):
                    ins = pe.matmul(ps[:], ones[:], sqo[:, 2 * h + i, :], start=(i == 0), stop=(i == 1))
                ins.then_inc(bank_done, 1)
            for j in range(KT):
                by_columns(f"r{j}", ("r", j), hx, T)
            for n in range(2):
                by_rows([f"zv{n}{t}" for t in range(NTX)], ("zv", n), h1, range(NTX))
            for w in ("zu", "gb", "ga"):
                for j in range(KT):
                    by_columns(f"{w}{j}", (w, j), hx, T)
            pe.wait_ge(S["zv_ready"], NTX)
            for j in range(KT):
                ps = opened(f"mix{j}")
                for t in range(NTX):
                    ins = pe.matmul(ps[:, t * P:(t + 1) * P], zv[:, t, j * P:(j + 1) * P], wsp[:, j, :],
                                    start=True, stop=True)
                ins.then_inc(bank_done, 1)
            pe.wait_ge(S["ob_ready"], KT)
            for j in range(KT):
                by_columns(f"wb{j}", ("wb", j), lambda kt: oo[:, kt, :], T)
            pe.wait_ge(S["zu_ready"], KT)
            for j in range(KT):
                by_columns(f"wa{j}", ("wa", j), lambda kt: zu[:, kt, :], T)
            pe.wait_ge(S["y_ready"], KT)
            for j in range(KT):
                by_columns(f"wout{j}", ("wout", j), lambda kt: yy[:, kt, :], T)
            ps = opened("ss2")
            for kt in range(KT):
                pe.wait_ge(S["squares"], 3 + kt)
                ins = pe.matmul(ps[:], ones[:], sqo[:, kt, :], start=(kt == 0), stop=(kt == KT - 1))
            ins.then_inc(bank_done, 1)
            pe.wait_ge(S["h2_ready"], KT)
            ps = opened("route")
            for t in range(NTX):
                o = ps[:, t * NE:(t + 1) * NE]
                pe.matmul(o, ones[0:1, :], brow[:], start=True, stop=False)
                for kt in range(KT):
                    ins = pe.matmul(o, h2[:, kt, t * P:(t + 1) * P], wrt[:, kt, :], start=False, stop=(kt == KT - 1))
            ins.then_inc(bank_done, 1)
            for t in range(NTX):
                for n in range(2):
                    ps = opened(f"tok{t}{n}")
                    for i in range(4):
                        ins = pe.transpose(ps[:, i * P:(i + 1) * P], h2[:, 4 * n + i, t * P:(t + 1) * P], ident[:])
                    ins.then_inc(bank_done, 1)
            pe.wait_ge(S["onehot"], 1)
            ps = opened("rank")
            for t in range(NTX + 1):
                o = ps[:, t * NE:(t + 1) * NE]
                for u in range(t):
                    ins = pe.matmul(o, ones[:], hot[:, u, :], start=(u == 0), stop=(t == NTX and u == NTX - 1))
                if t < NTX:
                    ins = pe.matmul(o, tri[:], hot[:, t, :], start=(t == 0), stop=True)
            ins.then_inc(bank_done, 1)

            n_blocks = load_plan(pe)
            for b in range(8):
                pe.wait_ge(bank_free[b], sum(n % 8 == b for n in JA.values()))
                pe.sem_inc(bank_free_e[b], 1)
            pe.sem_inc(weights_used_e, RING_E - 1)

            def turn(ps, src, n):
                for q in range(4):
                    ins = pe.transpose(ps[:, q * P:(q + 1) * P], src[:, (4 * n + q) * P:(4 * n + q + 1) * P], ident[:])
                ins.then_inc(bank_done_e, 1)

            pe.wait_ge(S["x_row_in"], 16)
            for n in range(2):
                pe.wait_ge(bank_free_e[n], 1)
                turn(psum[n], xrow, n)
            with pe.Fori(0, n_blocks) as i:
                def opened_e(name):
                    bank, use = bank_e[name]
                    before = 1 if bank < 2 else 0
                    pe.wait_ge(bank_free_e[bank], i * uses_e[bank] + (before + use + 1))
                    return psum[bank]

                def chunk_e(c):
                    pe.wait_ge(weights_in_e[c % RING_E], i * (16 * CHUNKS_E // RING_E) + 16 * (c // RING_E + 1))
                    return ring_e[c % RING_E]

                def up_half(name, n, c0):
                    ps = opened_e(name)
                    for kt in range(KT):
                        if kt % 4 == 0:
                            slot_e = chunk_e(c0 + kt // 4)
                        ins = pe.matmul(ps[:], xcol[:, kt, :], slot_e[:, (kt % 4) * 512:(kt % 4 + 1) * 512],
                                        start=(kt == 0), stop=(kt == KT - 1))
                        if kt % 4 == 0:
                            ins.then_inc(weights_used_e, 1)
                    ins.then_inc(bank_done_e, 1)

                def turn_h(n):
                    pe.wait_ge(S["h_made"], i * 3 + (n + 1))
                    turn(opened_e(f"h{n}"), hh, n)

                pe.wait_ge(S["x_turned"], i * 2 + 2)
                for n in range(2):
                    up_half(f"g{n}", n, 4 * n)
                    up_half(f"u{n}", n, 4 * n + 2)
                turn_h(0)
                up_half("g2", 2, 8)
                up_half("u2", 2, 10)
                turn_h(1)
                pe.wait_ge(S["x_row_in"], i * 16 + 32)
                turn(opened_e("xa"), xrow, 0)
                turn(opened_e("xb"), xrow, 1)
                turn_h(2)
                down = [opened_e("d0"), opened_e("d1")]
                for kt in range(FET):
                    if kt % 4 == 0:
                        pe.wait_ge(S["h_turned"], i * 3 + (kt // 4 + 1))
                    if kt % 2 == 0:
                        slot_e = chunk_e(12 + kt // 2)
                    for n in range(2):
                        ins = pe.matmul(down[n][:], hcol[:, kt, :],
                                        slot_e[:, (kt % 2) * D + n * 512:(kt % 2) * D + (n + 1) * 512],
                                        start=(kt == 0), stop=(kt == FET - 1))
                        if kt % 2 == 0 and n == 0:
                            ins.then_inc(weights_used_e, 1)
                        if kt == FET - 1:
                            ins.then_inc(bank_done_e, 1)

            pe.wait_ge(S["moe_stored"], 1)
            pe.wait_ge(S["moe_dve_done"], 1)
            pe.wait_ge(S["moe_summed"], NTX)
            for j in range(KT):
                ps = opened(f"y{j}")
                for t in range(NTX):
                    ins = pe.transpose(ps[:, t * P:(t + 1) * P], yg[:, 0, t, j * P:(j + 1) * P], ident[:])
                ins.then_inc(bank_done, 1)

            def squares(n):
                ps = opened(f"sn{n}")
                for kt in range(KT):
                    pe.wait_ge(S["b_sq_full"], KT * n + kt + 1)
                    ins = pe.matmul(ps[:], ones[:], sqb[n][:, kt, :], start=(kt == 0), stop=(kt == KT - 1))
                ins.then_inc(bank_done, 1)

            squares(0)
            squares(1)
            for t in range(KT):
                pe.wait_ge(S["b_qb_ready"], t + 1)
                for i in range(2):
                    ps = opened(f"qt{t}{i}")
                    for n in range(4):
                        ins = pe.transpose(ps[:, n * P:(n + 1) * P],
                                           qb[t % 2][:, 4 * i + n, :, :].rearrange("p s h -> p (s h)"), ident[:])
                    ins.then_inc(bank_done, 1)
                pe.wait_ge(S["b_cp_ready"], S5G // 4)
                for i in range(2):
                    ps = opened(f"kk{t}{i}")
                    for n in range(4):
                        g = 4 * i + n
                        ins = pe.matmul(ps[0:16, n * P:(n + 1) * P], qb[t % 2][:, g, 0, :],
                                        cp[:, 8 * t + g, 0:S5T, :].rearrange("p k h -> p (k h)"),
                                        start=True, stop=True)
                    ins.then_inc(bank_done, 1)
                pe.wait_ge(S["b_qt_ready"], 6 * t + 6)
                if t == 0:
                    pe.wait_ge(S["b_u2_in"], 16 * S5T)
                for i in range(2):
                    ps = opened(f"s{t}{i}")
                    for n in range(4):
                        for f in range(2):
                            g = 4 * i + n
                            o = (2 * n + f) * S5C
                            ins = pe.matmul(ps[:, o:o + S5C], qt[:, g, f, :], u2[:, 8 * t + g, :],
                                            start=True, stop=True)
                    ins.then_inc(bank_done, 1)
            pe.wait_ge(mt_in, 16 * S5T)
            for t in range(KT):
                ps = opened(f"yu{t}")
                for n in range(8):
                    ins = pe.matmul(ps[:, n * S5C:(n + 1) * S5C], mt[:, t, n, :], u2[:, 8 * t + n, :],
                                    start=True, stop=True)
                ins.then_inc(bank_done, 1)
            pe.wait_ge(S["b_scanned"], 1)
            for t in range(KT):
                ps = opened(f"ys{t}")
                for n in range(8):
                    ins = pe.matmul(ps[:, n * S5C:(n + 1) * S5C],
                                    cp[:, 8 * t + n, 1:S5T + 1, :].rearrange("p k h -> p (k h)"),
                                    xs[:, 0:S5C, 0, 8 * t + n], start=True, stop=True)
                ins.then_inc(bank_done, 1)
            by_columns, by_rows = split_products(pe, psum, phase_b)
            for b in range(2 * KT):
                by_columns(f"glu{b}", ("glu", b), lambda kt: (high_g[:, kt, :], low_b[:, kt, :]),
                           split_before=None if b else 0)

            def dense(n):
                squares(2 + 2 * n)
                for b in range(2 * FFT):
                    by_columns(f"gu{n}{b}", (f"gu{n}", b), lambda kt: (high_b[:, kt, :], low_b[:, kt, :]),
                               split_before=None if b else (1 + 3 * n) * KT + n * FFT)
                pe.wait_ge(split_ready, (2 + 3 * n) * KT + (n + 1) * FFT)
                for j in range(KT):
                    by_columns(f"down{n}{j}", (f"down{n}", j), hid, depth=FFT)

            dense(0)
            squares(3)
            pe.wait_ge(S["b_rope_in"], 48)
            for s in range(NR + 2):
                if s < NR:
                    if s == 2 * KT:
                        for n in range(2):
                            by_rows([f"dv{n}{t}" for t in range(NTX)], ("dv", n), high_b, low_p)
                    by_columns(f"pr{s}", (ROPED[s][0], ROPED[s][1]), lambda kt: (high_b[:, kt, :], low_p[:, kt, :]),
                               split_before=None if s else 2 * KT + FFT)
                if 1 <= s <= NR and ROPED[s - 1][2]:
                    pe.wait_ge(S["b_sqt_ready"], norm_index[s - 1] + 1)
                    ps = opened(f"pn{s - 1}")
                    pe.matmul(ps[:], half1, sqt[:, norm_index[s - 1] % 2, :], start=True, stop=True) \
                        .then_inc(bank_done, 1)
                if s >= 2:
                    if ROPED[s - 2][2]:
                        pe.wait_ge(S["b_normed_q"], norm_index[s - 2] + 1)
                    else:
                        pe.wait_ge(S["b_raw_ready"], s - 1)
                    ps = opened(f"rot{s - 2}")
                    pe.matmul(ps[:], rope, roped_tile(s - 2), start=True, stop=True).then_inc(bank_done, 1)
            ps = opened("wi")
            for t in range(NTX):
                for kt in range(KT):
                    for part in (high_b, low_p):
                        ins = pe.matmul(ps[:, t * IH:(t + 1) * IH], part[:, kt, t * P:(t + 1) * P].bitcast(F32),
                                        wiw[:, kt, :], start=(kt == 0 and part is high_b),
                                        stop=(kt == KT - 1 and part is low_p))
            ins.then_inc(bank_done, 1)
            pe.wait_ge(S["b_rotated"], NR)
            pe.wait_ge(S["b_v_rows"], 2 * NTX)
            for s in range(NPAIR + VALUE_LAG):
                if TURN_LAG <= s < NPAIR + TURN_LAG:
                    k = s - TURN_LAG
                    t, h = PAIRS[k]
                    pe.wait_ge(S["b_diag_ready"], k + 1)
                    ps = opened(f"pt{k}")
                    for b in range(t + 1):
                        ins = pe.matmul(ps[:, b * P:(b + 1) * P], pp[:, k % 4, b * P:(b + 1) * P],
                                        diag[:, k % 4, :], start=True, stop=True)
                    ins.then_inc(bank_done, 1)
                if s >= VALUE_LAG:
                    k = s - VALUE_LAG
                    t, h = PAIRS[k]
                    pe.wait_ge(S["b_pt_ready"], k + 1)
                    if h % 2 == 0:
                        ps = opened(f"av{k}")
                        av = ps
                    r = 64 * (h % 2)
                    for b in range(t + 1):
                        ins = pe.matmul(av[r:r + 64, 0:P], vt[:, b, h * HD:(h + 1) * HD],
                                        pT[:, k % 2, b * P:(b + 1) * P], start=(b == 0), stop=(b == t))
                    ins.then_inc(av_done if h % 2 else bank_done, 1)
                if s < NPAIR:
                    t, h = PAIRS[s]
                    ps = opened(f"lg{s}")
                    r = 64 * (h % 2)
                    pe.matmul(ps[:, 0:(t + 1) * P], qT[r:r + 64, h // 2, t * P:(t + 1) * P],
                              kT[r:r + 64, h // 2, 0:(t + 1) * P], start=True, stop=True).then_inc(bank_done, 1)
                    if h == 1 and t < NTX - 1:
                        for i in range(IH):
                            ps = opened(f"ix{t + 1}{i}")
                            r = 64 * (i % 2)
                            pe.matmul(ps[:, 0:(t + 2) * P], qiT[r:r + 64, i // 2, (t + 1) * P:(t + 2) * P],
                                      kiT[r:r + 64, 0:(t + 2) * P], start=True, stop=True).then_inc(bank_done, 1)
            pe.wait_ge(split_ready, 4 * KT + FFT)
            for j in range(KT):
                by_columns(f"wo{j}", ("wo", j), lambda kt: (high_b[:, kt, :], low_b[:, kt, :]))
            dense(1)

        @block.scalar
        def _(act):
            steps = [0]

            def link(ins):
                steps[0] += 1
                ins.then_inc(act_step, 1)
                act.wait_ge(act_step, steps[0])

            act.dma_start(cols[:], io["cols"]).then_inc(s_cols, 16)
            act.dma_start(ones[:], io["ones"]).then_inc(s_cols, 16)
            act.wait_ge(s_cols, 32)
            cc = colspan("c").rearrange("p (s k) -> p k s", s=2)
            nc.scalar.activation(csilu[:], cc, ACT.Silu).then_inc(S["csilu_ready"], 1)
            act.wait_ge(s_x, 16)
            nc.scalar.activation(sqx, x, ACT.Square).then_inc(S["squares"], 1)
            act.wait_ge(s_ctx, 16)
            nc.scalar.activation(sqc, ctxt, ACT.Square).then_inc(S["squares"], 1)
            act.wait_ge(S["variance"], 2)
            nc.scalar.activation(rs1, rs1, ACT.Sqrt).then_inc(S["root"], 1)
            for n in range(4):
                ps = result(act, f"modrow{n}")
                nc.scalar.activation(modrow[0:2, n, :], ps[0:2, :], ACT.Copy).then_inc(S["modrow_ready"], 1)
                act.wait_ge(S["modrow_ready"], n + 1)
                act.sem_inc(free(f"modrow{n}"), 1)
            act.wait_ge(S["mod1_ready"], 3)
            act.wait_ge(S["normed1"], 2)
            for kt in range(KT):
                for s, (a, b) in enumerate(((0, T), (T, TA))):
                    nc.scalar.activation(h1[:, kt, a:b], h1[:, kt, a:b], ACT.Identity, bias=modc[:, kt, s:s + 1],
                                         scale=scale1[:, kt, s:s + 1]).then_inc(S["h1_ready"], 1)
            for name, a, b in (("lrx", 0, T), ("lrc", T, TA)):
                ps = result(act, name)
                nc.scalar.activation(lr[0:64, a:b], ps[0:64, 0:b - a], ACT.Copy).then_inc(S["lr_ready"], 1)
                act.wait_ge(S["lr_ready"], 1 + (a > 0))
                act.sem_inc(free(name), 1)
            for h in range(HEADS):
                for s, a, b in (("x", 0, T), ("c", T, TA)):
                    ps = result(act, f"k{s}{h}")
                    nc.scalar.activation(kk[:, h, a:b], ps[:, 0:b - a], ACT.Copy).then_inc(free(f"k{s}{h}"), 1)
            for d in range(2):
                act.wait_ge(S["z_ready"], d + 1)
                zf = la[d].rearrange("p a b -> p (a b)")
                link(nc.scalar.activation(eb, zf, ACT.Abs))
                link(nc.scalar.activation(eb, eb, ACT.Exp, scale=-1.0))
                nc.scalar.activation(eb, eb, ACT.Ln, bias=1.0).then_inc(S["softplus"], 1)
                act.wait_ge(S["b_ready"], d + 1)
                nc.scalar.activation(decay[:, d, :], blast[:, d, :], ACT.Exp, scale=1.0 / 16).then_inc(S["decay_ready"], 1)
                ebx = eb[:, 0:HEADS * T].rearrange("p (a b) -> p a b", a=HEADS)
                if d == 0:
                    for h in range(HEADS):
                        ps = result(act, f"q{h}")
                        nc.scalar.activation(qq[:, h, :], ps[:], ACT.Copy, scale=float(HK) ** -0.5) \
                            .then_inc(free(f"q{h}"), 1)
                nc.scalar.activation(ebx, la[d][:, :, 0:T], ACT.Exp, scale=1.0 / 16).then_inc(S["eb_full"], 1)
                act.wait_ge(S["eb_used"], 2 * d + 1)
                nc.scalar.activation(ebx, la[d][:, :, 0:T], ACT.Exp, scale=-1.0 / 16).then_inc(S["eb_full"], 1)
                act.wait_ge(S["kexp_in"], d + 1)
                nc.scalar.activation(zf, zf, ACT.Exp, scale=1.0 / 16).then_inc(S["kexp_out"], 1)
            n_v = 0
            for n in range(2):
                for t in range(NTX + NTC):
                    ps = result(act, f"v{n}{t}")
                    nc.scalar.activation(vv[:, t, n * 512:(n + 1) * 512], ps[:], ACT.Copy).then_inc(S["v_ready"], 1)
                    n_v += 1
                    act.wait_ge(S["v_ready"], n_v)
                    act.sem_inc(free(f"v{n}{t}"), 1)
            step = [0, 0]
            n_first = 0

            def keys(i):
                d, m, is_x, _, _ = GLA[i]
                ps = result(act, f"kT{d}{is_x}{m}")
                nc.scalar.activation(kst[:, d, :], ps[:], ACT.Copy).then_inc(S["kst_ready"], 1)
                act.wait_ge(S["kst_ready"], i + 1)
                act.sem_inc(free(f"kT{d}{is_x}{m}"), 1)

            keys(0)
            for i, (d, m, is_x, cs, last) in enumerate(GLA):
                if i + 1 < len(GLA):
                    keys(i + 1)
                for c in cs:
                    if is_x:
                        if step[d] < 4:
                            if n_first == 0:
                                act.wait_ge(S["zeros_stored"], 16 * (2 * NBLK + 1))
                            ps = result(act, f"o{d}{m}{c}")
                            nc.scalar.activation(oo[:, :, m * P + c * GC:m * P + c * GC + GC],
                                                 ps.rearrange("p (f t) -> p f t", t=GC), ACT.Copy) \
                                .then_inc(S["o_first"], 1)
                            n_first += 1
                            act.wait_ge(S["o_first"], n_first)
                            act.sem_inc(free(f"o{d}{m}{c}"), 1)
                        step[d] += 1
            act.wait_ge(S["o_done"], 8)
            nc.scalar.activation(sqo, oo, ACT.Square).then_inc(S["sqo_ready"], 1)
            act.wait_ge(S["variance"], 2 + HEADS)
            nc.scalar.activation(rso, rso, ACT.Sqrt).then_inc(S["root"], 1)
            for j in range(KT):
                ps = result(act, f"r{j}")
                if j >= 2:
                    act.wait_ge(S["ob_ready"], j - 1)
                nc.scalar.activation(rtmp[:, j % 2, :], ps[:], ACT.Silu).then_inc(S["silu_r"], 1)
                act.wait_ge(S["silu_r"], j + 1)
                act.sem_inc(free(f"r{j}"), 1)
            n_z = 0
            for n in range(2):
                for t in range(NTX):
                    ps = result(act, f"zv{n}{t}")
                    nc.scalar.activation(zv[:, t, n * 512:(n + 1) * 512], ps[:], ACT.Gelu_apprx_tanh) \
                        .then_inc(S["gelu_done"], 1)
                    n_z += 1
                    act.wait_ge(S["gelu_done"], n_z)
                    act.sem_inc(free(f"zv{n}{t}"), 1)
            for j in range(KT):
                ps = result(act, f"zu{j}")
                nc.scalar.activation(zu[:, j, :], ps[:], ACT.Gelu_apprx_tanh).then_inc(S["gelu_done"], 1)
                act.wait_ge(S["gelu_done"], 2 * NTX + j + 1)
                act.sem_inc(free(f"zu{j}"), 1)
            act.wait_ge(S["variance"], 2 + HEADS + NTX)
            nc.scalar.activation(varz[:], varz[:], ACT.Sqrt).then_inc(S["root"], 1)
            for w, dst, key, first in (("gb", sgb, "sgb_ready", KT), ("ga", sga, "sga_ready", 0)):
                for j in range(KT):
                    ps = result(act, f"{w}{j}")
                    nc.scalar.activation(dst[:, j, :], ps[:], ACT.Sigmoid, bias=col("b_branch", first + j)) \
                        .then_inc(S[key], 1)
                    act.wait_ge(S[key], j + 1)
                    act.sem_inc(free(f"{w}{j}"), 1)
            act.wait_ge(S["b_s5_in"], 32)
            nc.scalar.activation(sp5[:, 3, :], sp5[:, 2, :], ACT.Exp).then_inc(S["b_coef_exp"], 1)
            act.wait_ge(S["b_coef_ready"], 1)
            nc.scalar.activation(sp5[:, 4, :], sp5[:, 4, :], ACT.Exp).then_inc(S["b_coef_exp"], 1)
            nc.scalar.activation(sp5[:, 8:12, :], sp5[:, 8:12, :], ACT.Sin).then_inc(S["b_coef_exp"], 1)
            for kt in range(KT):
                act.wait_ge(S["x1_ready"], kt + 1)
                nc.scalar.activation(sqo[:, kt, :], x[:, kt, :], ACT.Square).then_inc(S["squares"], 1)
            act.wait_ge(S["variance"], 3 + HEADS + NTX)
            nc.scalar.activation(rs2, rs2, ACT.Sqrt).then_inc(S["root"], 1)
            act.wait_ge(S["normed2"], 1)
            for kt in range(KT):
                nc.scalar.activation(h2[:, kt, :], h2[:, kt, :], ACT.Identity, bias=modc[:, 24 + kt, 0:1],
                                     scale=scale2[:, kt:kt + 1]).then_inc(S["h2_ready"], 1)
            act.wait_ge(S["logit_max"], 1)
            nc.scalar.activation(prob[:], prob[:], ACT.Exp).then_inc(S["logit_exp"], 1)
            for t in range(NTX):
                for n in range(2):
                    ps = result(act, f"tok{t}{n}")
                    nc.scalar.activation(tok[:, t, n * 512:(n + 1) * 512], ps[:], ACT.Copy).then_inc(S["tok_ready"], 1)
                    act.wait_ge(S["tok_ready"], 2 * t + n + 1)
                    act.sem_inc(free(f"tok{t}{n}"), 1)


            n_blocks = load_plan(act)

            def turned(name, dst, ps, done, count):
                nc.scalar.activation(dst, ps, ACT.Copy).then_inc(done, 1)
                act.wait_ge(done, count)
                act.sem_inc(bank_free_e[bank_e[name][0]], 1)

            for n in range(2):
                act.wait_ge(bank_done_e, n + 1)
                turned(f"x{'ab'[n]}", xcol[:, 4 * n:4 * n + 4, :].rearrange("p a b -> p (a b)"), psum[n][:],
                       S["x_turned"], n + 1)
            act.sem_inc(S["y_stored"], 16)
            with act.Fori(0, n_blocks) as i:
                for n in range(3):
                    ps = result_e(act, i, f"g{n}")
                    nc.scalar.activation(hs[:, n, :], ps[:], ACT.Silu).then_inc(S["sig_ready"], 1)
                    act.wait_ge(S["sig_ready"], i * 3 + (n + 1))
                    act.sem_inc(bank_free_e[bank_e[f"g{n}"][0]], 1)
                    if n:
                        turned(f"h{n - 1}", hcol[:, 4 * n - 4:4 * n, :].rearrange("p a b -> p (a b)"),
                               result_e(act, i, f"h{n - 1}")[:], S["h_turned"], i * 3 + n)
                for n in range(2):
                    turned(f"x{'ab'[n]}", xcol[:, 4 * n:4 * n + 4, :].rearrange("p a b -> p (a b)"),
                           result_e(act, i, f"x{'ab'[n]}")[:], S["x_turned"], i * 2 + (3 + n))
                turned("h2", hcol[:, 8:12, :].rearrange("p a b -> p (a b)"), result_e(act, i, "h2")[:],
                       S["h_turned"], i * 3 + 3)
                act.wait_ge(S["y_stored"], i * 16 + 16)
                for n in range(2):
                    turned(f"d{n}", yrow[:, n * 512:(n + 1) * 512], result_e(act, i, f"d{n}")[:],
                           S["y_copied"], i * 2 + (n + 1))
                act.dma_start(scratch["ybuf"][bass.ds(i * BLK, BLK), :], yrow).then_inc(S["y_stored"], 16)
            act.wait_ge(S["y_stored"], n_blocks * 16 + 16)
            act.sem_inc(S["moe_stored"], 1)

            def squared(n, wait, count):
                for kt in range(KT):
                    act.wait_ge(wait, count - KT + kt + 1)
                    nc.scalar.activation(sqb[n][:, kt, :], x[:, kt, :], ACT.Square).then_inc(S["b_sq_full"], 1)
                ps = result(act, f"sn{n}")
                copied(act, nc.scalar.activation(RS[:], ps[:], ACT.Sqrt, bias=eps[:], scale=1.0 / D), S["root"], 5 + n,
                       f"sn{n}")

            squared(0, S["b_x2_ready"], KT)
            squared(1, S["b_x2_ready"], 2 * KT)
            for t in range(KT):
                for i in range(2):
                    ps = result(act, f"qt{t}{i}").rearrange("p (g n) -> p g n", g=4)
                    q = qt[:, 4 * i:4 * i + 4, :, :]
                    nc.scalar.activation(q[:, :, 0, :], ps, ACT.Copy).then_inc(S["b_qt_ready"], 1)
                    nc.scalar.activation(q[:, :, 1, 0:S5P], ps[:, :, S5P:], ACT.Copy, scale=-1.0) \
                        .then_inc(S["b_qt_ready"], 1)
                    copied(act, nc.scalar.activation(q[:, :, 1, S5P:], ps[:, :, 0:S5P], ACT.Copy),
                           S["b_qt_ready"], 6 * t + 3 * i + 3, f"qt{t}{i}")
                if t >= 2:
                    act.wait_ge(k_stored[t % 2], 16 * (t // 2 + (t % 2 == 0)))
                for i in range(2):
                    ps = result(act, f"kk{t}{i}")
                    copied(act, nc.scalar.activation(ksb[t % 2][0:16, 4 * i:4 * i + 4, :, :],
                                                     ps[0:16, :].rearrange("p (g k h) -> p g k h", g=4, h=S5H),
                                                     ACT.Copy), S["b_ksb_ready"], 2 * t + i + 1, f"kk{t}{i}")
                for i in range(2):
                    ps = result(act, f"s{t}{i}")
                    g = 8 * t + 4 * i
                    copied(act, nc.scalar.activation(xs[:, 1:S5C + 1, :, g:g + 4],
                                                     ps.rearrange("p (g f c) -> p c f g", g=4, f=2), ACT.Copy),
                           S["b_s_copied"], 2 * t + i + 1, f"s{t}{i}")
            for t in range(KT):
                ps = result(act, f"yu{t}")
                copied(act, nc.scalar.activation(ys2[:, t], ps.rearrange("p (g c) -> p g c", g=8), ACT.Copy),
                       S["b_ys_copied"], t + 1, f"yu{t}")
            for t in (3, KT - 1):
                act.wait_ge(S["b_ys_added"], t + 1)
                for s in range(S5T):
                    rows = ys2[16 * s:16 * s + 16, t - 3:t + 1].rearrange("p t g c -> p (t g) c")
                    act.dma_start(scratch["yd"][8 * (t - 3):8 * (t + 1), :, s, :].rearrange("g h c -> h g c"), rows) \
                        .then_inc(S["b_ys_stored"], 16)
            for kt in range(KT):
                act.wait_ge(S["b_y5_ready"], kt + 1)
                nc.scalar.activation(hb[:, kt, :], hb[:, kt, :], ACT.Gelu_apprx_tanh).then_inc(S["b_g5_ready"], 1)
            split_to = [0]
            weights_high_part(act, 1, split_to)

            def high_part(dst, src, ready, first):
                for kt in range(KT):
                    act.wait_ge(ready, first + kt + 1)
                    nc.scalar.activation(dst[:, kt, :], src[:, kt, :], ACT.Copy).then_inc(high_ready, 1)

            high_part(high_g, hb, S["b_g5_ready"], 0)
            n_sig = 0
            for j in range(KT):
                for i in range(2):
                    weights_high_part(act, ahead("glu", "glu", 2 * j + i), split_to)
                ps = result(act, f"glu{2 * j + 1}")
                if n_sig >= 2:
                    act.wait_ge(S["b_st_used"], n_sig - 1)
                n_sig += 1
                copied(act, nc.scalar.activation(st[:, j % 2, :], ps[:], ACT.Sigmoid), S["b_sig_b"], n_sig,
                       f"glu{2 * j + 1}")

            def dense_act(n, n_sig):
                high_part(high_b, raw, S["b_h_full"], h_count[2 + 2 * n] - KT)
                for j in range(FFT):
                    weights_high_part(act, ahead(f"down{n}", f"gu{n}", 2 * j), split_to)
                    ps = result(act, f"gu{n}{2 * j}")
                    act.wait_ge(S["b_st_used"], n_sig - 1)
                    n_sig += 1
                    copied(act, nc.scalar.activation(st[:, j % 2, :], ps[:], ACT.Silu), S["b_sig_b"], n_sig,
                           f"gu{n}{2 * j}")
                    if j < FFT - 1:
                        weights_high_part(act, ahead(f"down{n}", f"gu{n}", 2 * j + 1), split_to)
                    act.wait_ge(product_ready, FFT * n + j + 1)
                    nc.scalar.activation(hid(j)[0], product[:, j % 3, :], ACT.Copy).then_inc(high_ready, 1)
                for j in range(KT):
                    weights_high_part(act, ahead(f"down{n}", f"down{n}", j, FFT), split_to)
                return n_sig

            squared(2, S["b_x_ready"], KT)
            n_sig = dense_act(0, n_sig)
            squared(3, S["b_x_ready"], 2 * KT)
            high_part(high_b, raw, S["b_h_full"], h_count[3] - KT)
            n_row = 0
            for s in range(NR + 1):
                if s == 2 * KT:
                    for n in range(2):
                        weights_high_part(act, ahead("dki", "dv", n, KT, True), split_to)
                        for t in range(NTX):
                            ps = result(act, f"dv{n}{t}")
                            n_row += 1
                            copied(act, nc.scalar.activation(vt[:, t, n * 512:(n + 1) * 512], ps[:], ACT.Copy),
                                   S["b_v_rows"], n_row, f"dv{n}{t}")
                if s < NR:
                    ps = result(act, f"pr{s}")
                    if ROPED[s][2]:
                        k = norm_index[s]
                        if k >= 2:
                            act.wait_ge(bank_done, JB[f"pn{norm_of[k - 2]}"] + 1)
                        nc.scalar.activation(sqt[:, k % 2, :], ps[:], ACT.Square).then_inc(S["b_sqt_ready"], 1)
                    copied(act, nc.scalar.activation(roped_tile(s), ps[:], ACT.Copy), S["b_raw_ready"], s + 1, f"pr{s}")
                if s >= 1 and ROPED[s - 1][2]:
                    k = norm_index[s - 1]
                    if k >= 2:
                        act.wait_ge(S["b_normed_q"], k - 1)
                    ps = result(act, f"pn{s - 1}")
                    copied(act, nc.scalar.activation(rst[:, k % 2, :], ps[:], ACT.Sqrt, bias=eps[:], scale=1.0 / HD),
                           S["b_rroot"], k + 1, f"pn{s - 1}")
                if s < NR:
                    weights_high_part(act, ahead("dki", ROPED[s][0], ROPED[s][1]), split_to)
            n_relu = 0
            for s in range(NPAIR + VALUE_LAG):
                if 1 <= s <= NPAIR:
                    t, h = PAIRS[s - 1]
                    b = (s - 1) % 4
                    act.wait_ge(S["b_logits"], s)
                    nc.scalar.activation(pp[:, b, 0:(t + 1) * P], pp[:, b, 0:(t + 1) * P], ACT.Exp,
                                         bias=nmx[:, b:b + 1], scale=float(HD) ** -0.5,
                                         accum_out=sm[:, b:b + 1]).then_inc(S["b_exped"], 1)
                if TURN_LAG <= s < NPAIR + TURN_LAG:
                    k = s - TURN_LAG
                    t, h = PAIRS[k]
                    ps = result(act, f"pt{k}")
                    if k >= 2 and k % 2 == 1:
                        act.wait_ge(av_done, (k - 2) // 2 + 1)
                    copied(act, nc.scalar.activation(pT[:, k % 2, 0:(t + 1) * P], ps[:, 0:(t + 1) * P],
                                                     ACT.Copy), S["b_pt_ready"], k + 1, f"pt{k}")
                if s >= VALUE_LAG and (s - VALUE_LAG) % 2 == 1:
                    k = s - VALUE_LAG
                    t, h = PAIRS[k]
                    name = f"av{k - 1}"
                    act.wait_ge(av_done, k // 2 + 1)
                    copied(act, nc.scalar.activation(oT[:, h // 2, t * P:(t + 1) * P], psum[JB[name] % 8][:, 0:P],
                                                     ACT.Copy), S["b_o_ready"], k // 2 + 1, name)
                if s < NPAIR:
                    t, h = PAIRS[s]
                    if h == 1 and t < NTX - 1:
                        for i in range(IH):
                            ps = result(act, f"ix{t + 1}{i}")
                            if n_relu >= 2:
                                act.wait_ge(relu_used, n_relu - 1)
                            n_relu += 1
                            copied(act, nc.scalar.activation(rl[:, i % 2, 0:(t + 2) * P], ps[:, 0:(t + 2) * P],
                                                             ACT.Relu), S["b_relu_ready"], n_relu, f"ix{t + 1}{i}")
            act.wait_ge(S["b_o_ready"], NPAIR // 2)
            high_part(high_b, oT, S["b_o_ready"], NPAIR // 2 - KT)
            for j in range(KT):
                weights_high_part(act, ahead("wo", "wo", j), split_to)
            squared(4, S["b_x_ready"], 3 * KT)
            dense_act(1, n_sig)
        @block.vector
        def _(dve):
            steps = [0]

            def link(ins):
                steps[0] += 1
                ins.then_inc(dve_step, 1)
                dve.wait_ge(dve_step, steps[0])

            link(nc.vector.memset(eps[:], EPS))
            dve.wait_ge(s_cols, 32)
            for i, (name, a, b) in enumerate((("ssx", 0, T), ("ssc", T, TA))):
                ps = result(dve, name)
                nc.vector.tensor_scalar(rs1[:, a:b], ps[:, 0:b - a], 1.0 / D, EPS, ALU.mult, ALU.add) \
                    .then_inc(S["variance"], 1)
                dve.wait_ge(S["variance"], i + 1)
                dve.sem_inc(free(name), 1)
            dve.wait_ge(S["root"], 1)
            link(nc.vector.reciprocal(rs1, rs1))
            nc.vector.tensor_tensor(h1[:, :, 0:T], x, rs1[:, 0:T].unsqueeze(1).to_broadcast([P, KT, T]), ALU.mult) \
                .then_inc(S["normed1"], 1)
            nc.vector.tensor_tensor(h1[:, :, T:TA], ctxt, rs1[:, T:TA].unsqueeze(1).to_broadcast([P, KT, TC]),
                                    ALU.mult).then_inc(S["normed1"], 1)
            dve.wait_ge(S["normed1"], 2)
            ps = result(dve, "mod1")
            link(nc.vector.tensor_tensor(modc[:, 0:16, :], ps[:, 0:32].rearrange("p (b s) -> p b s", s=2),
                                         colspan("b_mod")[:, 0:16].unsqueeze(2).to_broadcast([P, 16, 2]), ALU.add))
            dve.sem_inc(free("mod1"), 1)
            link(nc.vector.tensor_scalar(scale1[:], modc[:, 8:16, :], 1.0, None, ALU.add))
            link(nc.vector.tensor_tensor(scale1[:], scale1[:],
                                         colspan("g_norm1").unsqueeze(2).to_broadcast([P, KT, 2]), ALU.mult))
            dve.sem_inc(S["mod1_ready"], 3)
            dve.wait_ge(S["csilu_ready"], 1)
            for c in range(2 * KT):
                kt, half = c // 2, modacc[:, c % 2 * 2 * D:(c % 2 + 1) * 2 * D]
                dve.wait_ge(mod_in[c % RING_M], 16 * (c // RING_M + 1))
                if kt == 0:
                    ins = nc.vector.tensor_scalar(half, ring_m[c % RING_M], csilu[:, kt, 0:1], None, ALU.mult)
                else:
                    ins = nc.vector.scalar_tensor_tensor(out=half, in0=ring_m[c % RING_M], scalar=csilu[:, kt, 0:1], in1=half,
                                                         op0=ALU.mult, op1=ALU.add)
                ins.then_inc(S["mod_used"], 1)
                dve.wait_ge(S["mod_used"], c + 1)
            ps = result(dve, "mod2")
            link(nc.vector.tensor_tensor(modc[:, 16:48, 0], ps[:, 0:32], colspan("b_mod")[:, 16:48], ALU.add))
            dve.sem_inc(free("mod2"), 1)
            link(nc.vector.tensor_scalar(scale2[:], modc[:, 32:40, 0], 1.0, None, ALU.add))
            link(nc.vector.tensor_tensor(scale2[:], scale2[:], colspan("g_norm2"), ALU.mult))
            link(nc.vector.memset(state, 0.0))
            link(nc.vector.memset(restart, 1.0))
            link(nc.vector.memset(restart[:, 0::GC], 0.0))
            dve.sem_inc(S["state_zero"], 1)
            for d in range(2):
                for h in range(HEADS):
                    for s, a, b in (("x", 0, T), ("c", T, TA)):
                        name = f"la{s}{d}{h}"
                        ps = result(dve, name)
                        link(nc.vector.tensor_scalar(la[d][:, h, a:b], ps[:, 0:b - a], col("b_gate2", 4 * d + h), None,
                                                     ALU.add))
                        dve.sem_inc(free(name), 1)
                dve.sem_inc(S["z_ready"], 1)
            link(nc.vector.memset(att_flat, 0.0))
            for d in range(2):
                zf = la[d].rearrange("p a b -> p (a b)")
                dve.wait_ge(S["softplus"], d + 1)
                link(nc.vector.scalar_tensor_tensor(out=zf, in0=zf, scalar=0.0, in1=eb, op0=ALU.min, op1=ALU.subtract))
                for h in range(HEADS):
                    row = la[d][:, h, :] if d == 0 else la[d][:, h, ::-1]
                    link(nc.vector.tensor_tensor_scan(row, restart, row, 0.0, ALU.mult, ALU.add))
                chunks = la[d].rearrange("p h (n t) -> p h n t", t=GC)
                end = chunks[:, :, :, GC - 1] if d == 0 else chunks[:, :, :, 0]
                nc.vector.tensor_copy(blast[:, d, :].rearrange("p (h n) -> p h n", h=HEADS), end) \
                    .then_inc(S["b_ready"], 1)
                ebx = eb[:, 0:HEADS * T].rearrange("p (a b) -> p a b", a=HEADS)
                dve.wait_ge(S["eb_full"], 2 * d + 1)
                if d == 0:
                    dve.wait_ge(free("q3"), JA["q3"] // 8 + 1)
                    dve.wait_ge(free("q2"), JA["q2"] // 8 + 1)
                    dve.wait_ge(free("q1"), JA["q1"] // 8 + 1)
                    dve.wait_ge(free("q0"), JA["q0"] // 8 + 1)
                    for h in range(HEADS):
                        for s in "xc":
                            dve.wait_ge(free(f"k{s}{h}"), JA[f"k{s}{h}"] // 8 + 1)
                nc.vector.tensor_tensor(qin[d], qq, ebx, ALU.mult).then_inc(S["eb_used"], 1)
                dve.wait_ge(S["eb_full"], 2 * d + 2)

                def keys_in():
                    nc.vector.tensor_tensor(kin[d], kk[:, :, 0:T], ebx, ALU.mult).then_inc(S["eb_used"], 1)
                    dve.wait_ge(S["eb_used"], 2 * d + 2)

                if d == 0:
                    keys_in()
                end = blast[:, d, :].rearrange("p (c o) -> p c o", o=1).to_broadcast([P, 48, GC])
                ch = zf.rearrange("p (c t) -> p c t", t=GC)
                nc.vector.tensor_tensor(ch, end, ch, ALU.subtract).then_inc(S["kexp_in"], 1)
                dve.wait_ge(S["kexp_out"], d + 1)
                nc.vector.tensor_tensor(zf, kk.rearrange("p a b -> p (a b)"), zf, ALU.mult).then_inc(kst_made, 1)
                dve.wait_ge(kst_made, d + 1)
                if d == 1:
                    keys_in()
                dve.sem_inc(S["gla_in"], 1)
            step = [0, 0]
            n_state = [0, 0]
            dve.wait_ge(s_const, 16 * 9)
            dve.wait_ge(S["decay_ready"], 2)

            n_masked = [0]

            def masked_scores(i):
                d, m, is_x, _, _ = GLA[i]
                if is_x:
                    name = f"att{d}{m}"
                    ps = result(dve, name)
                    nc.vector.copy_predicated(att[:, d, :].rearrange("p (h t) -> p h t", h=HEADS),
                                              gmask[:, d, :].unsqueeze(1).to_broadcast([P, HEADS, P]),
                                              ps.rearrange("p (h t) -> p h t", h=HEADS)).then_inc(S["att_ready"], 1)
                    n_masked[0] += 1
                    dve.wait_ge(S["att_ready"], n_masked[0])
                    dve.sem_inc(free(name), 1)

            masked_scores(0)
            for i, (d, m, is_x, cs, last) in enumerate(GLA):
                if i + 1 < len(GLA):
                    masked_scores(i + 1)
                for n, c in enumerate(cs):
                    if is_x:
                        at = m * P + c * GC
                        if step[d] >= 4:
                            name = f"o{d}{m}{c}"
                            ps = result(dve, name)
                            dve.wait_ge(S["o_first"], 8)
                            link(nc.vector.tensor_tensor(oo[:, :, at:at + GC], oo[:, :, at:at + GC],
                                                         ps.rearrange("p (f t) -> p f t", t=GC), ALU.add))
                            dve.sem_inc(free(name), 1)
                            dve.sem_inc(S["o_done"], 1)
                        step[d] += 1
                    if last and n == 1:
                        continue
                    chunk = (0 if is_x else 8) + 2 * m + c
                    for half in range(2):
                        name = f"st{d}{is_x}{m}{c}{half}"
                        ps = result(dve, name)
                        for h in (2 * half, 2 * half + 1):
                            nc.vector.scalar_tensor_tensor(
                                out=state[:, d, h, :], in0=state[:, d, h, :],
                                scalar=decay[:, d, h * 12 + chunk:h * 12 + chunk + 1],
                                in1=ps[:, (h % 2) * HV:(h % 2 + 1) * HV], op0=ALU.mult, op1=ALU.add) \
                                .then_inc(state_sem[d], 1)
                            n_state[d] += 1
                            dve.wait_ge(state_sem[d], n_state[d])
                        dve.sem_inc(free(name), 1)
            for h in range(HEADS):
                ps = result(dve, f"on{h}")
                nc.vector.tensor_scalar(rso[:, h, :], ps[:], 1.0 / HV, EPS, ALU.mult, ALU.add).then_inc(S["variance"], 1)
                dve.wait_ge(S["variance"], 2 + h + 1)
                dve.sem_inc(free(f"on{h}"), 1)
            dve.wait_ge(S["root"], 2)
            link(nc.vector.reciprocal(rso, rso))
            for j in range(KT):
                link(nc.vector.scalar_tensor_tensor(out=oo[:, j, :], in0=oo[:, j, :], scalar=col("gla_g", j),
                                                    in1=rso[:, j // 2, :], op0=ALU.mult, op1=ALU.mult))
            for j in range(KT):
                dve.wait_ge(S["silu_r"], j + 1)
                nc.vector.tensor_tensor(oo[:, j, :], oo[:, j, :], rtmp[:, j % 2, :], ALU.mult) \
                    .then_inc(S["ob_ready"], 1)
            for t in range(NTX):
                dve.wait_ge(S["gelu_done"], NTX + t + 1)
                link(nc.vector.bn_stats(stats[:, 0, :], zv[:, t, 0:512]))
                link(nc.vector.bn_stats(stats[:, 1, :], zv[:, t, 512:D]))
                link(nc.vector.bn_aggr(meanvar[:, t, :], stats[:]))
                nc.vector.tensor_scalar(varz[:, t:t + 1], meanvar[:, t, 1:2], EPS, None, ALU.add) \
                    .then_inc(S["variance"], 1)
            dve.wait_ge(S["root"], 3)
            link(nc.vector.reciprocal(varz[:], varz[:]))
            dve.wait_ge(s_late, 32)
            for t in range(NTX):
                link(nc.vector.tensor_scalar(zv[:, t, :], zv[:, t, :], meanvar[:, t, 0:1], varz[:, t:t + 1],
                                             ALU.subtract, ALU.mult))
                link(nc.vector.tensor_tensor(zv[:, t, :], zv[:, t, :], lng, ALU.mult))
                nc.vector.tensor_tensor(zv[:, t, :], zv[:, t, :], lnb, ALU.add).then_inc(S["zv_ready"], 1)
            dve.wait_ge(S["gelu_done"], 2 * NTX + KT)
            for j in range(KT):
                ps = result(dve, f"mix{j}")
                link(nc.vector.tensor_tensor(mtmp[:, 0, :].rearrange("p (t s) -> p t s", t=NTX),
                                             ps.rearrange("p (t s) -> p t s", t=NTX),
                                             bsp[:, j, :].unsqueeze(1).to_broadcast([P, NTX, P]), ALU.add))
                dve.sem_inc(free(f"mix{j}"), 1)
                nc.vector.tensor_tensor(zu[:, j, :], zu[:, j, :], mtmp[:, 0, :], ALU.mult).then_inc(S["zu_ready"], 1)
                dve.wait_ge(S["zu_ready"], j + 1)
            for j in range(KT):
                ps = result(dve, f"wb{j}")
                dve.wait_ge(S["sgb_ready"], j + 1)
                link(nc.vector.tensor_tensor(yy[:, j, :], ps[:], sgb[:, j, :], ALU.mult))
                dve.sem_inc(free(f"wb{j}"), 1)
            lre, lim, dt, size, ang = (sp5[:, i, :] for i in (0, 1, 3, 4, 5))
            sin4, n4 = sp5[:, 8:12, :], sp5[:, 12:16, :]
            dve.wait_ge(S["b_coef_exp"], 1)
            link(nc.vector.tensor_tensor(size, lre, dt, ALU.mult))
            link(nc.vector.tensor_tensor(ang, lim, dt, ALU.mult))
            for i in range(4):
                link(nc.vector.tensor_scalar(n4[:, i, :], ang, phase[:, i:i + 1], 0.5 / np.pi, ALU.add, ALU.mult))
            link(nc.vector.tensor_scalar(n4, n4, 12582912.0, -12582912.0, ALU.add, ALU.add))
            for i in range(4):
                link(nc.vector.scalar_tensor_tensor(out=sin4[:, i, :], in0=n4[:, i, :], scalar=-TURN[0], in1=ang,
                                                    op0=ALU.mult, op1=ALU.add))
                link(nc.vector.scalar_tensor_tensor(out=sin4[:, i, :], in0=n4[:, i, :], scalar=-TURN[1],
                                                    in1=sin4[:, i, :], op0=ALU.mult, op1=ALU.add))
                link(nc.vector.scalar_tensor_tensor(out=sin4[:, i, :], in0=n4[:, i, :], scalar=-TURN[2],
                                                    in1=sin4[:, i, :], op0=ALU.mult, op1=ALU.add))
                link(nc.vector.tensor_scalar(sin4[:, i, :], sin4[:, i, :], phase[:, i:i + 1], None, ALU.add))
            link(nc.vector.tensor_scalar(sin4, sin4, 3.14159250, -3.14159250, ALU.min, ALU.max))
            dve.sem_inc(S["b_coef_ready"], 1)
            for j in range(KT):
                ps = result(dve, f"wa{j}")
                dve.wait_ge(S["sga_ready"], j + 1)
                link(nc.vector.tensor_tensor(sga[:, j, :], ps[:], sga[:, j, :], ALU.mult))
                dve.sem_inc(free(f"wa{j}"), 1)
                nc.vector.tensor_tensor(yy[:, j, :], yy[:, j, :], sga[:, j, :], ALU.add).then_inc(S["y_ready"], 1)
            dve.wait_ge(S["b_coef_exp"], 3)
            link(nc.vector.tensor_tensor(sin4, sin4, size.unsqueeze(1).to_broadcast([P, 4, S5G]), ALU.mult))
            are, aim = sin4[:, 2, :], sin4[:, 3, :]
            link(nc.vector.memset(pw[:, 0, :, :], 0.0))
            link(nc.vector.memset(pw[0:64, 0, 0, :], 1.0))
            link(nc.vector.memset(pw[64:128, 0, 1, :], 1.0))
            link(nc.vector.tensor_copy(pw[:, 1, :, :], sin4[:, 0:2, :]))
            t2 = sp5[:, 12:14, :]
            ai2 = sp5[:, 14:16, :]
            link(nc.vector.tensor_copy(ai2[:, 0, :], aim))
            link(nc.vector.tensor_scalar(ai2[:, 1, :], aim, -1.0, None, ALU.mult))
            ar2 = are.unsqueeze(1).to_broadcast([P, 2, S5G])
            for k in range(1, S5T):
                link(nc.vector.tensor_tensor(t2, pw[:, k, ::-1, :], ai2, ALU.mult))
                link(nc.vector.tensor_tensor(pw[:, k + 1, :, :], pw[:, k, :, :], ar2, ALU.mult))
                link(nc.vector.tensor_tensor(pw[:, k + 1, :, :], pw[:, k + 1, :, :], t2, ALU.add))
            r8, i8 = ab8[:, 0, 0, :], ab8[:, 1, 0, :]
            link(nc.vector.tensor_copy(r8, are))
            link(nc.vector.tensor_copy(i8, aim))
            ta, tb = sp5[:, 6, :], sp5[:, 7, :]
            for _ in range(3):
                link(nc.vector.tensor_tensor(ta, r8, r8, ALU.mult))
                link(nc.vector.tensor_tensor(tb, i8, i8, ALU.mult))
                link(nc.vector.scalar_tensor_tensor(out=i8, in0=i8, scalar=2.0, in1=r8, op0=ALU.mult, op1=ALU.mult))
                link(nc.vector.tensor_tensor(r8, ta, tb, ALU.subtract))
            link(nc.vector.tensor_copy(ab8[:, 0, 1, :], r8))
            link(nc.vector.tensor_scalar(ab8[:, 1, 1, :], i8, -1.0, None, ALU.mult))
            am, wre, wim, den = (sp5[:, i, :] for i in (16, 17, 18, 19))
            link(nc.vector.tensor_scalar(am, are, -1.0, None, ALU.add))
            link(nc.vector.tensor_tensor(ta, lre, lre, ALU.mult))
            link(nc.vector.tensor_tensor(tb, lim, lim, ALU.mult))
            link(nc.vector.tensor_tensor(den, ta, tb, ALU.add))
            link(nc.vector.reciprocal(den, den))
            link(nc.vector.tensor_tensor(ta, am, lre, ALU.mult))
            link(nc.vector.tensor_tensor(tb, aim, lim, ALU.mult))
            link(nc.vector.tensor_tensor(wre, ta, tb, ALU.add))
            link(nc.vector.tensor_tensor(wre, wre, den, ALU.mult))
            link(nc.vector.tensor_tensor(ta, aim, lre, ALU.mult))
            link(nc.vector.tensor_tensor(tb, am, lim, ALU.mult))
            link(nc.vector.tensor_tensor(wim, ta, tb, ALU.subtract))
            link(nc.vector.tensor_tensor(wim, wim, den, ALU.mult))
            dve.wait_ge(S["b_s5_in"], 64)
            for g in range(0, S5G, 16):
                b0, b1 = (bb[:, i, g:g + 16, :] for i in range(2))
                t0, t1 = (tmp[:, i, :].rearrange("p (g h) -> p g h", h=S5H) for i in range(2))
                wr, wm = (w[:, g:g + 16].unsqueeze(2).to_broadcast([P, 16, S5H]) for w in (wre, wim))
                link(nc.vector.tensor_tensor(t0, b1, wm, ALU.mult))
                link(nc.vector.tensor_tensor(t1, b0, wm, ALU.mult))
                link(nc.vector.tensor_tensor(b0, b0, wr, ALU.mult))
                link(nc.vector.tensor_tensor(b0, b0, t0, ALU.subtract))
                link(nc.vector.tensor_tensor(b1, b1, wr, ALU.mult))
                link(nc.vector.tensor_tensor(b1, b1, t1, ALU.add))
            link(nc.vector.tensor_scalar(cc[64:128], cc[64:128], -1.0, None, ALU.mult))

            for j in range(KT):
                ps = result(dve, f"wout{j}")
                nc.vector.scalar_tensor_tensor(out=x[:, j, :], in0=ps[:], scalar=modc[:, 16 + j, 0:1], in1=x[:, j, :],
                                               op0=ALU.mult, op1=ALU.add).then_inc(S["x1_ready"], 1)
                dve.wait_ge(S["x1_ready"], j + 1)
                dve.sem_inc(free(f"wout{j}"), 1)
            dve.sem_inc(weights_used, 1)
            ps = result(dve, "ss2")
            nc.vector.tensor_scalar(rs2, ps[:], 1.0 / D, EPS, ALU.mult, ALU.add).then_inc(S["variance"], 1)
            dve.wait_ge(S["root"], 4)
            dve.sem_inc(free("ss2"), 1)
            link(nc.vector.reciprocal(rs2, rs2))
            nc.vector.tensor_tensor(h2, x, rs2.unsqueeze(1).to_broadcast([P, KT, T]), ALU.mult) \
                .then_inc(S["normed2"], 1)

            ps = result(dve, "route")
            link(nc.vector.tensor_copy(prob[:], ps[:, 0:NTX * NE].rearrange("p (t e) -> p t e", t=NTX)))
            dve.sem_inc(free("route"), 1)
            link(nc.vector.tensor_reduce(rsum[:], prob[:], AX.X, ALU.max))
            nc.vector.tensor_tensor(prob[:], prob[:], rsum[:].unsqueeze(2).to_broadcast([P, NTX, NE]), ALU.subtract) \
                .then_inc(S["logit_max"], 1)
            dve.wait_ge(S["logit_exp"], 1)
            link(nc.vector.tensor_reduce(rsum[:], prob[:], AX.X, ALU.add))
            link(nc.vector.reciprocal(rsum[:], rsum[:]))
            link(nc.vector.tensor_tensor(prob[:], prob[:], rsum[:].unsqueeze(2).to_broadcast([P, NTX, NE]), ALU.mult))
            TG = NTX * NG
            pg = prob[:].rearrange("p t (g e) -> p (t g) e", e=EG)

            def first_max(v, best, hit, n):
                link(nc.vector.tensor_reduce(best, v, AX.X, ALU.max))
                link(nc.vector.tensor_tensor(hit, v, best.unsqueeze(2).to_broadcast([P, n, 4]), ALU.is_equal))
                b = before[:, 0:n]
                link(nc.vector.tensor_copy(b, hit[:, :, 0]))
                for i in range(1, 4):
                    link(nc.vector.tensor_tensor(hit[:, :, i], hit[:, :, i], b, ALU.is_gt))
                    if i < 3:
                        link(nc.vector.tensor_tensor(b, hit[:, :, i], b, ALU.max))

            first_max(pg, best1[:], hit1[:], TG)
            link(nc.vector.tensor_tensor(rest[:], pg, hit1[:], ALU.mult))
            link(nc.vector.tensor_tensor(rest[:], pg, rest[:], ALU.subtract))
            link(nc.vector.tensor_tensor(rest[:], rest[:], hit1[:], ALU.subtract))
            first_max(rest[:], best2[:], hit2[:], TG)
            link(nc.vector.tensor_tensor(gscore[:], best1[:], best2[:], ALU.add))
            gs = gscore[:].rearrange("p (t g) -> p t g", g=NG)
            first_max(gs, rsum[:], ghit[:], NTX)
            gh = ghit[:].rearrange("p t g -> p (t g)").unsqueeze(2).to_broadcast([P, TG, EG])
            link(nc.vector.tensor_tensor(hit1[:], hit1[:], gh, ALU.mult))
            link(nc.vector.tensor_tensor(hit2[:], hit2[:], gh, ALU.mult))
            link(nc.vector.tensor_tensor(hot[:].rearrange("p t (g e) -> p (t g) e", e=EG), hit1[:], hit2[:], ALU.add))
            dve.sem_inc(S["onehot"], 1)
            h16 = [h[:].rearrange("p (t g) e -> p t (g e)", g=NG) for h in (hit1, hit2)]
            for k in range(2):
                link(nc.vector.tensor_tensor(etmp[:], prob[:], h16[k], ALU.mult))
                link(nc.vector.tensor_reduce(tokw[:, k, :], etmp[:], AX.X, ALU.add))
            link(nc.vector.tensor_tensor(rsum[:], tokw[:, 0, :], tokw[:, 1, :], ALU.add))
            link(nc.vector.reciprocal(rsum[:], rsum[:]))
            for k in range(2):
                link(nc.vector.tensor_tensor(tokw[:, k, :], tokw[:, k, :], rsum[:], ALU.mult))
            ps = result(dve, "rank")
            link(nc.vector.tensor_copy(rank[:], ps[:, 0:(NTX + 1) * NE].rearrange("p (t e) -> p t e", e=NE)))
            dve.sem_inc(free("rank"), 1)
            count = rank[:, NTX, :]
            link(nc.vector.tensor_scalar(nblk[:], count, 0.5, None, ALU.is_gt))
            for i in range(1, T // BLK):
                link(nc.vector.scalar_tensor_tensor(out=nblk[:], in0=count, scalar=i * BLK + 0.5, in1=nblk[:],
                                                    op0=ALU.is_gt, op1=ALU.add))
            link(nc.vector.tensor_tensor_scan(ends[:], ones[:, 0:NE], nblk[:], 0.0, ALU.mult, ALU.add))
            link(nc.vector.tensor_tensor(nblk[:], ends[:], nblk[:], ALU.subtract))
            link(nc.vector.tensor_scalar(nblk[:], nblk[:], float(BLK), None, ALU.mult))
            link(nc.vector.tensor_tensor(rank[:, 0:NTX, :], rank[:, 0:NTX, :],
                                         nblk[:].unsqueeze(1).to_broadcast([P, NTX, NE]), ALU.add))
            for k in range(2):
                link(nc.vector.tensor_tensor(etmp[:], rank[:, 0:NTX, :], h16[k], ALU.mult))
                link(nc.vector.tensor_reduce(slotf[:, k, :], etmp[:], AX.X, ALU.add))
            nc.vector.tensor_copy(slot[:], slotf[:].rearrange("p k t -> p (k t)")).then_inc(S["slots_ready"], 1)
            for b in range(NBLK):
                nc.vector.tensor_scalar(ends_le[0:1, b, :], ends[0:1, :], float(b) + 0.5, None, ALU.is_lt) \
                    .then_inc(le_made, 1)
            dve.wait_ge(le_made, NBLK)
            link(nc.vector.tensor_reduce(planf[0:1, 1:1 + NBLK], ends_le[0:1, :, :], AX.X, ALU.add))
            link(nc.vector.tensor_copy(planf[0:1, 0:1], ends[0:1, NE - 1:NE]))
            link(nc.vector.tensor_scalar(planf[0:1, 1:1 + NBLK], planf[0:1, 1:1 + NBLK], NE - 1.0, None, ALU.min))
            nc.vector.tensor_copy(plan[0:1, 0:1 + NBLK], planf[0:1, 0:1 + NBLK]).then_inc(S["plan_ready"], 1)

            n_blocks = load_plan(dve)
            with dve.Fori(0, n_blocks) as i:
                for n in range(3):
                    ps = result_e(dve, i, f"u{n}")
                    dve.wait_ge(S["sig_ready"], i * 3 + (n + 1))
                    nc.vector.tensor_tensor(hh[:, n * 512:(n + 1) * 512], ps[:], hs[:, n, :], ALU.mult) \
                        .then_inc(S["h_made"], 1)
                    dve.wait_ge(S["h_made"], i * 3 + (n + 1))
                    dve.sem_inc(bank_free_e[bank_e[f"u{n}"][0]], 1)
            dve.sem_inc(S["moe_dve_done"], 1)
            dve.wait_ge(S["moe_gathered"], 16 * 2 * NTX)
            for t in range(NTX):
                link(nc.vector.tensor_scalar(yg[:, 0, t, :], yg[:, 0, t, :], tokw[:, 0, t:t + 1], None, ALU.mult))
                nc.vector.scalar_tensor_tensor(out=yg[:, 0, t, :], in0=yg[:, 1, t, :], scalar=tokw[:, 1, t:t + 1],
                                               in1=yg[:, 0, t, :], op0=ALU.mult, op1=ALU.add) \
                    .then_inc(S["moe_summed"], 1)

            n_x2 = 0
            for j in range(KT):
                ps = result(dve, f"y{j}")
                n_x2 += 1
                copied(dve, nc.vector.scalar_tensor_tensor(out=x[:, j, :], in0=ps[:], scalar=modc[:, 40 + j, 0:1],
                                                           in1=x[:, j, :], op0=ALU.mult, op1=ALU.add),
                       S["b_x2_ready"], n_x2, f"y{j}")

            def rms(n):
                dve.wait_ge(S["root"], 4 + n + 1)
                link(nc.vector.reciprocal(RS[:], RS[:]))

            def normed(dst, kt, gain, done, count):
                nc.vector.scalar_tensor_tensor(out=dst[:, kt, :], in0=x[:, kt, :], scalar=gain, in1=RS[:],
                                               op0=ALU.mult, op1=ALU.mult).then_inc(done, 1)
                dve.wait_ge(done, count)

            rms(0)
            for kt in range(KT):
                normed(x, kt, col("g_final", kt), S["b_x2_ready"], KT + kt + 1)
            rms(1)
            for kt in range(KT):
                normed(hb, kt, col("norm_mix", kt), S["b_h_full"], kt + 1)
                nc.vector.tensor_copy(u_s[:, kt, ::-1, :], hb[:, kt, :].rearrange("p (c s) -> p s c", s=S5T)) \
                    .then_inc(S["b_s5_u_made"], 1)
            dve.wait_ge(S["b_cp_ready"], S5G // 4)
            for t in range(KT):
                g = slice(8 * t, 8 * t + 8)
                tv = tmpq.rearrange("p (g k h) -> p g k h", g=8, h=S5H)
                b0, b1 = (bb[:, i, g, :].unsqueeze(2).to_broadcast([P, 8, S5T, S5H]) for i in range(2))
                if t >= 2:
                    dve.wait_ge(bank_done, JB[f"kk{t - 2}1"] + 1)
                link(nc.vector.tensor_tensor(qb[t % 2], b0, powers(0, S5T, 0, 8 * t, 8), ALU.mult))
                link(nc.vector.tensor_tensor(tv, b1, powers(0, S5T, 1, 8 * t, 8), ALU.mult))
                nc.vector.tensor_tensor(qb[t % 2], qb[t % 2], tv, ALU.add).then_inc(S["b_qb_ready"], 1)
                dve.wait_ge(S["b_qb_ready"], t + 1)
            dve.wait_ge(S["b_s_copied"], 2 * KT)
            link(nc.vector.memset(xs[:, 0, :, :], 0.0))
            ts = scaled
            for c in range(1, S5C - 1):
                nc.vector.tensor_tensor(ts[:, 0], xs[:, c, :, :], ab8[:, 0], ALU.mult).then_inc(scan_part, 1)
                nc.vector.tensor_tensor(ts[:, 1], xs[:, c, ::-1, :], ab8[:, 1], ALU.mult).then_inc(scan_part, 1)
                dve.wait_ge(scan_part, 2 * c)
                link(nc.vector.tensor_tensor(xs[:, c + 1], xs[:, c + 1], ts[:, 0], ALU.add))
                link(nc.vector.tensor_tensor(xs[:, c + 1], xs[:, c + 1], ts[:, 1], ALU.add))
            dve.sem_inc(S["b_scanned"], 1)
            for t in range(KT):
                name = f"ys{t}"
                ps = result(dve, name)
                dve.wait_ge(S["b_ys_copied"], t + 1)
                copied(dve, nc.vector.tensor_tensor(ys2[:, t], ys2[:, t], ps.rearrange("p (g c) -> p g c", g=8), ALU.add),
                       S["b_ys_added"], t + 1, name)
            dve.wait_ge(S["b_yn_in"], 16)
            for kt in range(KT):
                hv = hb[:, kt, :].rearrange("p (c s) -> p c s", s=S5T)
                nc.vector.scalar_tensor_tensor(out=hv, in0=hv, scalar=col("s5_d", kt),
                                               in1=yn[:, kt].rearrange("p s c -> p c s"), op0=ALU.mult, op1=ALU.add) \
                    .then_inc(S["b_y5_ready"], 1)
            split_to, n_high = [0], [0]
            weights_low_part(dve, 1, split_to)

            def low_tile(dst, high, src, kt):
                n_high[0] += 1
                dve.wait_ge(high_ready, n_high[0])
                nc.vector.tensor_tensor(dst[:, kt, :], src[:, kt, :], high[:, kt, :].bitcast(F32), ALU.subtract) \
                    .then_inc(split_ready, 1)

            def low_part(dst, high, src):
                for kt in range(KT):
                    low_tile(dst, high, src, kt)

            low_part(low_b, high_g, hb)
            n_sig = 0
            for j in range(KT):
                for i in range(2):
                    weights_low_part(dve, ahead("glu", "glu", 2 * j + i), split_to)
                ps = result(dve, f"glu{2 * j}")
                n_sig += 1
                dve.wait_ge(S["b_sig_b"], n_sig)
                link(nc.vector.tensor_tensor(st[:, j % 2, :], ps[:], st[:, j % 2, :], ALU.mult))
                dve.sem_inc(free(f"glu{2 * j}"), 1)
                link(nc.vector.tensor_tensor(x[:, j, :], x[:, j, :], st[:, j % 2, :], ALU.add))
                dve.sem_inc(S["b_st_used"], 1)
                dve.sem_inc(S["b_x_ready"], 1)
            n_x = KT

            def normed_all(n, gain, first, low):
                rms(n)
                for kt in range(KT + 1):
                    if kt < KT:
                        normed(raw, kt, col(gain, first + kt), S["b_h_full"], h_count[n] - KT + kt + 1)
                    if kt:
                        low_tile(low, high_b, raw, kt - 1)

            def dense_dve(n, n_sig, n_x):
                normed_all(2 + 2 * n, "norm_ffn", KT * n, low_b)
                for j in range(FFT):
                    name = f"gu{n}{2 * j + 1}"
                    for i in range(2 if j < FFT - 1 else 1):
                        weights_low_part(dve, ahead(f"down{n}", f"gu{n}", 2 * j + i), split_to)
                    ps = result(dve, name)
                    n_sig += 1
                    dve.wait_ge(S["b_sig_b"], n_sig)
                    copied(dve, nc.vector.tensor_tensor(product[:, j % 3, :], ps[:], st[:, j % 2, :], ALU.mult),
                           product_ready, FFT * n + j + 1, name)
                    dve.sem_inc(S["b_st_used"], 1)
                    n_high[0] += 1
                    dve.wait_ge(high_ready, n_high[0])
                    nc.vector.tensor_tensor(hid(j)[1], product[:, j % 3, :], hid(j)[0].bitcast(F32),
                                            ALU.subtract).then_inc(split_ready, 1)
                for j in range(KT):
                    weights_low_part(dve, ahead(f"down{n}", f"down{n}", j, FFT), split_to)
                    name = f"down{n}{j}"
                    ps = result(dve, name)
                    n_x += 1
                    copied(dve, nc.vector.tensor_tensor(x[:, j, :], x[:, j, :], ps[:], ALU.add), S["b_x_ready"], n_x,
                           name)
                return n_sig, n_x

            n_sig, n_x = dense_dve(0, n_sig, n_x)
            normed_all(3, "norm_mix", KT, low_p)
            dve.wait_ge(S["b_rope_in"], 48)
            for s in range(NR + 2):
                if s == 2 * KT:
                    for n in range(2):
                        weights_low_part(dve, ahead("dki", "dv", n, KT, True), split_to)
                if 1 <= s <= NR and ROPED[s - 1][2]:
                    k = norm_index[s - 1]
                    dve.wait_ge(S["b_rroot"], k + 1)
                    link(nc.vector.reciprocal(rst[:, k % 2, :], rst[:, k % 2, :]))
                    gain = ROPED[s - 1][3]
                    dve.wait_ge(S["b_raw_ready"], s)
                    nc.vector.scalar_tensor_tensor(out=roped_tile(s - 1), in0=roped_tile(s - 1),
                                                   scalar=1.0 if gain is None else col("qk_gain", gain),
                                                   in1=rst[:, k % 2, :], op0=ALU.mult, op1=ALU.mult) \
                        .then_inc(S["b_normed_q"], 1)
                    dve.wait_ge(S["b_normed_q"], k + 1)
                if s < NR:
                    weights_low_part(dve, ahead("dki", ROPED[s][0], ROPED[s][1]), split_to)
                if s >= 2:
                    name = f"rot{s - 2}"
                    ps = result(dve, name)
                    v = roped_tile(s - 2)
                    link(nc.vector.tensor_tensor(rt[:, 0, :], ps[:], cossin[:, 1, :], ALU.mult))
                    dve.sem_inc(free(name), 1)
                    dve.wait_ge(S["b_turned_cos"], s - 1)
                    nc.vector.tensor_tensor(v, v, rt[:, 0, :], ALU.add).then_inc(S["b_rotated"], 1)
                    dve.wait_ge(S["b_rotated"], s - 1)
            ps = result(dve, "wi")
            link(nc.vector.tensor_scalar(wi, ps[:, 0:NTX * IH].rearrange("p (t h) -> p t h", h=IH),
                                         float(IH) ** -0.5, float(HD) ** -0.5, ALU.mult, ALU.mult))
            dve.sem_inc(free("wi"), 1)
            link(nc.vector.memset(bias[0][:, 0:P], 0.0))
            dve.sem_inc(S["b_bias0"], 1)
            dve.wait_ge(S["b_masked"], 1)
            def scale_rows(s):
                b = s % 4
                dve.wait_ge(S["b_exped"], s + 1)
                link(nc.vector.reciprocal(rsm[:, b:b + 1], sm[:, b:b + 1]))
                nc.vector.tensor_scalar(diag[:, b, :], ident[:], rsm[:, b:b + 1], None, ALU.mult) \
                    .then_inc(S["b_diag_ready"], 1)

            def index_scores(t):
                w = (t + 1) * P
                for i in range(IH):
                    n = IH * (t - 1) + i + 1
                    dve.wait_ge(S["b_relu_ready"], n)
                    if i == 0:
                        ins = nc.vector.tensor_scalar(score[:, 0:w], rl[:, i % 2, 0:w], wi[:, t, i:i + 1], None,
                                                      ALU.mult)
                    else:
                        ins = nc.vector.scalar_tensor_tensor(out=score[:, 0:w], in0=rl[:, i % 2, 0:w],
                                                             scalar=wi[:, t, i:i + 1], in1=score[:, 0:w],
                                                             op0=ALU.mult, op1=ALU.add)
                    ins.then_inc(relu_used, 1)
                    dve.wait_ge(relu_used, n)
                dve.sem_inc(S["b_score_ready"], 1)

            rounds, first = TOPK // 8, 3
            for s in range(NPAIR + 1):
                if s < NPAIR:
                    t, h = PAIRS[s]
                    w = (t + 1) * P
                    b = s % 4
                    name = f"lg{s}"
                    ps = result(dve, name)
                    if s >= 4:
                        dve.wait_ge(bank_done, JB[f"pt{s - 4}"] + 1)
                    link(nc.vector.tensor_tensor_reduce(pp[:, b, 0:w], ps[:, 0:w], bias[t % 2][:, 0:w], 1.0, -3.0e38,
                                                        ALU.add, ALU.max, mx[:, b:b + 1]))
                    dve.sem_inc(free(name), 1)
                    nc.vector.tensor_scalar(nmx[:, b:b + 1], mx[:, b:b + 1], -float(HD) ** -0.5, None, ALU.mult) \
                        .then_inc(S["b_logits"], 1)
                if s >= 1:
                    scale_rows(s - 1)
                if s < NPAIR and t < NTX - 1:
                    w = (t + 2) * P
                    if h == 1:
                        index_scores(t + 1)
                    if h >= first:
                        if h == first:
                            dve.wait_ge(S["b_masked"], t + 2)
                        for _ in range(rounds * (h - first) // (AH - first), rounds * (h - first + 1) // (AH - first)):
                            link(nc.vector.max(m8[:], score[:, 0:w]))
                            link(nc.vector.match_replace(score[:, 0:w], m8[:], score[:, 0:w], TAKEN))
                    if h == AH - 1:
                        link(nc.vector.tensor_scalar(bias[(t + 1) % 2][:, 0:w], score[:, 0:w], TAKEN / 2, MASKED,
                                                     ALU.is_gt, ALU.mult))
            low_part(low_b, high_b, oT)
            for j in range(KT):
                weights_low_part(dve, ahead("wo", "wo", j), split_to)
                name = f"wo{j}"
                ps = result(dve, name)
                n_x += 1
                copied(dve, nc.vector.tensor_tensor(x[:, j, :], x[:, j, :], ps[:], ALU.add), S["b_x_ready"], n_x, name)
            dense_dve(1, n_sig, n_x)


def _tiles(w, b, width=P):
    return w[:, b * width:(b + 1) * width].reshape(-1, P, width).transpose(1, 0, 2)


def _stream(stream, parts):
    units = []
    for name, kind, b0, b1 in stream:
        for b in range(b0, b1):
            if kind == "col":
                units.append(_tiles(parts[name], b))
            else:
                t = _tiles(parts[name], b, 4 * P)
                units.append(t.reshape(P, -1, P))
    a = np.concatenate(units, axis=1)
    n = -(-a.shape[1] // CH)
    pad = np.zeros((P, n * CH - a.shape[1], P), np.float32)
    a = np.concatenate([a, pad], axis=1) if pad.shape[1] else a
    return np.ascontiguousarray(a.reshape(P, n, CH * P).transpose(1, 0, 2))


def _columns(v):
    return np.asarray(v, np.float32).reshape(-1, P).T


def layouts(inputs):
    g = {k: np.asarray(v) for k, v in inputs.items()}
    io = {}
    io["xt"] = np.ascontiguousarray(g["x"][0].T.reshape(KT, P, T))
    io["ct"] = np.ascontiguousarray(g["ctx"][0].T.reshape(KT, P, TC))
    w = g["w_in"][0]
    cut = np.cumsum([0, D, D, 512, 512, D, D, RANK, RANK, D, D])
    zu, zv, q, k, v, r, lf, lb, ga, gb = (w[:, a:b] for a, b in zip(cut[:-1], cut[1:]))
    lr = np.zeros((D, P), np.float32)
    lr[:, 0:RANK] = lf
    lr[:, 32:32 + RANK] = lb
    io["wa_stream"] = _stream(STREAM_A, dict(mod=g["w_mod"][0], lr=lr, k=k, q=q, v=v, r=r, zv=zv, zu=zu, ga=ga, gb=gb,
                                             wb=g["w_branch_b"][0], wa=g["w_branch_a"][0], wout=g["w_out"][0]))
    io["mod2"] = np.ascontiguousarray(g["w_mod"][0][:, 2 * D:].reshape(KT, P, 2, 2 * D).transpose(0, 2, 1, 3)) \
        .reshape(2 * KT, P, 2 * D)
    packed = dict(b_mod=g["b_mod"], g_norm1=g["g_norm1"], g_norm2=g["g_norm2"], gla_g=g["gla_norm_g"],
                  b_branch=g["b_branch"], g_final=g["g_final"], b_gate2=g["b_gate2"], s5_d=g["s5_d_2"],
                  norm_mix=g["norm_mix_2"], norm_ffn=g["norm_ffn_2"])
    parts = [_columns(packed[n]) for n in packed] + [_columns(g["c"]), _columns(g["c_ctx"])]
    parts += [np.tile(g[n][0], 2)[:, None] for n in ("dsa_q_norm_2", "dsa_k_norm_2")]
    io["cols"] = np.ascontiguousarray(np.concatenate(parts, axis=1))
    assert io["cols"].shape[1] == NCOL
    io["ident"] = np.eye(P, dtype=np.float32)
    io["ones"] = np.ones((P, P), np.float32)
    i = np.arange(P)
    io["tri"] = (i[:, None] < i[None, :]).astype(np.float32)
    same = (i[:, None] // GC) == (i[None, :] // GC)
    io["gmask"] = np.ascontiguousarray(np.stack([same & (i[:, None] <= i[None, :]), same & (i[:, None] >= i[None, :])],
                                                axis=1).astype(np.uint32))
    wg = np.zeros((64, 2, 512), np.float32)
    wg[0:RANK, 0] = g["w_gate2"][0, 0]
    wg[32:32 + RANK, 1] = g["w_gate2"][0, 1]
    io["wgate"] = wg
    io["wrouter"] = np.ascontiguousarray(g["w_router"].reshape(KT, P, NE).transpose(1, 0, 2))
    io["b_router"] = g["b_router"].reshape(1, NE)
    io["sgu_w"] = np.ascontiguousarray(g["sgu_w"][0].transpose(2, 0, 1))
    io["sgu_ln_g"] = g["sgu_ln_g"][0]
    io["sgu_ln_b"] = g["sgu_ln_b"][0]
    io["sgu_b"] = g["sgu_b"][0].reshape(-1)
    layouts_more(g, io)
    return io


def kernel(**inputs):
    import concourse.bacc as bacc
    from concourse.bass_utils import run_bass_kernel_spmd as run

    arrays = {f"in_{n}": a for n, a in layouts(inputs).items()}
    nc = bacc.Bacc("TRN2", target_bir_lowering=False, num_devices=1)
    io = {n[3:]: nc.dram_tensor(n, a.shape, mybir.dt.from_np(a.dtype), kind="ExternalInput").ap()
          for n, a in arrays.items()}
    out = nc.dram_tensor("out_dram", (KT, P, T), F32, kind="ExternalOutput").ap()
    block_kernel(nc, io, out, dram_scratch(nc))
    r = run(nc, [arrays], core_ids=[0])
    return np.ascontiguousarray(r.results[0]["out_dram"].reshape(D, T).T).reshape(1, T, D)
```
